# Optimizing a Trainium2 kernel written in Bass

```python
import math
import jax
import jax.numpy as jnp
from jax import lax
import numpy as np

D_MODEL = 1024
BATCH = 1
SEQ = 256
DEPTH = 2

MEM_LEN = 256
N_EVEN = (DEPTH + 1) // 2
N_ODD = DEPTH // 2
EPS = 1e-6

CONV_CH = D_MODEL // 2
CONV_TAPS = 3
RET_HEADS = 8
RET_DK = D_MODEL // 16
RET_DV = D_MODEL // 16
RET_QK = RET_HEADS * RET_DK
RET_V = RET_HEADS * RET_DV
RET_CHUNK = 128
RET_THETA = 10000.0
RET_MAX_RATE = 1.0 / 32.0
RET_MIN_RATE = 1.0 / 512.0
EVEN_SPLITS = (CONV_CH, CONV_CH, CONV_CH, RET_QK, RET_QK, RET_V, RET_V)
EVEN_IN = sum(EVEN_SPLITS)
EVEN_OUT = CONV_CH + RET_V
DIFF_HEADS = 8
DIFF_D = D_MODEL // 16
DIFF_QK = 2 * DIFF_HEADS * DIFF_D
DIFF_V = DIFF_HEADS * 2 * DIFF_D
ODD_SPLITS = (DIFF_QK, DIFF_QK, DIFF_V)
ODD_IN = sum(ODD_SPLITS)
ROPE_DIM = DIFF_D // 4
ROPE_THETA = 500000.0
Q_BLOCK = 128
XA_HEADS = 4
XA_HD = D_MODEL // XA_HEADS
D_FF = 2816
N_EXPERTS = 8
TOP_K = 2
D_FF_EXPERT = 3584

kernel_name = "hybrid_conv_retention_diffattn_moe_encoder"

def rms_norm(x, g):
    x32 = x.astype(jnp.float32)
    y = x32 * lax.rsqrt(jnp.mean(x32 * x32, axis=-1, keepdims=True) + EPS)
    return (y * g.astype(jnp.float32)).astype(x.dtype)

def group_rms_norm(x, g):
    H, d = x.shape[1], x.shape[3]
    x32 = x.astype(jnp.float32)
    y = x32 * lax.rsqrt(jnp.mean(x32 * x32, axis=-1, keepdims=True) + EPS)
    return y * g.astype(jnp.float32).reshape(1, H, 1, d)

def split_cols(x, sizes):
    out, start = [], 0
    for s in sizes:
        out.append(x[..., start:start + s])
        start += s
    return out

def rotary(x, positions, rot_dim, theta):
    half = rot_dim // 2
    inv_freq = jnp.exp(-math.log(theta) * jnp.arange(half, dtype=jnp.float32) * (2.0 / rot_dim))
    ang = positions.astype(jnp.float32)[:, None, :, None] * inv_freq
    cos, sin = jnp.cos(ang), jnp.sin(ang)
    x32 = x.astype(jnp.float32)
    x1, x2 = x32[..., :half], x32[..., half:rot_dim]
    out = jnp.concatenate([x1 * cos - x2 * sin, x1 * sin + x2 * cos, x32[..., rot_dim:]], axis=-1)
    return out.astype(x.dtype)

def short_conv_mixer(h, gate_b, gate_c, conv_w):
    u = gate_c * h
    L = u.shape[1]
    up = jnp.pad(u, ((0, 0), (1, 1), (0, 0)))
    conv = conv_w[0] * up[:, :L] + conv_w[1] * up[:, 1:L + 1] + conv_w[2] * up[:, 2:]
    return gate_b * conv

def retention_direction(q, k, v, log_gamma, strict):
    B, H, L, dk = q.shape
    dv = v.shape[-1]
    C = RET_CHUNK
    NC = L // C
    qc = q.astype(jnp.float32).reshape(B, H, NC, C, dk)
    kc = k.astype(jnp.float32).reshape(B, H, NC, C, dk)
    vc = v.astype(jnp.float32).reshape(B, H, NC, C, dv)
    idx = jnp.arange(C, dtype=jnp.float32)
    lg = log_gamma[:, None]
    dist = idx[:, None] - idx[None, :]
    mask = dist > 0 if strict else dist >= 0
    decay = jnp.where(mask, jnp.exp(lg[:, :, None] * jnp.where(mask, dist, 0.0)), 0.0)
    scores = jnp.einsum('bhnid,bhnjd->bhnij', qc, kc) * decay[None, :, None]
    intra = jnp.einsum('bhnij,bhnjv->bhniv', scores, vc)
    k_dec = jnp.exp(lg * (C - 1.0 - idx))
    kv = jnp.einsum('bhnjd,hj,bhnjv->nbhdv', kc, k_dec, vc)
    chunk_decay = jnp.exp(lg * C)[:, :, None]

    def step(state, kv_n):
        return chunk_decay * state + kv_n, state

    _, prev = lax.scan(step, jnp.zeros((B, H, dk, dv), jnp.float32), kv)
    q_dec = jnp.exp(lg * (idx + 1.0))
    inter = jnp.einsum('bhnid,hi,nbhdv->bhniv', qc, q_dec, prev)
    return (intra + inter).reshape(B, H, L, dv)

def bidirectional_retention(q, k, v, p_fwd, p_bwd):
    lg_f = -jnp.exp(p_fwd.astype(jnp.float32))
    lg_b = -jnp.exp(p_bwd.astype(jnp.float32))
    fwd = retention_direction(q, k, v, lg_f, False)
    bwd = retention_direction(jnp.flip(q, 2), jnp.flip(k, 2), jnp.flip(v, 2), lg_b, True)
    return fwd + jnp.flip(bwd, 2)

def even_token_mixer(h, positions, w_in, conv_w, p_fwd, p_bwd, gn_g, w_out):
    B, L, _ = h.shape
    gb, gc, hc, q, k, v, g = split_cols(h @ w_in, EVEN_SPLITS)
    a = short_conv_mixer(hc, gb, gc, conv_w)

    def to_heads(t, d):
        return t.reshape(B, L, RET_HEADS, d).transpose(0, 2, 1, 3)

    q = rotary(to_heads(q, RET_DK), positions, RET_DK, RET_THETA)
    k = rotary(to_heads(k, RET_DK), positions, RET_DK, RET_THETA) * (RET_DK ** -0.5)
    o = bidirectional_retention(q, k, to_heads(v, RET_DV), p_fwd, p_bwd)
    o = group_rms_norm(o, gn_g).transpose(0, 2, 1, 3).reshape(B, L, RET_V)
    r = (jax.nn.silu(g.astype(jnp.float32)) * o).astype(h.dtype)
    return jnp.concatenate([a, r], axis=-1) @ w_out

def diff_attention_mixer(h, positions, w_in, lam_q1, lam_k1, lam_q2, lam_k2, gn_g, w_out, lambda_init):
    B, L, _ = h.shape
    q, k, v = split_cols(h @ w_in, ODD_SPLITS)
    q = rotary(q.reshape(B, L, 2 * DIFF_HEADS, DIFF_D).transpose(0, 2, 1, 3), positions, ROPE_DIM, ROPE_THETA)
    k = rotary(k.reshape(B, L, 2 * DIFF_HEADS, DIFF_D).transpose(0, 2, 1, 3), positions, ROPE_DIM, ROPE_THETA)
    v = v.reshape(B, L, DIFF_HEADS, 2 * DIFF_D).transpose(0, 2, 1, 3).astype(jnp.float32)
    f32 = jnp.float32
    lam = (jnp.exp(jnp.sum(lam_q1.astype(f32) * lam_k1.astype(f32)))
           - jnp.exp(jnp.sum(lam_q2.astype(f32) * lam_k2.astype(f32))) + lambda_init)
    nb = L // Q_BLOCK
    q_blocks = q.reshape(B, 2 * DIFF_HEADS, nb, Q_BLOCK, DIFF_D).transpose(2, 0, 1, 3, 4)
    scale = DIFF_D ** -0.5

    def attend(qb):
        s = jnp.einsum('bgqd,bgkd->bgqk', qb, k).astype(f32) * scale
        p = jax.nn.softmax(s, axis=-1).reshape(B, DIFF_HEADS, 2, Q_BLOCK, L)
        return jnp.einsum('bhqk,bhkv->bhqv', p[:, :, 0] - lam * p[:, :, 1], v)

    o = lax.map(attend, q_blocks)
    o = o.transpose(1, 2, 0, 3, 4).reshape(B, DIFF_HEADS, L, 2 * DIFF_D)
    o = group_rms_norm(o, gn_g) * (1.0 - lambda_init)
    o = o.transpose(0, 2, 1, 3).reshape(B, L, DIFF_V).astype(h.dtype)
    return o @ w_out

def memory_cross_attention(h, mem_n, wq, wkv, wo):
    B, L, D = h.shape
    M = mem_n.shape[1]
    q = (h @ wq).reshape(B, L, XA_HEADS, XA_HD)
    k, v = split_cols(mem_n @ wkv, (D, D))
    k = k.reshape(B, M, XA_HEADS, XA_HD)
    v = v.reshape(B, M, XA_HEADS, XA_HD).astype(jnp.float32)
    s = jnp.einsum('blhd,bmhd->bhlm', q, k).astype(jnp.float32) * (XA_HD ** -0.5)
    p = jax.nn.softmax(s, axis=-1)
    o = jnp.einsum('bhlm,bmhd->blhd', p, v).reshape(B, L, D).astype(h.dtype)
    return o @ wo

def swiglu(h, w_gate, w_up, w_down):
    return (jax.nn.silu(h @ w_gate) * (h @ w_up)) @ w_down

def moe_swiglu(h, router_w, w_gate, w_up, w_down):
    B, L, D = h.shape
    t = h.reshape(B * L, D)
    logits = (t @ router_w).astype(jnp.float32)
    top_v, top_i = lax.top_k(logits, TOP_K)
    top_w = jax.nn.softmax(top_v, axis=-1)
    gates = jnp.sum(jax.nn.one_hot(top_i, N_EXPERTS, dtype=jnp.float32) * top_w[..., None], axis=1)
    out = jnp.zeros((B * L, D), jnp.float32)
    for e in range(N_EXPERTS):
        out = out + gates[:, e:e + 1] * swiglu(t, w_gate[e], w_up[e], w_down[e])
    return out.astype(h.dtype).reshape(B, L, D)

def setup_inputs(seed: int = 0) -> dict:
    key = jax.random.key(seed)
    ks = iter(jax.random.split(key, 48))
    f32 = jnp.float32

    def nrm(shape, fan_in):
        return jax.random.normal(next(ks), shape, f32) * (fan_in ** -0.5)

    def gain(shape):
        return 1.0 + 0.01 * jax.random.normal(next(ks), shape, f32)

    x = jax.random.normal(next(ks), (BATCH, SEQ, D_MODEL), f32)
    mem = jax.random.normal(next(ks), (BATCH, MEM_LEN, D_MODEL), f32)
    offsets = jax.random.randint(next(ks), (BATCH, 1), 0, SEQ, dtype=jnp.int32)
    positions = offsets + jnp.arange(SEQ, dtype=jnp.int32)[None, :]
    rates = jnp.exp(jnp.linspace(math.log(RET_MAX_RATE), math.log(RET_MIN_RATE), RET_HEADS)).astype(f32)
    base = jnp.log(-jnp.log1p(-rates))
    return {
        "x": x,
        "mem": mem,
        "positions": positions,
        "mem_norm_g": gain((D_MODEL,)),
        "final_norm_g": gain((D_MODEL,)),
        "mix_norm_g": gain((DEPTH, D_MODEL)),
        "xa_norm_g": gain((DEPTH, D_MODEL)),
        "ffn_norm_g": gain((DEPTH, D_MODEL)),
        "xa_wq": nrm((DEPTH, D_MODEL, D_MODEL), D_MODEL),
        "xa_wkv": nrm((DEPTH, D_MODEL, 2 * D_MODEL), D_MODEL),
        "xa_wo": nrm((DEPTH, D_MODEL, D_MODEL), D_MODEL),
        "ev_w_in": nrm((N_EVEN, D_MODEL, EVEN_IN), D_MODEL),
        "ev_conv_w": nrm((N_EVEN, CONV_TAPS, CONV_CH), CONV_TAPS),
        "ev_ret_decay_f": base[None, :] + 0.05 * jax.random.normal(next(ks), (N_EVEN, RET_HEADS), f32),
        "ev_ret_decay_b": base[None, :] + 0.05 * jax.random.normal(next(ks), (N_EVEN, RET_HEADS), f32),
        "ev_ret_gn_g": gain((N_EVEN, RET_V)),
        "ev_w_out": nrm((N_EVEN, EVEN_OUT, D_MODEL), EVEN_OUT),
        "ffd_w_gate": nrm((N_EVEN, D_MODEL, D_FF), D_MODEL),
        "ffd_w_up": nrm((N_EVEN, D_MODEL, D_FF), D_MODEL),
        "ffd_w_down": nrm((N_EVEN, D_FF, D_MODEL), D_FF),
        "od_w_in": nrm((N_ODD, D_MODEL, ODD_IN), D_MODEL),
        "od_lam_q1": 0.1 * jax.random.normal(next(ks), (N_ODD, DIFF_D), f32),
        "od_lam_k1": 0.1 * jax.random.normal(next(ks), (N_ODD, DIFF_D), f32),
        "od_lam_q2": 0.1 * jax.random.normal(next(ks), (N_ODD, DIFF_D), f32),
        "od_lam_k2": 0.1 * jax.random.normal(next(ks), (N_ODD, DIFF_D), f32),
        "od_gn_g": gain((N_ODD, DIFF_V)),
        "od_w_out": nrm((N_ODD, DIFF_V, D_MODEL), DIFF_V),
        "moe_router": nrm((N_ODD, D_MODEL, N_EXPERTS), D_MODEL),
        "moe_w_gate": nrm((N_ODD, N_EXPERTS, D_MODEL, D_FF_EXPERT), D_MODEL),
        "moe_w_up": nrm((N_ODD, N_EXPERTS, D_MODEL, D_FF_EXPERT), D_MODEL),
        "moe_w_down": nrm((N_ODD, N_EXPERTS, D_FF_EXPERT, D_MODEL), D_FF_EXPERT),
    }

def reference(x, mem, positions, mem_norm_g, final_norm_g, mix_norm_g, xa_norm_g, ffn_norm_g,
              xa_wq, xa_wkv, xa_wo, ev_w_in, ev_conv_w, ev_ret_decay_f, ev_ret_decay_b, ev_ret_gn_g,
              ev_w_out, ffd_w_gate, ffd_w_up, ffd_w_down, od_w_in, od_lam_q1, od_lam_k1, od_lam_q2,
              od_lam_k2, od_gn_g, od_w_out, moe_router, moe_w_gate, moe_w_up, moe_w_down):
    mem_n = rms_norm(mem, mem_norm_g)
    for i in range(DEPTH):
        j = i // 2
        h = rms_norm(x, mix_norm_g[i])
        if i % 2 == 0:
            x = x + even_token_mixer(h, positions, ev_w_in[j], ev_conv_w[j], ev_ret_decay_f[j],
                                     ev_ret_decay_b[j], ev_ret_gn_g[j], ev_w_out[j])
        else:
            lambda_init = 0.8 - 0.6 * math.exp(-0.3 * i)
            x = x + diff_attention_mixer(h, positions, od_w_in[j], od_lam_q1[j], od_lam_k1[j],
                                         od_lam_q2[j], od_lam_k2[j], od_gn_g[j], od_w_out[j], lambda_init)
        x = x + memory_cross_attention(rms_norm(x, xa_norm_g[i]), mem_n, xa_wq[i], xa_wkv[i], xa_wo[i])
        h = rms_norm(x, ffn_norm_g[i])
        if i % 2 == 0:
            x = x + swiglu(h, ffd_w_gate[j], ffd_w_up[j], ffd_w_down[j])
        else:
            x = x + moe_swiglu(h, moe_router[j], moe_w_gate[j], moe_w_up[j], moe_w_down[j])
    return rms_norm(x, final_norm_g)


_drawn_inputs = setup_inputs


def setup_inputs(seed=0):
    import zlib

    import numpy as np

    out = dict(_drawn_inputs(seed))
    spreads = {}
    factors = {'mem_norm_g': 8.0,
     'final_norm_g': 33.063,
     'xa_norm_g': 8.0,
     'ffn_norm_g': 2.858,
     'ev_ret_gn_g': 3.506,
     'od_lam_q1': 2.9,
     'od_lam_k1': 2.695,
     'od_gn_g': 11.026}
    for name, (base, spread) in spreads.items():
        noise = np.random.default_rng([zlib.crc32(name.encode()), seed]).standard_normal(out[name].shape)
        drawn = base * np.exp(spread * noise) if base else spread * noise
        out[name] = jnp.asarray(drawn.astype(out[name].dtype))
    for name, factor in factors.items():
        out[name] = (out[name] * factor).astype(out[name].dtype)
    return out
```

```python
import math
from contextlib import ExitStack

import numpy as np

import concourse.bass as bass
from concourse import mybir

F32 = mybir.dt.float32
F32R = mybir.dt.float32r
I32 = mybir.dt.int32
ACT = mybir.ActivationFunctionType
ALU = mybir.AluOpType
AX = mybir.AxisListType

P = 128
RAW = 6
CUT = 3
AHEAD = CUT - 1
EPS = 1e-6

RET_THETA, ROPE_THETA = 10000.0, 500000.0


def shapes(x, mem, moe_gate, ffd_gate, ev_in):
    s = {}
    s["L"], s["D"] = x.shape[1], x.shape[2]
    s["M"] = mem.shape[1]
    s["E"], s["FE"] = moe_gate.shape[1], moe_gate.shape[3]
    s["FF"] = ffd_gate.shape[2]
    return s


STREAM = [("evq", 2), ("evk", 2), ("evv", 2), ("evg", 2), ("evc", 6), ("k0", 4), ("v0", 4), ("evo", 4),
          ("q0", 4), ("o0", 4), ("fgu", 22), ("fdn", 11), ("odq", 4), ("odk", 4), ("odv", 4), ("k1", 4),
          ("v1", 4), ("odo", 4), ("q1", 4), ("o1", 4)]
FIRST = {}
_n = 0
for _name, _k in STREAM:
    FIRST[_name] = _n
    _n += _k
FIRST["moe"] = _n
BANKS = {}
_n = 0
for _name, _k in [("evq", 2), ("evk", 2), ("evv", 2), ("evg", 2), ("evc", 6), ("k0", 4), ("v0", 4), ("evo", 4),
                  ("q0", 4), ("o0", 4), ("odq", 4), ("odk", 4), ("odv", 4), ("k1", 4), ("v1", 4),
                  ("odo", 4), ("q1", 4), ("o1", 4)]:
    BANKS[_name] = _n
    _n += _k
TURNS = {}
_n = 0
for _name, _k in [("x0", 8), ("mem", 8), ("ret", 4), ("xa0", 8), ("ffn", 8), ("x1", 8), ("dif", 8), ("xa1", 8),
                  ("moe", 8)]:
    TURNS[_name] = (_n, _k)
    _n += _k
NORMS = {n: i for i, n in enumerate(["x0", "mem", "ret", "xa0", "ffn", "x1", "dif", "xa1", "moe", "fin"])}

ROWS = {}
_n = 0
for _name, _k in [("mem", 8), ("x0", 8), ("x1", 8), ("xa0", 8), ("xa1", 8), ("ffn", 8), ("moe", 8), ("ret", 4),
                  ("dif", 8), ("conv", 12)]:
    ROWS[_name] = _n
    _n += _k
N_ROWS = _n

CONST = {}
_n = 0
for _name, _k in [("ident", P), ("before", P), ("slot", P), ("after_i", 512), ("before_i", 512), ("freq", 40),
                  ("experts", 16)]:
    CONST[_name] = (_n, _n + _k)
    _n += _k
N_CONST = _n


def constants():
    c = np.zeros((P, N_CONST), np.float32)
    p = np.arange(P)

    def put(name, a):
        c[:, CONST[name][0]:CONST[name][1]] = a
    put("ident", np.eye(P))
    put("before", (p[:, None] < p[None, :]))
    put("slot", np.broadcast_to(p[None, :], (P, P)))
    j = (np.arange(2)[None, :, None] * P + p[:, None, None])
    d = np.arange(2 * P)[None, None, :] - j
    put("after_i", np.maximum(d, 0).reshape(P, -1))
    put("before_i", np.maximum(-d, 0).reshape(P, -1))
    f = []
    for theta, rot in ((RET_THETA, 64), (ROPE_THETA, 16)):
        half = rot // 2
        f.append(np.exp(np.float32(-math.log(theta)) * np.arange(half, dtype=np.float32) * np.float32(2.0 / rot)))
    put("freq", np.concatenate(f)[None, :].astype(np.float32))
    put("experts", np.arange(16)[None, :])
    return c


def trunk_kernel(nc, x, mem, positions, mem_norm_g, final_norm_g, mix_norm_g, xa_norm_g, ffn_norm_g, xa_wq, xa_wkv,
                 xa_wo, ev_w_in, ev_conv_w, ev_ret_decay_f, ev_ret_decay_b, ev_ret_gn_g, ev_w_out, ffd_w_gate,
                 ffd_w_up, ffd_w_down, od_w_in, od_lam_q1, od_lam_k1, od_lam_q2, od_lam_k2, od_gn_g, od_w_out,
                 moe_router, moe_w_gate, moe_w_up, moe_w_down, consts, out):
    D = x.shape[2]
    KT = D // P
    NE = moe_router.shape[2]
    NB = moe_w_gate.shape[3] // 512
    FT = ffd_w_gate.shape[2] // P
    RH = ev_ret_decay_f.shape[1]
    DH = od_gn_g.shape[1] // P
    XH = 4
    PASS = 6 * NB
    LAM0 = 0.8 - 0.6 * math.exp(-0.3)
    BLK = P

    ctx = ExitStack()
    with ctx:
        def sb(name, shape, dt=F32, stack=ctx):
            return stack.enter_context(nc.sbuf_tensor(name, shape, dt))

        def sem(name):
            return ctx.enter_context(nc.semaphore(name))

        raw = sb("raw", [P, RAW, 2048])
        w_hi = sb("w_hi", [P, CUT, 2048], F32R)
        w_lo = sb("w_lo", [P, CUT, 2048], F32R)
        X = sb("X", [P, 2, D])
        a_hi = sb("a_hi", [P, KT, 256], F32R)
        a_lo = sb("a_lo", [P, KT, 256], F32R)
        ta = sb("ta", [P, 2048])
        tb = sb("tb", [P, 2048])
        rot = sb("rot", [P, 2, 512])
        const = sb("const", [P, 3 * P + 56])
        ident, before, slot = const[:, 0:P], const[:, P:2 * P], const[:, 2 * P:3 * P]
        freq, experts = const[:, 3 * P:3 * P + 40], const[:, 3 * P + 40:3 * P + 56]
        rows = sb("rows", [N_ROWS, P])
        cols = sb("cols", [P, N_ROWS])
        pos_i = sb("pos_i", [2, P], I32)
        pos_f = sb("pos_f", [2, P])
        pos = sb("pos", [P, 2])
        ang = sb("ang", [P, 2, 40])
        turnsb = sb("turnsb", [P, 2, 40])
        cos = sb("cos", [P, 2, 40])
        sin = sb("sin", [P, 2, 40])
        decay = sb("decay", [P, 2, RH])
        lamv = sb("lamv", [P, 4, 64])
        lams = sb("lams", [P, 4])
        router = sb("router", [P, KT, NE])
        r_hi = sb("r_hi", [P, KT, NE], F32R)
        r_lo = sb("r_lo", [P, KT, NE], F32R)
        half = sb("half", [P, 16])
        sums = sb("sums", [P, 16])
        var = sb("var", [P, 16])
        rstd = sb("rstd", [P, 16])
        mx = sb("mx", [P, 16])
        nmx = sb("nmx", [P, 16])
        den = sb("den", [P, 16])
        rden = sb("rden", [P, 16])
        row16 = sb("row16", [1, 4, 16])
        table = sb("table", [1, 24], I32)

        with ExitStack() as s:
            u = sb("u", [P, 11264], F32, s)
        with ExitStack() as s:
            f_hi = sb("f_hi", [P, FT, 256], F32R, s)
            f_lo = sb("f_lo", [P, FT, 256], F32R, s)
        with ExitStack() as s:
            e_hi = sb("e_hi", [P, KT, BLK], F32R, s)
            e_lo = sb("e_lo", [P, KT, BLK], F32R, s)
            at_hi = sb("at_hi", [P, 4, BLK], F32R, s)
            at_lo = sb("at_lo", [P, 4, BLK], F32R, s)
            e_sig = sb("e_sig", [P, 512], F32, s)
            e_act = sb("e_act", [P, 512], F32, s)
            pack = sb("pack", [P, 2, BLK], F32, s)
            pgate = sb("pgate", [P, 2, BLK], F32, s)
            spread = sb("spread", [P, 2 * P], F32, s)
            y = sb("y", [P, D], F32, s)
            ones = sb("ones", [P, P], F32, s)
            lg = sb("lg", [P, 12, 16], F32, s)
            pos16 = sb("pos16", [P, 2, 16], F32, s)
            gate16 = sb("gate16", [P, 2, 16], F32, s)
        ctx.enter_context(nc.sbuf_tensor("region", [P, 11264], F32))
        with ExitStack() as s:
            od_o = sb("od_o", [P, 2, D], F32, s)
        m_hi = sb("m_hi", [P, KT, 256], F32R)
        m_lo = sb("m_lo", [P, KT, 256], F32R)

        dmat = u[:, 0:4096].rearrange("p (h n) -> p h n", h=RH)
        xa_v0 = u[:, 0:2048].rearrange("p (t n) -> p t n", t=2)
        ev_v = u[:, 4096:5120].rearrange("p (t n) -> p t n", t=2)
        ev_g = u[:, 5120:6144].rearrange("p (t n) -> p t n", t=2)
        xa_q0 = u[:, 4096:6144].rearrange("p (k n) -> p k n", k=KT)
        ev_qt = u[:, 6144:7168].rearrange("p (k n) -> p k n", k=4)
        ev_kt = u[:, 7168:8192].rearrange("p (k n) -> p k n", k=4)
        xa_k0 = u[:, 8192:10240].rearrange("p (k n) -> p k n", k=KT)
        after_i, before_i = u[:, 10240:10752], u[:, 10752:11264]
        od_qt = u[:, 0:2048].rearrange("p (k n) -> p k n", k=KT)
        xa_q1 = od_qt
        od_kt = u[:, 2048:4096].rearrange("p (k n) -> p k n", k=KT)
        od_v = u[:, 4096:6144].rearrange("p (t n) -> p t n", t=2)
        xa_k1 = u[:, 6144:8192].rearrange("p (k n) -> p k n", k=KT)
        xa_v1 = u[:, 8192:10240].rearrange("p (t n) -> p t n", t=2)
        od_s = od_o[:, :, :]
        tat = ta[:, :].rearrange("p (t n) -> p t n", t=2)
        tbt = tb[:, :].rearrange("p (t n) -> p t n", t=2)
        ev_qr = ta[:, 0:1024].rearrange("p (t n) -> p t n", t=2)
        ev_kr = ta[:, 1024:2048].rearrange("p (t n) -> p t n", t=2)
        ev_c = tb[:, 0:1024].rearrange("p (k n) -> p k n", k=4)
        ev_u = tb[:, 1024:2048].rearrange("p (k n) -> p k n", k=4)
        ret_s = ta[:, :].rearrange("p (s j i) -> p s j i", s=4, j=2)
        xa_p = ta[:, :].rearrange("p (h t m) -> p h t m", h=XH, t=2)
        xa_pt = tb[:, :].rearrange("p (h m l) -> p h m l", h=XH, m=2)
        od_p = ta[:, :].rearrange("p (s g t k) -> p s g t k", s=2, g=2, t=2)
        od_pt = tb[:, :].rearrange("p (s k q) -> p s k q", s=4, k=2)
        f_sig, f_act = ta[:, 0:512], ta[:, 512:1024]
        fin_g = tb[:, 0:D]
        fin_o = u[:, 0:2048].rearrange("p (t n) -> p t n", t=2)

        ps = ctx.enter_context(nc.psum_tensor("ps", [P, 8, 512], F32))

        def pair(b):
            return ps[:, b, :].rearrange("p (a n) -> p a n", a=2)

        in_x, in_mem, in_row, in_const, in_pos, in_misc, in_fin = (sem(n) for n in (
            "in_x", "in_mem", "in_row", "in_const", "in_pos", "in_misc", "in_fin"))
        raw_in = [sem(f"raw_in{i}") for i in range(RAW)]
        hi_cut, lo_cut, slab_used, acc_free = sem("hi_cut"), sem("lo_cut"), sem("slab_used"), sem("acc_free")
        act_link, dve_link, pool_link = sem("act_link"), sem("dve_link"), sem("pool_link")
        setup_t, setup_v, setup_s = sem("setup_t"), sem("setup_v"), sem("setup_s")
        n_sq, n_var, n_rstd, n_out = sem("n_sq"), sem("n_var"), sem("n_rstd"), sem("n_out")
        t_ps, t_hi, t_lo = sem("t_ps"), sem("t_hi"), sem("t_lo")
        g_silu, d_exp, d_got = sem("g_silu"), sem("d_exp"), sem("d_got")
        qk_ps, qk_t = sem("qk_ps"), sem("qk_t")
        conv_hi, conv_lo = sem("conv_hi"), sem("conv_lo")
        rs_ps, rs_dec, rs_o, sq_heads = sem("rs_ps"), sem("rs_dec"), sem("rs_o"), sem("sq_heads")
        xs_ps, xs_mx, xs_exp, xs_n, xs_tp, xs_t, xs_o, xs_hi, xs_lo = (sem(n) for n in (
            "xs_ps", "xs_mx", "xs_exp", "xs_n", "xs_tp", "xs_t", "xs_o", "xs_hi", "xs_lo"))
        f_silu, f_mul, f_rnd, f_low, f_add = (sem(n) for n in ("f_silu", "f_mul", "f_rnd", "f_low", "f_add"))
        oq_ps, oq_t = sem("oq_ps"), sem("oq_t")
        ds_ps, ds_mx, ds_exp, ds_c, ds_tp, ds_t, ds_o, ds_out, lam_e, lam_s = (sem(n) for n in (
            "ds_ps", "ds_mx", "ds_exp", "ds_c", "ds_tp", "ds_t", "ds_o", "ds_out", "lam_e", "lam_s"))
        r_ps, r_m, r_cnt, r_tab, r_e, r_w = (sem(n) for n in ("r_ps", "r_m", "r_cnt", "r_tab", "r_e", "r_w"))
        packed, e_ps, e_h, e_l = sem("packed"), sem("e_ps"), sem("e_h"), sem("e_l")
        g_sig, act_rdy = sem("g_sig"), sem("act_rdy")
        at_ps, at_h, at_l = sem("at_ps"), sem("at_h"), sem("at_l")
        pg_rdy, pg_ps, pg_t = sem("pg_rdy"), sem("pg_ps"), sem("pg_t")
        y_sb, c_ps, x_half, combined, out_rdy, out_done = (sem(n) for n in (
            "y_sb", "c_ps", "x_half", "combined", "out_rdy", "out_done"))

        def kpn(w):
            return w.rearrange("(k p) n -> p k n", p=P)

        wi, od = kpn(ev_w_in[0]), kpn(od_w_in[0])

        def t_slab(w, c0):
            return [w[:, 4 * h:4 * h + 4, c0:c0 + 512] for h in range(2)]

        def f_slab(w, c0):
            return w[:, 0:KT, c0:c0 + 256]

        def t_all(w, c0=0, n=2):
            return [s for b in range(n) for s in t_slab(w, c0 + 512 * b)]

        def f_all(w, c0=0, n=4):
            return [f_slab(w, c0 + 256 * b) for b in range(n)]

        C = ev_conv_w.shape[2]
        slabs = {
            "evq": t_slab(wi, 3 * C), "evk": t_slab(wi, 3 * C + 512), "evv": t_slab(wi, 3 * C + 1024),
            "evg": t_slab(wi, 3 * C + 1536),
            "evc": f_all(wi, C, 2) + f_all(wi, 2 * C, 2) + f_all(wi, 0, 2),
            "evo": t_all(kpn(ev_w_out[0])), "odo": t_all(kpn(od_w_out[0])),
            "odq": t_all(od, 0), "odk": t_all(od, D), "odv": t_all(od, 2 * D),
        }
        for i in range(2):
            slabs[f"q{i}"] = f_all(kpn(xa_wq[i]))
            slabs[f"k{i}"] = f_all(kpn(xa_wkv[i]))
            slabs[f"v{i}"] = t_all(kpn(xa_wkv[i]), D)
            slabs[f"o{i}"] = t_all(kpn(xa_wo[i]))
        ffg, ffu, ffd = kpn(ffd_w_gate[0]), kpn(ffd_w_up[0]), kpn(ffd_w_down[0])
        eg = moe_w_gate[0].rearrange("e (k p) n -> e p k n", p=P)
        eu = moe_w_up[0].rearrange("e (k p) n -> e p k n", p=P)
        ed = moe_w_down[0].rearrange("e (k p) n -> e p k n", p=P)

        def shaped(t, k):
            return t.rearrange("p (k n) -> p k n", k=k)

        G0 = FIRST["moe"]

        def load(sp, n, src, r=0, first=False):
            if not first:
                sp.wait_ge(lo_cut, n - RAW + 1 + RAW * r)
            k = src.shape[1]
            sp.dma_start(shaped(raw[:, n % RAW, :], k), src).then_inc(raw_in[n % RAW], 16)

        def cut_hi(act, n, r=0):
            act.wait_ge(raw_in[n % RAW], 16 * (n // RAW + 1) + 16 * r)
            if n >= CUT:
                act.wait_ge(slab_used, n - CUT + 1 + RAW * r)
            nc.scalar.activation(w_hi[:, n % CUT, :], raw[:, n % RAW, :], ACT.Copy).then_inc(hi_cut, 1)

        def cut_lo(dve, n, r=0):
            dve.wait_ge(hi_cut, n + 1 + RAW * r)
            nc.vector.tensor_tensor(w_lo[:, n % CUT, :], raw[:, n % RAW, :], w_hi[:, n % CUT, :].bitcast(F32),
                                    ALU.subtract).then_inc(lo_cut, 1)

        block = ctx.enter_context(nc.Block())

        @block.sync
        def _(sp):
            sp.dma_start(X[:, :, :], x[0].rearrange("(t p) n -> p t n", p=P)).then_inc(in_x, 16)
            n = 0
            for name, k in STREAM:
                if name in ("fgu", "fdn"):
                    continue
                if name == "odq":
                    n = FIRST["odq"]
                for i, s in enumerate(slabs[name]):
                    load(sp, n + i, s, first=n + i < RAW)
                n += k
                if name == "evk":
                    sp.dma_start(tbt, mem[0].rearrange("(t p) n -> p t n", p=P)).then_inc(in_mem, 16)
                if name == "o0":
                    g = FIRST["fgu"]
                    with sp.Fori(0, 3) as r:
                        for j in range(3):
                            load(sp, g + 2 * j, ffg[:, :, bass.ds(r * 768 + 256 * j, 256)], r)
                            load(sp, g + 2 * j + 1, ffu[:, :, bass.ds(r * 768 + 256 * j, 256)], r)
                    for j in range(9, 11):
                        load(sp, g + 2 * j, f_slab(ffg, 256 * j))
                        load(sp, g + 2 * j + 1, f_slab(ffu, 256 * j))
                    for j in range(11):
                        load(sp, FIRST["fdn"] + j, ffd[:, 2 * j:2 * j + 2, :])

            def expert(q, e):
                def at(w, rows_, c):
                    return w[bass.ds(e, 1), :, rows_, c][0] if not isinstance(e, int) else w[e, :, rows_, c]
                for h in range(2):
                    load(sp, G0 + h, at(eg, slice(4 * h, 4 * h + 4), slice(0, 512)), 7 * q)
                for h in range(2):
                    load(sp, G0 + 2 + h, at(eu, slice(4 * h, 4 * h + 4), slice(0, 512)), 7 * q)
                with sp.Fori(1, NB) as b:
                    r = 7 * q + b - 1
                    for h in range(2):
                        load(sp, G0 + 4 + h, at(eg, slice(4 * h, 4 * h + 4), bass.ds(b * 512, 512)), r)
                    for h in range(2):
                        load(sp, G0 + 6 + h, at(eu, slice(4 * h, 4 * h + 4), bass.ds(b * 512, 512)), r)
                    for h in range(2):
                        load(sp, G0 + 8 + h, at(ed, bass.ds(b * 4 - 4 + 2 * h, 2), slice(0, D)), r)
                for h in range(2):
                    load(sp, G0 + 4 + h, at(ed, slice(4 * NB - 4 + 2 * h, 4 * NB - 2 + 2 * h), slice(0, D)), 7 * q + 6)

            with sp.Fori(0, NE) as q:
                expert(q, q)
            sp.wait_ge(r_tab, 1)
            n_pass = sp.value_load(table[0:1, 0:1], min_val=NE, max_val=NE + 3)
            with sp.If(n_pass > NE):
                with sp.Fori(NE, n_pass) as q:
                    col = sp.value_load(table[0:1, bass.ds(q + 1, 1)], min_val=NE, max_val=2 * NE - 1)
                    expert(q, col - NE)
            for t in range(2):
                sp.wait_ge(out_rdy, t + 1)
                sp.dma_start(out[0, t * P:(t + 1) * P, :], fin_o[:, t, :]).then_inc(out_done, 16)
            sp.wait_ge(out_done, 32)

        @block.gpsimd
        def _(pool):
            c = 0
            for name, w in (("ident", P), ("before", P), ("slot", P), ("freq", 56)):
                a = CONST[name][0]
                pool.dma_start(const[:, c:c + w], consts[:, a:a + w]).then_inc(in_const, 16)
                c += w
            pool.dma_start(after_i, consts[:, CONST["after_i"][0]:CONST["after_i"][1]]).then_inc(in_misc, 16)
            pool.dma_start(before_i, consts[:, CONST["before_i"][0]:CONST["before_i"][1]]).then_inc(in_misc, 16)
            pool.dma_start(decay[:, 0, :], ev_ret_decay_f[0].partition_broadcast(P)).then_inc(in_misc, 16)
            pool.dma_start(decay[:, 1, :], ev_ret_decay_b[0].partition_broadcast(P)).then_inc(in_misc, 16)
            for i, v in enumerate((od_lam_q1, od_lam_k1, od_lam_q2, od_lam_k2)):
                pool.dma_start(lamv[:, i, :], v[0].partition_broadcast(P)).then_inc(in_misc, 16)
            pool.dma_start(router[:, :, :], kpn(moe_router[0])).then_inc(in_misc, 16)
            nc.gpsimd.memset(half[:, :], -0.5).then_inc(pool_link, 1)
            pool.wait_ge(pool_link, 1)

            def root(k, w):
                pool.wait_ge(n_var, k + 1)
                nc.gpsimd.tensor_tensor(rstd[:, 0:w], var[:, 0:w], half[:, 0:w], ALU.pow).then_inc(n_rstd, 1)

            for name, k in NORMS.items():
                if name == "fin":
                    pool.wait_ge(acc_free, BANKS["o1"] + 4)
                    pool.dma_start(fin_g, final_norm_g.partition_broadcast(P)).then_inc(in_fin, 16)
                root(k, 16 if name in ("ret", "dif") else 2)

        @block.scalar
        def _(act):
            links = [0]

            def link(ins):
                links[0] += 1
                ins.then_inc(act_link, 1)
                act.wait_ge(act_link, links[0])

            for name, v in (("mem", mem_norm_g), ("x0", mix_norm_g[0]), ("x1", mix_norm_g[1]), ("xa0", xa_norm_g[0]),
                            ("xa1", xa_norm_g[1]), ("ffn", ffn_norm_g[0]), ("moe", ffn_norm_g[1]),
                            ("ret", ev_ret_gn_g[0]), ("dif", od_gn_g[0])):
                r, k = ROWS[name], v.shape[0] // P
                act.dma_start(rows[r:r + k, :], v.rearrange("(k p) -> k p", p=P)).then_inc(in_row, 16)
            act.dma_start(rows[ROWS["conv"]:N_ROWS, :],
                          ev_conv_w[0].rearrange("j (k p) -> (j k) p", p=P)).then_inc(in_row, 16)
            act.dma_start(pos_i[:, :], positions[0].rearrange("(k p) -> k p", p=P)).then_inc(in_pos, 16)

            def squares(name, src):
                k = 2 * [n for n in NORMS if n not in ("ret", "dif")].index(name)
                for t in range(2):
                    nc.scalar.activation(rot[:, :, :].rearrange("p a n -> p (a n)"), src[:, t, :], ACT.Square,
                                         accum_out=sums[:, t:t + 1]).then_inc(n_sq, 1)
                    act.wait_ge(n_sq, k + t + 1)

            def turn_hi(name, hi, k0=0):
                base, n = TURNS[name]
                for k in range(n):
                    act.wait_ge(t_ps, (base + k) // 2 + 1)
                    nc.scalar.activation(hi[:, k0 + k, :], pair(4 + k // 2)[:, k % 2, :], ACT.Copy,
                                         scale=cols[:, ROWS[name] + k:ROWS[name] + k + 1]).then_inc(t_hi, 1)

            def stage(name, k, events=()):
                events = dict(events)
                for i in range(k):
                    cut_hi(act, FIRST[name] + i + AHEAD)
                    if i in events:
                        events[i]()

            act.wait_ge(in_x, 16)
            squares("x0", X)
            act.wait_ge(setup_v, 3)
            nc.scalar.activation(sin[:, :, :], ang[:, :, :], ACT.Sin).then_inc(setup_s, 1)
            nc.scalar.activation(cos[:, :, :], ang[:, :, :], ACT.Sin, scale=0.5).then_inc(setup_s, 1)
            for n in range(AHEAD):
                cut_hi(act, n)
            act.wait_ge(setup_v, 4)
            turn_hi("x0", a_hi)
            act.wait_ge(in_misc, 9 * 16)
            nc.scalar.activation(decay[:, :, :], decay[:, :, :], ACT.Exp).then_inc(setup_s, 1)
            stage("evq", 2)
            act.wait_ge(in_mem, 16)
            squares("mem", tbt)
            turn_hi("mem", m_hi)
            stage("evk", 2)
            stage("evv", 2)
            for h in range(RH):
                act.wait_ge(d_exp, h + 1)
                nc.scalar.activation(dmat[:, h, :], dmat[:, h, :], ACT.Exp).then_inc(d_got, 1)
            stage("evg", 2)
            stage("evc", 6)
            act.wait_ge(acc_free, BANKS["evc"])
            nc.scalar.activation(ev_g, ev_g, ACT.Silu).then_inc(g_silu, 1)
            act.wait_ge(acc_free, BANKS["evc"] + 6)
            nc.scalar.activation(a_hi[:, 0:4, :], ev_u, ACT.Copy).then_inc(conv_hi, 1)
            stage("k0", 4)
            act.wait_ge(rs_o, 1)
            nc.scalar.activation(ta[:, 0:1024].rearrange("p (t n) -> p t n", t=2), ps[:, 6:8, :],
                                 ACT.Square).then_inc(sq_heads, 1)
            stage("v0", 4)
            turn_hi("ret", a_hi, 4)
            stage("evo", 4)

            def cross(i):
                name = f"xa{i}"
                act.wait_ge(acc_free, BANKS[f"q{i}"])
                squares(name, X)
                turn_hi(name, a_hi)
                stage(f"q{i}", 4)
                for h in range(XH):
                    act.wait_ge(xs_mx, XH * i + h + 1)
                    for t in range(2):
                        nc.scalar.activation(xa_p[:, h, t, :], pair(4 + h)[:, t, :], ACT.Exp,
                                             bias=nmx[:, 2 * h + t:2 * h + t + 1], scale=1.0 / 16.0,
                                             accum_out=den[:, 2 * h + t:2 * h + t + 1]).then_inc(xs_exp, 1)
                for h in range(XH):
                    act.wait_ge(xs_tp, XH * i + h + 1)
                    nc.scalar.activation(xa_pt[:, h, :, :], pair(4 + h), ACT.Copy).then_inc(xs_t, 1)
                for h in range(XH):
                    act.wait_ge(xs_o, XH * i + h + 1)
                    nc.scalar.activation(a_hi[:, 2 * h:2 * h + 2, :], pair(4 + h), ACT.Copy).then_inc(xs_hi, 1)
                stage(f"o{i}", 4)

            cross(0)
            act.wait_ge(acc_free, BANKS["odq"])
            squares("ffn", X)
            turn_hi("ffn", a_hi)
            g = FIRST["fgu"]

            def ff_pair(j, r, f):
                cut_hi(act, g + 2 * j + AHEAD, r)
                act.wait_ge(slab_used, g + 2 * j + 1 + 6 * r)
                nc.scalar.activation(f_sig, ps[:, 2 * (j % 3), :], ACT.Silu).then_inc(f_silu, 1)
                cut_hi(act, g + 2 * j + 1 + AHEAD, r)
                act.wait_ge(f_mul, f + 1)
                nc.scalar.activation(f_hi[:, bass.ds(2 * f, 2), :], f_act.rearrange("p (a n) -> p a n", a=2),
                                     ACT.Copy).then_inc(f_rnd, 1)

            with act.Fori(0, 3) as r:
                for j in range(3):
                    ff_pair(j, r, 3 * r + j)
            for j in range(9, 11):
                ff_pair(j, 0, j)
            stage("fdn", 11)

            act.wait_ge(f_add, 2)
            squares("x1", X)
            turn_hi("x1", a_hi)
            stage("odq", 4)
            stage("odk", 4)
            for b in range(8):
                act.wait_ge(oq_ps, b + 1)
                dst = (od_qt if b < 4 else od_kt)[:, 2 * (b % 4):2 * (b % 4) + 2, :]
                nc.scalar.activation(dst, pair(4 + b % 4), ACT.Copy).then_inc(oq_t, 1)
            stage("odv", 4)
            act.wait_ge(lam_s, 1)
            nc.scalar.activation(lams[:, 2:4], lams[:, 0:2], ACT.Exp).then_inc(lam_e, 1)
            stage("k1", 4)
            stage("v1", 4)

            def d_exps(h):
                act.wait_ge(ds_mx, h + 1)
                if h >= 2:
                    act.wait_ge(ds_tp, h - 1)
                for g_ in range(2):
                    for t in range(2):
                        i = 2 * g_ + t
                        nc.scalar.activation(od_p[:, h % 2, g_, t, :], pair(4 + 2 * (h % 2) + g_)[:, t, :], ACT.Exp,
                                             bias=nmx[:, 4 * (h % 2) + i:4 * (h % 2) + i + 1], scale=0.125,
                                             accum_out=den[:, 4 * (h % 2) + i:4 * (h % 2) + i + 1]).then_inc(ds_exp, 1)

            for h in range(DH + 1):
                if h < DH:
                    d_exps(h)
                if h >= 1:
                    act.wait_ge(ds_tp, h)
                    nc.scalar.activation(od_pt[:, (h - 1) % 4, :, :], pair((h - 1) % 2), ACT.Copy).then_inc(ds_t, 1)
            act.wait_ge(ds_out, DH)
            nc.scalar.activation(tat, od_s, ACT.Square).then_inc(sq_heads, 1)
            turn_hi("dif", a_hi)
            stage("odo", 4)
            cross(1)

            act.wait_ge(acc_free, BANKS["o1"] + 4)
            squares("moe", X)
            turn_hi("moe", a_hi)
            nc.scalar.activation(r_hi[:, :, :], router[:, :, :], ACT.Copy).then_inc(r_w, 1)
            act.wait_ge(r_m, 1)
            nc.scalar.activation(lg[:, 9, 2:4], lg[:, 9, 0:2], ACT.Exp).then_inc(r_e, 1)
            act.wait_ge(r_tab, 1)
            n_pass = act.value_load(table[0:1, 0:1], min_val=NE, max_val=NE + 3)
            nc.scalar.activation(mx[:, 0:1], ident[:, 0:1], ACT.Copy).then_inc(g_sig, 1)

            def pack_hi(k):
                act.wait_ge(e_ps, k + 1)
                for i in range(KT):
                    nc.scalar.activation(e_hi[:, i, :], ps[:, 6 + i // 4, (i % 4) * P:(i % 4 + 1) * P], ACT.Copy,
                                         scale=cols[:, ROWS["moe"] + i:ROWS["moe"] + i + 1]).then_inc(e_h, 1)

            def e_silu(i, opening=0):
                act.wait_ge(slab_used, G0 + 6 * i + opening)
                act.wait_ge(act_rdy, i + 1)
                nc.scalar.activation(e_sig[:, :], ps[:, 0, :], ACT.Silu).then_inc(g_sig, 1)

            def e_turn_hi(i):
                act.wait_ge(at_ps, i + 1)
                nc.scalar.activation(at_hi[:, :, :], shaped(ps[:, 4, :], 4), ACT.Copy).then_inc(at_h, 1)

            pack_hi(0)
            with act.Fori(0, n_pass) as q:
                cut_hi(act, G0 + 2, 7 * q)
                cut_hi(act, G0 + 3, 7 * q)
                e_silu(7 * q, 2)
                cut_hi(act, G0 + 4, 7 * q)
                cut_hi(act, G0 + 5, 7 * q)
                with act.Fori(1, NB) as b:
                    i = 7 * q + b
                    r = i - 1
                    cut_hi(act, G0 + 6, r)
                    cut_hi(act, G0 + 7, r)
                    e_silu(i)
                    e_turn_hi(i - 1)
                    cut_hi(act, G0 + 8, r)
                    cut_hi(act, G0 + 9, r)
                    cut_hi(act, G0 + 4, i)
                    cut_hi(act, G0 + 5, i)
                e_turn_hi(7 * q + NB - 1)
                with act.If(q < n_pass - 1):
                    cut_hi(act, G0, 7 * q + 7)
                    pack_hi(q + 1)
                    cut_hi(act, G0 + 1, 7 * q + 7)
            act.wait_ge(combined, n_pass + 1)
            n_fin = 2 * [n for n in NORMS if n not in ("ret", "dif")].index("fin")
            for t in range(2):
                nc.scalar.activation(rot[:, :, :].rearrange("p a n -> p (a n)"), X[:, t, :], ACT.Square,
                                     accum_out=sums[:, t:t + 1]).then_inc(n_sq, 1)
                act.wait_ge(n_sq, n_fin + t + 1)

        @block.vector
        def _(dve):
            links = [0]

            def link(ins):
                links[0] += 1
                ins.then_inc(dve_link, 1)
                dve.wait_ge(dve_link, links[0])

            V = nc.vector

            def means(name, w, count):
                V.tensor_scalar(var[:, 0:w], sums[:, 0:w], 1.0 / count, EPS, ALU.mult, ALU.add).then_inc(n_var, 1)
                dve.wait_ge(n_rstd, NORMS[name] + 1)

            def norm(name, src, dst):
                k = 2 * [n for n in NORMS if n not in ("ret", "dif")].index(name)
                dve.wait_ge(n_sq, k + 2)
                means(name, 2, D)
                for t in range(2):
                    ins = V.tensor_scalar(dst[:, t, :], src[:, t, :], rstd[:, t:t + 1], None, ALU.mult)
                    ins.then_inc(n_out, 1)

            def turn_lo(name, hi, lo, k0=0):
                base, n = TURNS[name]
                for k in range(n):
                    dve.wait_ge(t_hi, base + (k | 1) + 1)
                    V.scalar_tensor_tensor(out=lo[:, k0 + k, :], in0=pair(4 + k // 2)[:, k % 2, :],
                                           scalar=cols[:, ROWS[name] + k:ROWS[name] + k + 1],
                                           in1=hi[:, k0 + k, :].bitcast(F32), op0=ALU.mult,
                                           op1=ALU.subtract).then_inc(t_lo, 1)

            def stage(name, k, events=()):
                events = dict(events)
                for i in range(k):
                    cut_lo(dve, FIRST[name] + i + AHEAD)
                    if i in events:
                        dve.wait_ge(slab_used, FIRST[name] + i + 1)
                        events[i]()

            def acc(name, i, w):
                b = (BANKS[name] + w * i) % 4
                return ps[:, b:b + w, :] if w > 1 else pair(b)

            def freed(ins, w):
                ins.then_inc(acc_free, w)

            dve.wait_ge(in_pos, 16)
            V.tensor_copy(pos_f[:, :], pos_i[:, :]).then_inc(setup_v, 1)
            dve.wait_ge(setup_t, 1)
            V.tensor_copy(pos[:, :], ps[:, 7, 0:2]).then_inc(setup_v, 1)
            dve.wait_ge(setup_v, 2)
            dve.wait_ge(in_const, 64)
            for t in range(2):
                link(V.tensor_scalar(ang[:, t, :], freq, pos[:, t:t + 1], None, ALU.mult))
            c1 = 6.28125
            rest = 2 * math.pi - c1
            c2 = math.floor(rest * 2 ** 20) / 2 ** 20
            c3 = rest - c2
            big = 12582912.0
            link(V.tensor_scalar(turnsb[:, :, :], ang[:, :, :], 1.0 / (2 * math.pi), None, ALU.mult))
            link(V.tensor_scalar(turnsb[:, :, :], turnsb[:, :, :], big, None, ALU.add))
            link(V.tensor_scalar(turnsb[:, :, :], turnsb[:, :, :], -big, None, ALU.add))
            link(V.scalar_tensor_tensor(out=ang[:, :, :], in0=turnsb[:, :, :], scalar=-c1, in1=ang[:, :, :],
                                        op0=ALU.mult, op1=ALU.add))
            link(V.scalar_tensor_tensor(out=ang[:, :, :], in0=turnsb[:, :, :], scalar=-c2, in1=ang[:, :, :],
                                        op0=ALU.mult, op1=ALU.add))
            link(V.scalar_tensor_tensor(out=ang[:, :, :], in0=turnsb[:, :, :], scalar=-c3, in1=ang[:, :, :],
                                        op0=ALU.mult, op1=ALU.add))
            V.tensor_scalar(ang[:, :, :], ang[:, :, :], 3.141592, -3.141592, ALU.min, ALU.max).then_inc(setup_v, 1)
            dve.wait_ge(setup_t, 2)
            V.tensor_copy(cols[:, :], ps[:, 6, 0:N_ROWS]).then_inc(setup_v, 1)
            dve.wait_ge(setup_v, 4)
            norm("x0", X, tat)
            dr = ROWS["dif"]
            link(V.tensor_scalar(cols[:, dr:dr + 8], cols[:, dr:dr + 8], 1.0 - LAM0, None, ALU.mult))
            for n in range(AHEAD):
                cut_lo(dve, n)
            turn_lo("x0", a_hi, a_lo)
            dve.wait_ge(setup_s, 2)
            link(V.tensor_tensor(cos[:, :, :], cos[:, :, :], cos[:, :, :], ALU.mult))
            link(V.tensor_scalar(cos[:, :, :], cos[:, :, :], -2.0, 1.0, ALU.mult, ALU.add))
            dve.wait_ge(setup_s, 3)
            link(V.tensor_scalar(decay[:, :, :], decay[:, :, :], -1.0, None, ALU.mult))

            def rotate(src, dst, heads, half_, f0, done):
                shape = [P, 2, heads, half_]
                c = cos[:, :, f0:f0 + half_].unsqueeze(2).broadcast_to(shape)
                s = sin[:, :, f0:f0 + half_].unsqueeze(2).broadcast_to(shape)
                s4 = src.rearrange("p t (h d) -> p t h d", h=heads)
                d4 = dst.rearrange("p t (h d) -> p t h d", h=heads)
                x1, x2 = s4[:, :, :, 0:half_], s4[:, :, :, half_:2 * half_]
                n = 2 * heads * half_
                a = rot[:, 0, 0:n].rearrange("p (t h d) -> p t h d", t=2, h=heads)
                b = rot[:, 1, 0:n].rearrange("p (t h d) -> p t h d", t=2, h=heads)
                V.tensor_tensor(a, x1, c, ALU.mult)
                link(V.tensor_tensor(b, x2, s, ALU.mult))
                link(V.tensor_tensor(d4[:, :, :, 0:half_], a, b, ALU.subtract))
                V.tensor_tensor(a, x1, s, ALU.mult)
                link(V.tensor_tensor(b, x2, c, ALU.mult))
                done(V.tensor_tensor(d4[:, :, :, half_:2 * half_], a, b, ALU.add))

            def rotated(ins):
                ins.then_inc(acc_free, 2)

            stage("evq", 2)
            norm("mem", tbt, tbt)
            turn_lo("mem", m_hi, m_lo)
            dve.wait_ge(slab_used, FIRST["evk"])
            rotate(acc("evq", 0, 2), ev_qr, RH, 32, 0, rotated)
            dve.wait_ge(acc_free, BANKS["evk"])
            stage("evk", 2, {1: lambda: rotate(acc("evk", 0, 2), ev_kr, RH, 32, 0, rotated)})
            stage("evv", 2, {1: lambda: freed(V.tensor_copy(ev_v, acc("evv", 0, 2)), 2)})
            dve.wait_ge(in_misc, 9 * 16)
            for h in range(RH):
                link(V.tensor_scalar(dmat[:, h, :], after_i, decay[:, 0, h:h + 1], None, ALU.mult))
                V.scalar_tensor_tensor(out=dmat[:, h, :], in0=before_i, scalar=decay[:, 1, h:h + 1],
                                       in1=dmat[:, h, :], op0=ALU.mult, op1=ALU.add).then_inc(d_exp, 1)

            stage("evg", 2, {1: lambda: freed(V.tensor_copy(ev_g, acc("evg", 0, 2)), 2)})

            def conv_event(i):
                def f():
                    w = ROWS["conv"]
                    s = slice(2 * (i % 2), 2 * (i % 2) + 2)
                    dve.wait_ge(acc_free, BANKS["evc"] + i)
                    if i < 2:
                        freed(V.tensor_copy(ev_c[:, s, :], acc("evc", i, 1)), 1)
                    elif i < 4:
                        freed(V.tensor_tensor(ev_u[:, s, :], acc("evc", i, 1), ev_c[:, s, :], ALU.mult), 1)
                    if i == 3:
                        dve.wait_ge(acc_free, BANKS["evc"] + 4)
                        for k in range(4):
                            link(V.tensor_scalar(ev_c[:, k, :], ev_u[:, k, :], cols[:, w + 4 + k:w + 5 + k], None,
                                                 ALU.mult))
                            link(V.scalar_tensor_tensor(out=ev_c[:, k, 1:256], in0=ev_u[:, k, 0:255],
                                                        scalar=cols[:, w + k:w + k + 1], in1=ev_c[:, k, 1:256],
                                                        op0=ALU.mult, op1=ALU.add))
                            link(V.scalar_tensor_tensor(out=ev_c[:, k, 0:255], in0=ev_u[:, k, 1:256],
                                                        scalar=cols[:, w + 8 + k:w + 9 + k], in1=ev_c[:, k, 0:255],
                                                        op0=ALU.mult, op1=ALU.add))
                    if i >= 4:
                        freed(V.tensor_tensor(ev_u[:, s, :], acc("evc", i, 1), ev_c[:, s, :], ALU.mult), 1)
                return f

            stage("evc", 6, {i: conv_event(i) for i in range(6)})
            dve.wait_ge(conv_hi, 1)
            V.tensor_tensor(a_lo[:, 0:4, :], ev_u, a_hi[:, 0:4, :].bitcast(F32), ALU.subtract).then_inc(conv_lo, 1)
            for b in range(4):
                dve.wait_ge(qk_ps, b + 1)
                dst = (ev_qt if b < 2 else ev_kt)[:, 2 * (b % 2):2 * (b % 2) + 2, :]
                V.tensor_copy(dst, pair(4 + b)).then_inc(qk_t, 1)
            stage("k0", 4, {i: (lambda i=i: freed(V.tensor_copy(xa_k0[:, 2 * i:2 * i + 2, :], acc("k0", i, 1)), 1))
                            for i in range(4)})
            for h in range(RH):
                dve.wait_ge(rs_ps, h + 1)
                dve.wait_ge(d_got, h + 1)
                V.scalar_tensor_tensor(out=ret_s[:, h % 4, :, :].rearrange("p j i -> p (j i)"), in0=ps[:, 4 + h % 2, :],
                                       scalar=0.125, in1=dmat[:, h, :], op0=ALU.mult, op1=ALU.mult).then_inc(rs_dec, 1)
            dve.wait_ge(sq_heads, 1)
            link(V.tensor_reduce(sums[:, 0:16], ta[:, 0:1024].rearrange("p (g d) -> p g d", d=64), AX.X, ALU.add))
            means("ret", 16, 64)
            tn = ta[:, 1024:2048].rearrange("p (g d) -> p g d", d=64)
            link(V.tensor_tensor(tn, ps[:, 6:8, :].rearrange("p t (h d) -> p (t h) d", d=64),
                                 rstd[:, 0:16].unsqueeze(2).broadcast_to([P, 16, 64]), ALU.mult))
            dve.wait_ge(g_silu, 1)
            tr = ta[:, 1024:2048].rearrange("p (t n) -> p t n", t=2)
            V.tensor_tensor(tr, tr, ev_g, ALU.mult).then_inc(n_out, 2)

            def v_event(i, name, dst):
                return lambda: freed(V.tensor_copy(dst[:, :, 512 * i:512 * i + 512], acc(name, i, 2)), 2)

            stage("v0", 4, {1: v_event(0, "v0", xa_v0), 3: v_event(1, "v0", xa_v0)})
            turn_lo("ret", a_hi, a_lo, 4)

            def x_event(i, name):
                def f():
                    s = slice(512 * i, 512 * i + 512)
                    freed(V.tensor_tensor(X[:, :, s], acc(name, i, 2), X[:, :, s], ALU.add), 2)
                return f

            stage("evo", 4, {1: x_event(0, "evo"), 3: x_event(1, "evo")})

            def cross(i, xq):
                name = f"xa{i}"
                norm(name, X, tat)
                turn_lo(name, a_hi, a_lo)

                def q_event(k):
                    return lambda: freed(V.tensor_copy(xq[:, 2 * k:2 * k + 2, :], acc(f"q{i}", k, 1)), 1)

                stage(f"q{i}", 4, {k: q_event(k) for k in range(4)})
                for h in range(XH):
                    dve.wait_ge(xs_ps, XH * i + h + 1)
                    link(V.tensor_reduce(mx[:, 2 * h:2 * h + 2], pair(4 + h), AX.X, ALU.max))
                    V.tensor_scalar(nmx[:, 2 * h:2 * h + 2], mx[:, 2 * h:2 * h + 2], -1.0 / 16.0, None,
                                    ALU.mult).then_inc(xs_mx, 1)
                for h in range(XH):
                    dve.wait_ge(xs_exp, 2 * (XH * i + h + 1))
                    link(V.reciprocal(rden[:, 2 * h:2 * h + 2], den[:, 2 * h:2 * h + 2]))
                    for t in range(2):
                        ins = V.tensor_scalar(xa_p[:, h, t, :], xa_p[:, h, t, :],
                                              rden[:, 2 * h + t:2 * h + t + 1], None, ALU.mult)
                    ins.then_inc(xs_n, 1)
                for h in range(XH):
                    dve.wait_ge(xs_hi, XH * i + h + 1)
                    V.tensor_tensor(a_lo[:, 2 * h:2 * h + 2, :], pair(4 + h), a_hi[:, 2 * h:2 * h + 2, :].bitcast(F32),
                                    ALU.subtract).then_inc(xs_lo, 1)
                stage(f"o{i}", 4, {1: x_event(0, f"o{i}"), 3: x_event(1, f"o{i}")})

            cross(0, xa_q0)
            norm("ffn", X, tat)
            turn_lo("ffn", a_hi, a_lo)
            g = FIRST["fgu"]

            def ff_pair(j, r, f):
                cut_lo(dve, g + 2 * j + AHEAD, r)
                cut_lo(dve, g + 2 * j + 1 + AHEAD, r)
                dve.wait_ge(slab_used, g + 2 * j + 2 + 6 * r)
                dve.wait_ge(f_silu, f + 1)
                V.tensor_tensor(f_act, ps[:, 2 * (j % 3) + 1, :], f_sig, ALU.mult).then_inc(f_mul, 1)
                dve.wait_ge(f_rnd, f + 1)
                V.tensor_tensor(f_lo[:, bass.ds(2 * f, 2), :], f_act.rearrange("p (a n) -> p a n", a=2),
                                f_hi[:, bass.ds(2 * f, 2), :].bitcast(F32), ALU.subtract).then_inc(f_low, 1)
                dve.wait_ge(f_low, f + 1)

            with dve.Fori(0, 3) as r:
                for j in range(3):
                    ff_pair(j, r, 3 * r + j)
            for j in range(9, 11):
                ff_pair(j, 0, j)

            def fd_event():
                for h in range(2):
                    V.tensor_tensor(X[:, :, 512 * h:512 * h + 512], ps[:, 2 * h:2 * h + 2, :],
                                    X[:, :, 512 * h:512 * h + 512], ALU.add).then_inc(f_add, 1)

            stage("fdn", 11, {10: fd_event})

            norm("x1", X, tat)
            turn_lo("x1", a_hi, a_lo)

            def qk_event(i, name, dst):
                def f():
                    d = dst[:, :, 512 * i:512 * i + 512]
                    a = acc(name, i, 2)
                    dve.wait_ge(acc_free, BANKS[name] + 2 * i)
                    link(V.tensor_copy(d, a))
                    rotate(a, d, 8, 8, 32, rotated)
                return f

            stage("odq", 4, {1: qk_event(0, "odq", tat), 3: qk_event(1, "odq", tat)})
            stage("odk", 4, {1: qk_event(0, "odk", tbt), 3: qk_event(1, "odk", tbt)})
            stage("odv", 4, {1: v_event(0, "odv", od_v), 3: v_event(1, "odv", od_v)})
            for i in range(2):
                V.tensor_tensor_reduce(rot[:, i, 0:64], lamv[:, 2 * i, :], lamv[:, 2 * i + 1, :], 1.0, 0.0, ALU.mult,
                                       ALU.add, lams[:, i:i + 1]).then_inc(dve_link, 1)
                links[0] += 1
            dve.wait_ge(dve_link, links[0])
            V.memset(lams[:, 2:4], 0.0).then_inc(lam_s, 1)
            dve.wait_ge(lam_e, 1)
            link(V.tensor_tensor(lams[:, 0:1], lams[:, 3:4], lams[:, 2:3], ALU.subtract))
            link(V.tensor_scalar(lams[:, 0:1], lams[:, 0:1], -LAM0, None, ALU.add))
            stage("k1", 4, {i: (lambda i=i: freed(V.tensor_copy(xa_k1[:, 2 * i:2 * i + 2, :], acc("k1", i, 1)), 1))
                            for i in range(4)})
            stage("v1", 4, {1: v_event(0, "v1", xa_v1), 3: v_event(1, "v1", xa_v1)})

            def d_max(h):
                o = 4 * (h % 2)
                dve.wait_ge(ds_ps, h + 1)
                link(V.tensor_reduce(mx[:, o:o + 4],
                                     ps[:, 4 + o // 2:6 + o // 2, :].rearrange("p g (t k) -> p (g t) k", t=2), AX.X,
                                     ALU.max))
                V.tensor_scalar(nmx[:, o:o + 4], mx[:, o:o + 4], -0.125, None, ALU.mult).then_inc(ds_mx, 1)

            def d_mix(h):
                o = 4 * (h % 2)
                dve.wait_ge(ds_exp, 4 * h + 4)
                link(V.reciprocal(rden[:, o:o + 4], den[:, o:o + 4]))
                link(V.tensor_scalar(rden[:, o + 2:o + 4], rden[:, o + 2:o + 4], lams[:, 0:1], None, ALU.mult))
                for t in range(2):
                    ins = V.tensor_scalar(od_p[:, h % 2, 0, t, :], od_p[:, h % 2, 0, t, :], rden[:, o + t:o + t + 1],
                                          None, ALU.mult)
                link(ins)
                for t in range(2):
                    ins = V.scalar_tensor_tensor(out=od_p[:, h % 2, 0, t, :], in0=od_p[:, h % 2, 1, t, :],
                                                 scalar=rden[:, o + 2 + t:o + 3 + t], in1=od_p[:, h % 2, 0, t, :],
                                                 op0=ALU.mult, op1=ALU.add)
                ins.then_inc(ds_c, 1)

            def d_out(h):
                dve.wait_ge(ds_o, h + 1)
                V.tensor_copy(od_s[:, :, h * P:(h + 1) * P],
                              ps[:, 2 + h % 2, 0:2 * P].rearrange("p (t v) -> p t v", t=2)).then_inc(ds_out, 1)

            d_max(0)
            for h in range(DH):
                if h + 1 < DH:
                    d_max(h + 1)
                d_mix(h)
                if h >= 1:
                    d_out(h - 1)
            d_out(DH - 1)
            dve.wait_ge(sq_heads, 2)
            link(V.tensor_reduce(sums[:, 0:16], ta[:, :].rearrange("p (g d) -> p g d", d=P), AX.X, ALU.add))
            means("dif", 16, P)
            V.tensor_tensor(ta[:, :].rearrange("p (g d) -> p g d", d=P), od_s.rearrange("p t (h d) -> p (t h) d", d=P),
                            rstd[:, 0:16].unsqueeze(2).broadcast_to([P, 16, P]), ALU.mult).then_inc(n_out, 2)
            turn_lo("dif", a_hi, a_lo)
            stage("odo", 4, {1: x_event(0, "odo"), 3: x_event(1, "odo")})
            cross(1, xa_q1)

            norm("moe", X, tat)
            turn_lo("moe", a_hi, a_lo)
            dve.wait_ge(r_w, 1)
            link(V.tensor_tensor(r_lo[:, :, :], router[:, :, :], r_hi[:, :, :].bitcast(F32), ALU.subtract))
            V.memset(ones[:, :], 1.0)
            V.memset(lg[:, 11, 0:1], 0.0).then_inc(r_cnt, 1)
            dve.wait_ge(r_ps, 1)

            def small(i):
                return lg[:, i, :].rearrange("p (t e) -> p t e", t=2)

            def wide(v):
                return v.unsqueeze(2).broadcast_to([P, 2, NE])

            logit, eq, first, one1, left, one2, rank = (small(i) for i in range(7))
            m1, m2, r1 = lg[:, 7, 0:2], lg[:, 7, 2:4], lg[:, 7, 4:6]
            e8 = experts[:, 0:NE].unsqueeze(1).broadcast_to([P, 2, NE])
            link(V.tensor_copy(logit, ps[:, 0, 0:16].rearrange("p (t e) -> p t e", t=2)))
            link(V.tensor_scalar(rank, e8, -1.0, float(NE), ALU.mult, ALU.add))

            def pick(vals, m, one):
                link(V.tensor_reduce(m, vals, AX.X, ALU.max))
                link(V.tensor_tensor(eq, vals, wide(m), ALU.is_equal))
                link(V.tensor_tensor(first, eq, rank, ALU.mult))
                link(V.tensor_reduce(r1, first, AX.X, ALU.max))
                link(V.tensor_tensor(one, rank, wide(r1), ALU.is_equal))

            pick(logit, m1, one1)
            link(V.scalar_tensor_tensor(out=left, in0=one1, scalar=-3e38, in1=logit, op0=ALU.mult, op1=ALU.add))
            pick(left, m2, one2)
            V.tensor_tensor(lg[:, 9, 0:2], m2, m1, ALU.subtract).then_inc(r_m, 1)
            mask = small(8)
            V.tensor_tensor(mask, one1, one2, ALU.add).then_inc(r_cnt, 1)
            dve.wait_ge(r_e, 1)
            w1, w2 = lg[:, 9, 4:6], lg[:, 9, 6:8]
            link(V.tensor_scalar(w1, lg[:, 9, 2:4], 1.0, None, ALU.add))
            link(V.reciprocal(w1, w1))
            link(V.tensor_tensor(w2, w1, lg[:, 9, 2:4], ALU.mult))
            link(V.tensor_tensor(first, one1, wide(w1), ALU.mult))
            link(V.tensor_tensor(left, one2, wide(w2), ALU.mult))
            for b in range(2):
                link(V.tensor_tensor(gate16[:, :, NE * b:NE * b + NE], first, left, ALU.add))
            dve.wait_ge(r_ps, 2)
            cps = ps[:, 1, 0:16].rearrange("p (t e) -> p t e", t=2)
            link(V.tensor_tensor(first, cps, mask, ALU.mult))
            link(V.tensor_tensor(first, first, mask, ALU.add))
            link(V.tensor_scalar(pos16[:, :, 0:NE], first, -1.0, None, ALU.add))
            link(V.tensor_scalar(pos16[:, :, NE:2 * NE], first, -1.0 - BLK, None, ALU.add))
            over, incl, rk, hit = (row16[:, i, 0:8] for i in range(4))
            link(V.tensor_scalar(over, ps[0:1, 1, 16:24], float(BLK), None, ALU.is_gt))
            link(V.tensor_tensor_scan(incl, ones[0:1, 0:8], over, 0.0, ALU.mult, ALU.add))
            link(V.tensor_tensor(rk, incl, over, ALU.subtract))
            link(V.tensor_scalar(row16[:, 0, 8:9], incl[:, 7:8], float(NE), None, ALU.add))
            link(V.tensor_copy(table[:, 0:1], row16[:, 0, 8:9]))
            link(V.tensor_copy(table[:, 1:1 + NE], experts[0:1, 0:NE]))
            for k in range(3):
                link(V.scalar_tensor_tensor(out=hit, in0=rk, scalar=float(k), in1=over, op0=ALU.is_equal,
                                            op1=ALU.mult))
                link(V.tensor_tensor(hit, hit, experts[0:1, NE:2 * NE], ALU.mult))
                link(V.tensor_reduce(row16[:, 1, 8 + k:9 + k], hit, AX.X, ALU.max))
            link(V.tensor_scalar(row16[:, 1, 8:11], row16[:, 1, 8:11], float(NE), None, ALU.max))
            V.tensor_copy(table[:, 1 + NE:4 + NE], row16[:, 1, 8:11]).then_inc(r_tab, 1)
            dve.wait_ge(r_tab, 1)
            n_pass = dve.value_load(table[0:1, 0:1], min_val=NE, max_val=NE + 3)
            V.memset(lg[:, 11, 1:2], 0.0).then_inc(act_rdy, 1)
            V.memset(lg[:, 11, 2:3], 0.0).then_inc(combined, 1)

            def column(k):
                return dve.value_load(table[0:1, bass.ds(k + 1, 1)], min_val=0, max_val=2 * NE - 1)

            def pack_tokens(col):
                for t in range(2):
                    ins = V.tensor_scalar(pack[:, t, :], slot, pos16[:, t, bass.ds(col, 1)], None, ALU.is_equal)
                ins.then_inc(packed, 1)

            def pack_lo(k):
                for i in range(KT):
                    dve.wait_ge(e_h, KT * k + 4 * (i // 4) + 4)
                    ins = V.scalar_tensor_tensor(out=e_lo[:, i, :], in0=ps[:, 6 + i // 4, (i % 4) * P:(i % 4 + 1) * P],
                                                 scalar=cols[:, ROWS["moe"] + i:ROWS["moe"] + i + 1],
                                                 in1=e_hi[:, i, :].bitcast(F32), op0=ALU.mult, op1=ALU.subtract)
                ins.then_inc(e_l, 1)

            def e_mul(i, opening=0):
                dve.wait_ge(slab_used, G0 + 6 * i + 2 + opening)
                dve.wait_ge(g_sig, i + 2)
                V.tensor_tensor(e_act[:, :], ps[:, 1, :], e_sig[:, :], ALU.mult).then_inc(act_rdy, 1)

            def e_turn_lo(i):
                dve.wait_ge(at_h, i + 1)
                V.tensor_tensor(at_lo[:, :, :], shaped(ps[:, 4, :], 4), at_hi[:, :, :].bitcast(F32),
                                ALU.subtract).then_inc(at_l, 1)

            pack_tokens(column(0))
            pack_lo(0)
            with dve.Fori(0, n_pass) as q:
                cut_lo(dve, G0 + 2, 7 * q)
                col = column(q)
                for t in range(2):
                    ins = V.tensor_scalar(pgate[:, t, :], slot, pos16[:, t, bass.ds(col, 1)],
                                          gate16[:, t, bass.ds(col, 1)], ALU.is_equal, ALU.mult)
                ins.then_inc(pg_rdy, 1)
                cut_lo(dve, G0 + 3, 7 * q)
                cut_lo(dve, G0 + 4, 7 * q)
                cut_lo(dve, G0 + 5, 7 * q)
                e_mul(7 * q, 2)
                dve.wait_ge(pg_ps, q + 1)
                V.tensor_copy(spread[:, :], ps[:, 5, 0:256]).then_inc(pg_t, 1)
                with dve.Fori(1, NB) as b:
                    i = 7 * q + b
                    r = i - 1
                    cut_lo(dve, G0 + 6, r)
                    cut_lo(dve, G0 + 7, r)
                    e_turn_lo(i - 1)
                    cut_lo(dve, G0 + 8, r)
                    cut_lo(dve, G0 + 9, r)
                    e_mul(i)
                    cut_lo(dve, G0 + 4, i)
                    cut_lo(dve, G0 + 5, i)
                e_turn_lo(7 * q + NB - 1)
                with dve.If(q < n_pass - 1):
                    pack_tokens(column(q + 1))
                    cut_lo(dve, G0, 7 * q + 7)
                    pack_lo(q + 1)
                    cut_lo(dve, G0 + 1, 7 * q + 7)
                dve.wait_ge(slab_used, G0 + PASS + PASS * q)
                V.tensor_copy(y[:, :], ps[:, 2:4, :].rearrange("p a n -> p (a n)")).then_inc(y_sb, 1)
                for t in range(2):
                    b0 = 6 if t == 0 else 2
                    dve.wait_ge(c_ps, 2 * q + t + 1)
                    V.tensor_tensor(X[:, t, :], ps[:, b0:b0 + 2, :].rearrange("p a n -> p (a n)"), X[:, t, :],
                                    ALU.add).then_inc(x_half if t == 0 else combined, 1)
            dve.wait_ge(in_fin, 16)
            norm("fin", X, tat)
            for t in range(2):
                dve.wait_ge(n_out, 2 * NORMS["fin"] + t + 1)
                V.tensor_tensor(fin_o[:, t, :], tat[:, t, :], fin_g, ALU.mult).then_inc(out_rdy, 1)

        @block.tensor
        def _(pe):
            T = nc.tensor

            def cuts(ah, al, wh, wl):
                return ((ah, wh), (ah, wl), (al, wh))

            def slab_ready(n, r=0):
                pe.wait_ge(lo_cut, n + 1 + RAW * r)

            def room(name, upto):
                if upto > 4:
                    pe.wait_ge(acc_free, upto - 4)

            def gemm_t(name, blocks, hi, lo, prior=None):
                for b in range(blocks):
                    c = BANKS[name] + 2 * b
                    room(name, c + 2)
                    for h in range(2):
                        n = FIRST[name] + 2 * b + h
                        slab_ready(n)
                        wh, wl = (shaped(w[:, n % CUT, :], 4) for w in (w_hi, w_lo))
                        for k in range(4):
                            for t in range(2):
                                ah, al = (a[:, 4 * h + k, t * P:(t + 1) * P] for a in (hi, lo))
                                for j, (s, m) in enumerate(cuts(ah, al, wh[:, k, :], wl[:, k, :])):
                                    mm = T.matmul(ps[:, (c + t) % 4, :], s, m, start=(h == 0 and k == 0 and j == 0),
                                                  stop=(h == 1 and k == 3 and j == 2))
                        mm.then_inc(slab_used, 1)

            def fm_slab(n, r, bank, hi, lo):
                slab_ready(n, r)
                wh, wl = (shaped(w[:, n % CUT, :], KT) for w in (w_hi, w_lo))
                for o in range(2):
                    for k in range(KT):
                        s_hi, s_lo = (w[:, k, o * P:(o + 1) * P] for w in (wh, wl))
                        for j, (s, m) in enumerate(cuts(s_hi, s_lo, hi[:, k, :], lo[:, k, :])):
                            mm = T.matmul(pair(bank)[:, o, :], s, m, start=(k == 0 and j == 0),
                                          stop=(k == KT - 1 and j == 2))
                mm.then_inc(slab_used, 1)

            def gemm_f(name, count, hi, lo):
                for i in range(count):
                    c = BANKS[name] + i
                    room(name, c + 1)
                    fm_slab(FIRST[name] + i, 0, c % 4, hi, lo)

            def turn(name, src, after):
                base, n = TURNS[name]
                pe.wait_ge(n_out, 2 * after)
                for b in range(n // 2):
                    for k in (2 * b, 2 * b + 1):
                        for t in range(2):
                            mm = T.transpose(pair(4 + b)[:, k % 2, t * P:(t + 1) * P], src[:, t, k * P:(k + 1) * P],
                                             ident)
                    mm.then_inc(t_ps, 1)

            def turned(name):
                base, n = TURNS[name]
                pe.wait_ge(t_lo, base + n)

            pe.wait_ge(in_const, 64)
            pe.wait_ge(setup_v, 1)
            T.transpose(ps[:, 7, 0:2], pos_f[:, :], ident[0:2, 0:2]).then_inc(setup_t, 1)
            pe.wait_ge(in_row, 160)
            T.transpose(ps[:, 6, 0:N_ROWS], rows[:, :], ident[0:N_ROWS, 0:N_ROWS]).then_inc(setup_t, 1)
            pe.wait_ge(setup_v, 4)
            turn("x0", tat, 1)
            turned("x0")
            gemm_t("evq", 1, a_hi, a_lo)
            turn("mem", tbt, 2)
            gemm_t("evk", 1, a_hi, a_lo)
            gemm_t("evv", 1, a_hi, a_lo)
            gemm_t("evg", 1, a_hi, a_lo)
            gemm_f("evc", 6, a_hi, a_lo)
            turned("mem")
            pe.wait_ge(acc_free, BANKS["evv"])
            for b in range(4):
                src = ev_qr if b < 2 else ev_kr
                for k in (2 * (b % 2), 2 * (b % 2) + 1):
                    for t in range(2):
                        mm = T.transpose(pair(4 + b)[:, k % 2, t * P:(t + 1) * P], src[:, t, k * P:(k + 1) * P], ident)
                mm.then_inc(qk_ps, 1)
            gemm_f("k0", 4, m_hi, m_lo)
            pe.wait_ge(qk_t, 4)

            def ret_scores(h):
                if h >= 2:
                    pe.wait_ge(rs_dec, h - 1)
                a, hp = 64 * (h % 2), h // 2
                for j in range(2):
                    mm = T.matmul(pair(4 + h % 2)[:, j, :], ev_kt[a:a + 64, hp, j * P:(j + 1) * P],
                                  ev_qt[a:a + 64, hp, :], start=True, stop=True)
                mm.then_inc(rs_ps, 1)

            ret_scores(0)
            ret_scores(1)
            for h in range(RH):
                pe.wait_ge(rs_dec, h + 1)
                for t in range(2):
                    for j in range(2):
                        mm = T.matmul(ps[:, 6 + t, 64 * h:64 * h + 64], ret_s[:, h % 4, j, t * P:(t + 1) * P],
                                      ev_v[:, j, 64 * h:64 * h + 64], start=(j == 0), stop=(j == 1))
                if h + 2 < RH:
                    ret_scores(h + 2)
            mm.then_inc(rs_o, 1)
            gemm_t("v0", 2, m_hi, m_lo)
            turn("ret", ta[:, 1024:2048].rearrange("p (t n) -> p t n", t=2), 3)
            turned("ret")
            pe.wait_ge(conv_lo, 1)
            gemm_t("evo", 2, a_hi, a_lo)

            def cross(i, xq, xk, xv):
                name = f"xa{i}"
                turn(name, tat, NORMS[name] + 1)
                turned(name)
                gemm_f(f"q{i}", 4, a_hi, a_lo)
                for h in range(XH):
                    pe.wait_ge(acc_free, BANKS[f"q{i}"] + h + 1)
                    for t in range(2):
                        for k in range(2):
                            mm = T.matmul(pair(4 + h)[:, t, :], xq[:, 2 * h + k, t * P:(t + 1) * P],
                                          xk[:, 2 * h + k, :], start=(k == 0), stop=(k == 1))
                    mm.then_inc(xs_ps, 1)
                for h in range(XH):
                    pe.wait_ge(xs_n, XH * i + h + 1)
                    for m in range(2):
                        for t in range(2):
                            mm = T.transpose(pair(4 + h)[:, m, t * P:(t + 1) * P], xa_p[:, h, t, m * P:(m + 1) * P],
                                             ident)
                    mm.then_inc(xs_tp, 1)
                for h in range(XH):
                    pe.wait_ge(xs_t, XH * i + h + 1)
                    for d in range(2):
                        for m in range(2):
                            mm = T.matmul(pair(4 + h)[:, d, :], xv[:, m, 256 * h + d * P:256 * h + (d + 1) * P],
                                          xa_pt[:, h, m, :], start=(m == 0), stop=(m == 1))
                    mm.then_inc(xs_o, 1)
                pe.wait_ge(xs_lo, XH * (i + 1))
                gemm_t(f"o{i}", 2, a_hi, a_lo)

            cross(0, xa_q0, xa_k0, xa_v0)

            turn("ffn", tat, NORMS["ffn"] + 1)
            turned("ffn")
            pe.wait_ge(acc_free, BANKS["odq"])
            g = FIRST["fgu"]

            def ff_pair(j, r, f, first=False):
                if not first:
                    pe.wait_ge(f_low, f - 2)
                fm_slab(g + 2 * j, r, 2 * (j % 3), a_hi, a_lo)
                fm_slab(g + 2 * j + 1, r, 2 * (j % 3) + 1, a_hi, a_lo)

            for j in range(3):
                ff_pair(j, 0, j, first=True)
            with pe.Fori(1, 3) as r:
                for j in range(3):
                    ff_pair(j, r, 3 * r + j)
            for j in range(9, 11):
                ff_pair(j, 0, j)
            for i in range(11):
                pe.wait_ge(f_low, 11)
                n = FIRST["fdn"] + i
                slab_ready(n)
                wh, wl = (shaped(w[:, n % CUT, :], 2) for w in (w_hi, w_lo))
                for k in range(2):
                    for t in range(2):
                        ah, al = (a[:, 2 * i + k, t * P:(t + 1) * P] for a in (f_hi, f_lo))
                        for h in range(2):
                            s = slice(512 * h, 512 * h + 512)
                            for j, (st, mv) in enumerate(cuts(ah, al, wh[:, k, s], wl[:, k, s])):
                                mm = T.matmul(ps[:, 2 * h + t, :], st, mv, start=(i == 0 and k == 0 and j == 0),
                                              stop=(i == 10 and k == 1 and j == 2))
                mm.then_inc(slab_used, 1)

            turn("x1", tat, NORMS["x1"] + 1)
            turned("x1")
            gemm_t("odq", 2, a_hi, a_lo)
            gemm_t("odk", 2, a_hi, a_lo)
            for b in range(8):
                if b % 4 == 0:
                    pe.wait_ge(acc_free, BANKS["odk" if b == 0 else "odv"])
                if b >= 4:
                    pe.wait_ge(oq_t, b - 3)
                src = tat if b < 4 else tbt
                for k in (2 * (b % 4), 2 * (b % 4) + 1):
                    for t in range(2):
                        mm = T.transpose(pair(4 + b % 4)[:, k % 2, t * P:(t + 1) * P], src[:, t, k * P:(k + 1) * P],
                                         ident)
                mm.then_inc(oq_ps, 1)
            gemm_t("odv", 2, a_hi, a_lo)
            gemm_f("k1", 4, m_hi, m_lo)
            gemm_t("v1", 2, m_hi, m_lo)
            pe.wait_ge(oq_t, 8)
            pe.wait_ge(acc_free, BANKS["odo"])

            def d_scores(h):
                if h >= 2:
                    pe.wait_ge(ds_exp, 4 * (h - 1))
                for g_ in range(2):
                    a = 64 * g_
                    for t in range(2):
                        mm = T.matmul(pair(4 + 2 * (h % 2) + g_)[:, t, :], od_qt[a:a + 64, h, t * P:(t + 1) * P],
                                      od_kt[a:a + 64, h, :], start=True, stop=True)
                mm.then_inc(ds_ps, 1)

            d_scores(0)
            d_scores(1)
            for h in range(DH):
                pe.wait_ge(ds_c, h + 1)
                for k in range(2):
                    for t in range(2):
                        mm = T.transpose(pair(h % 2)[:, k, t * P:(t + 1) * P], od_p[:, h % 2, 0, t, k * P:(k + 1) * P],
                                         ident)
                mm.then_inc(ds_tp, 1)
                if h + 2 < DH:
                    d_scores(h + 2)
                pe.wait_ge(ds_t, h + 1)
                if h >= 2:
                    pe.wait_ge(ds_out, h - 1)
                for t in range(2):
                    for k in range(2):
                        mm = T.matmul(ps[:, 2 + h % 2, t * P:(t + 1) * P], od_pt[:, h % 4, k, t * P:(t + 1) * P],
                                      od_v[:, k, h * P:(h + 1) * P], start=(k == 0), stop=(k == 1))
                mm.then_inc(ds_o, 1)
            turn("dif", tat, NORMS["dif"] + 1)
            turned("dif")
            gemm_t("odo", 2, a_hi, a_lo)
            cross(1, xa_q1, xa_k1, xa_v1)

            turn("moe", tat, NORMS["moe"] + 1)
            turned("moe")
            pe.wait_ge(r_cnt, 1)
            pe.wait_ge(acc_free, BANKS["o1"] + 4)
            for t in range(2):
                for k in range(KT):
                    ah, al = (a[:, k, t * P:(t + 1) * P] for a in (a_hi, a_lo))
                    for j, (s, m) in enumerate(cuts(ah, al, r_hi[:, k, :], r_lo[:, k, :])):
                        mm = T.matmul(ps[:, 0, 8 * t:8 * t + 8], s, m, start=(k == 0 and j == 0),
                                      stop=(k == KT - 1 and j == 2))
            mm.then_inc(r_ps, 1)
            pe.wait_ge(r_cnt, 2)
            mask = lg[:, 8, :]
            T.matmul(ps[:, 1, 0:8], before, mask[:, 0:8], start=True, stop=True)
            T.matmul(ps[:, 1, 8:16], before, mask[:, 8:16], start=True, stop=False)
            T.matmul(ps[:, 1, 8:16], ones[:, :], mask[:, 0:8], start=False, stop=True)
            T.matmul(ps[:, 1, 16:24], ones[:, :], mask[:, 0:8], start=True, stop=False)
            T.matmul(ps[:, 1, 16:24], ones[:, :], mask[:, 8:16], start=False, stop=True).then_inc(r_ps, 1)
            pe.wait_ge(r_tab, 1)
            n_pass = pe.value_load(table[0:1, 0:1], min_val=NE, max_val=NE + 3)

            def gather(k):
                pe.wait_ge(packed, k + 1)
                for i in range(KT):
                    for t in range(2):
                        mm = T.matmul(ps[:, 6 + i // 4, (i % 4) * P:(i % 4 + 1) * P], tat[:, t, i * P:(i + 1) * P],
                                      pack[:, t, :], start=(t == 0), stop=(t == 1))
                mm.then_inc(e_ps, 1)

            def half_in(n, r, bank, h):
                slab_ready(n, r)
                wh, wl = (shaped(w[:, n % CUT, :], 4) for w in (w_hi, w_lo))
                for k in range(4):
                    ah, al = e_hi[:, 4 * h + k, :], e_lo[:, 4 * h + k, :]
                    for j, (s, m) in enumerate(cuts(ah, al, wh[:, k, :], wl[:, k, :])):
                        mm = T.matmul(ps[:, bank, :], s, m, start=(h == 0 and k == 0 and j == 0),
                                      stop=(h == 1 and k == 3 and j == 2))
                mm.then_inc(slab_used, 1)

            def turn_act(i):
                pe.wait_ge(act_rdy, i + 2)
                for k in range(4):
                    mm = T.transpose(ps[:, 4, k * P:(k + 1) * P], e_act[:, k * P:(k + 1) * P], ident)
                mm.then_inc(at_ps, 1)

            def down(n, r, i, first, last):
                pe.wait_ge(at_l, i + 1)
                for h in range(2):
                    slab_ready(n + h, r)
                    wh, wl = (shaped(w[:, (n + h) % CUT, :], 2) for w in (w_hi, w_lo))
                    for k in range(2):
                        ah, al = at_hi[:, 2 * h + k, :], at_lo[:, 2 * h + k, :]
                        for o in range(2):
                            c = slice(512 * o, 512 * o + 512)
                            for j, (s, m) in enumerate(cuts(ah, al, wh[:, k, c], wl[:, k, c])):
                                mm = T.matmul(ps[:, 2 + o, :], s, m,
                                              start=(first and h == 0 and k == 0 and j == 0),
                                              stop=(last and h == 1 and k == 1 and j == 2), skip_group_check=True)
                    mm.then_inc(slab_used, 1)

            gather(0)
            with pe.Fori(0, n_pass) as q:
                pe.wait_ge(e_l, q + 1)
                i = 7 * q
                pe.wait_ge(g_sig, i + 1)
                half_in(G0, i, 0, 0)
                half_in(G0 + 1, i, 0, 1)
                pe.wait_ge(act_rdy, i + 1)
                half_in(G0 + 2, i, 1, 0)
                half_in(G0 + 3, i, 1, 1)
                pe.wait_ge(combined, q + 1)
                pe.wait_ge(pg_rdy, q + 1)
                for t in range(2):
                    mm = T.transpose(ps[:, 5, t * P:(t + 1) * P], pgate[:, t, :], ident)
                mm.then_inc(pg_ps, 1)
                for lo_, hi_ in ((1, 2), (2, NB)):
                    with pe.Fori(lo_, hi_) as b:
                        i = 7 * q + b
                        pe.wait_ge(g_sig, i + 1)
                        half_in(G0 + 4, i - 1, 0, 0)
                        half_in(G0 + 5, i - 1, 0, 1)
                        turn_act(i - 1)
                        pe.wait_ge(act_rdy, i + 1)
                        half_in(G0 + 6, i - 1, 1, 0)
                        half_in(G0 + 7, i - 1, 1, 1)
                        down(G0 + 8, i - 1, i - 1, lo_ == 1, False)
                turn_act(7 * q + NB - 1)
                with pe.If(q < n_pass - 1):
                    gather(q + 1)
                down(G0 + 4, 7 * q + 6, 7 * q + NB - 1, False, True)
                pe.wait_ge(y_sb, q + 1)
                pe.wait_ge(pg_t, q + 1)
                with pe.If(q < n_pass - 1):
                    pe.wait_ge(e_l, q + 2)
                for t in range(2):
                    b0 = 6 if t == 0 else 2
                    for o in range(2):
                        mm = T.matmul(ps[:, b0 + o, :], spread[:, t * P:(t + 1) * P], y[:, 512 * o:512 * o + 512],
                                      start=True, stop=True)
                    mm.then_inc(c_ps, 1)


INPUTS = ["x", "mem", "positions", "mem_norm_g", "final_norm_g", "mix_norm_g", "xa_norm_g", "ffn_norm_g", "xa_wq",
          "xa_wkv", "xa_wo", "ev_w_in", "ev_conv_w", "ev_ret_decay_f", "ev_ret_decay_b", "ev_ret_gn_g", "ev_w_out",
          "ffd_w_gate", "ffd_w_up", "ffd_w_down", "od_w_in", "od_lam_q1", "od_lam_k1", "od_lam_q2", "od_lam_k2",
          "od_gn_g", "od_w_out", "moe_router", "moe_w_gate", "moe_w_up", "moe_w_down"]


def kernel(**inputs):
    import concourse.bacc as bacc
    from concourse.bass_utils import run_bass_kernel_spmd

    nc = bacc.Bacc("TRN2", target_bir_lowering=False, num_devices=1)
    arrays, args = {}, {}
    for name in INPUTS + ["consts"]:
        a = constants() if name == "consts" else np.ascontiguousarray(inputs[name])
        arrays[f"in_{name}"] = a
        args[name] = nc.dram_tensor(f"in_{name}", a.shape, mybir.dt.from_np(a.dtype), kind="ExternalInput").ap()
    shape = tuple(inputs["x"].shape)
    args["out"] = nc.dram_tensor("out_0", shape, F32, kind="ExternalOutput").ap()
    trunk_kernel(nc, **args)
    r = run_bass_kernel_spmd(nc, [arrays], core_ids=[0])
    return r.results[0]["out_0"]
```

```python
import math
from contextlib import ExitStack

import numpy as np

import concourse.bass as bass
from concourse import mybir

F32 = mybir.dt.float32
F32R = mybir.dt.float32r
I32 = mybir.dt.int32
ACT = mybir.ActivationFunctionType
ALU = mybir.AluOpType
AX = mybir.AxisListType

P = 128
RAW = 6
CUT = 3
AHEAD = CUT - 1
EPS = 1e-6

RET_THETA, ROPE_THETA = 10000.0, 500000.0


def shapes(x, mem, moe_gate, ffd_gate, ev_in):
    s = {}
    s["L"], s["D"] = x.shape[1], x.shape[2]
    s["M"] = mem.shape[1]
    s["E"], s["FE"] = moe_gate.shape[1], moe_gate.shape[3]
    s["FF"] = ffd_gate.shape[2]
    return s


STREAM = [("evq", 2), ("evk", 2), ("evv", 2), ("evg", 2), ("evc", 6), ("k0", 4), ("v0a", 2), ("evo", 4),
          ("v0b", 2), ("q0", 4), ("o0", 4), ("k1a", 2), ("fgu", 22), ("fdn", 11), ("k1b", 2), ("odq", 4), ("odk", 4),
          ("odv", 4), ("v1a", 2), ("odo", 4), ("v1b", 2), ("q1", 4), ("o1", 4)]
FIRST = {}
_n = 0
for _name, _k in STREAM:
    FIRST[_name] = _n
    _n += _k
FIRST["moe"] = _n
BANKS = {}
_n = 0
for _name, _k in STREAM:
    if _name not in ("fgu", "fdn"):
        BANKS[_name] = _n
        _n += _k
TURNS = {}
_n = 0
for _name, _k in [("x0", 8), ("mem", 8), ("ret", 4), ("xa0", 8), ("ffn", 8), ("x1", 8), ("dif", 8), ("xa1", 8),
                  ("moe", 8)]:
    TURNS[_name] = (_n, _k)
    _n += _k
NORMS = {n: i for i, n in enumerate(["x0", "mem", "ret", "xa0", "ffn", "x1", "dif", "xa1", "moe", "fin"])}

ROWS = {}
_n = 0
for _name, _k in [("mem", 8), ("x0", 8), ("x1", 8), ("xa0", 8), ("xa1", 8), ("ffn", 8), ("moe", 8), ("ret", 4),
                  ("dif", 8), ("conv", 12)]:
    ROWS[_name] = _n
    _n += _k
N_ROWS = _n

CONST = {}
_n = 0
for _name, _k in [("ident", P), ("before", P), ("slot", P), ("freq", 40), ("experts", 16), ("after_i", 512),
                  ("before_i", 512)]:
    CONST[_name] = (_n, _n + _k)
    _n += _k
N_CONST = _n


def constants():
    c = np.zeros((P, N_CONST), np.float32)
    p = np.arange(P)

    def put(name, a):
        c[:, CONST[name][0]:CONST[name][1]] = a
    put("ident", np.eye(P))
    put("before", (p[:, None] < p[None, :]))
    put("slot", np.broadcast_to(p[None, :], (P, P)))
    j = (np.arange(2)[None, :, None] * P + p[:, None, None])
    d = np.arange(2 * P)[None, None, :] - j
    put("after_i", np.maximum(d, 0).reshape(P, -1))
    put("before_i", np.maximum(-d, 0).reshape(P, -1))
    f = []
    for theta, rot in ((RET_THETA, 64), (ROPE_THETA, 16)):
        half = rot // 2
        f.append(np.exp(np.float32(-math.log(theta)) * np.arange(half, dtype=np.float32) * np.float32(2.0 / rot)))
    put("freq", np.concatenate(f)[None, :].astype(np.float32))
    put("experts", np.arange(16)[None, :])
    return c


def trunk_kernel(nc, x, mem, positions, mem_norm_g, final_norm_g, mix_norm_g, xa_norm_g, ffn_norm_g, xa_wq, xa_wkv,
                 xa_wo, ev_w_in, ev_conv_w, ev_ret_decay_f, ev_ret_decay_b, ev_ret_gn_g, ev_w_out, ffd_w_gate,
                 ffd_w_up, ffd_w_down, od_w_in, od_lam_q1, od_lam_k1, od_lam_q2, od_lam_k2, od_gn_g, od_w_out,
                 moe_router, moe_w_gate, moe_w_up, moe_w_down, consts, out):
    D = x.shape[2]
    KT = D // P
    NE = moe_router.shape[2]
    NB = moe_w_gate.shape[3] // 512
    FT = ffd_w_gate.shape[2] // P
    RH = ev_ret_decay_f.shape[1]
    DH = od_gn_g.shape[1] // P
    XH = 4
    PASS = 6 * NB
    LAM0 = 0.8 - 0.6 * math.exp(-0.3)
    BLK = P

    ctx = ExitStack()
    with ctx:
        def sb(name, shape, dt=F32, stack=ctx):
            return stack.enter_context(nc.sbuf_tensor(name, shape, dt))

        def sem(name):
            return ctx.enter_context(nc.semaphore(name))

        raw = sb("raw", [P, RAW, 2048])
        w_hi = sb("w_hi", [P, CUT, 2048], F32R)
        w_lo = sb("w_lo", [P, CUT, 2048], F32R)
        X = sb("X", [P, 2, D])
        with ExitStack() as s:
            od_o = sb("od_o", [P, 2, D], F32, s)
        a_hi = sb("a_hi", [P, KT, 256], F32R)
        a_lo = sb("a_lo", [P, KT, 256], F32R)
        ta = sb("ta", [P, 2048])
        tb = sb("tb", [P, 2048])
        rot = sb("rot", [P, 2, 512])
        const = sb("const", [P, 3 * P + 56])
        ident, before, slot = const[:, 0:P], const[:, P:2 * P], const[:, 2 * P:3 * P]
        freq, experts = const[:, 3 * P:3 * P + 40], const[:, 3 * P + 40:3 * P + 56]
        rows = sb("rows", [N_ROWS, P])
        cols = sb("cols", [P, N_ROWS])
        pos_i = sb("pos_i", [2, P], I32)
        pos_f = sb("pos_f", [2, P])
        pos = sb("pos", [P, 2])
        ang = sb("ang", [P, 2, 40])
        turnsb = sb("turnsb", [P, 2, 40])
        cos = sb("cos", [P, 2, 40])
        sin = sb("sin", [P, 2, 40])
        decay = sb("decay", [P, 2, RH])
        lamv = sb("lamv", [P, 4, 64])
        lams = sb("lams", [P, 4])
        half = sb("half", [P, 16])
        sums = sb("sums", [P, 16])
        var = sb("var", [P, 16])
        rstd = sb("rstd", [P, 16])
        mx = sb("mx", [P, 16])
        nmx = sb("nmx", [P, 16])
        den = sb("den", [P, 16])
        rden = sb("rden", [P, 16])
        row16 = sb("row16", [1, 4, 16])
        logits = sb("logits", [NE, 256])
        table = sb("table", [1, 24], I32)

        with ExitStack() as s:
            u = sb("u", [P, 11264], F32, s)
        with ExitStack() as s:
            f_hi = sb("f_hi", [P, FT, 256], F32R, s)
            f_lo = sb("f_lo", [P, FT, 256], F32R, s)
        with ExitStack() as s:
            e_hi = sb("e_hi", [P, KT, BLK], F32R, s)
            e_lo = sb("e_lo", [P, KT, BLK], F32R, s)
            at_hi = sb("at_hi", [P, 4, BLK], F32R, s)
            at_lo = sb("at_lo", [P, 4, BLK], F32R, s)
            e_sig = sb("e_sig", [P, 512], F32, s)
            e_act = sb("e_act", [P, 512], F32, s)
            pack = sb("pack", [P, 2, BLK], F32, s)
            pgate = sb("pgate", [P, 2, BLK], F32, s)
            spread = sb("spread", [P, 2 * P], F32, s)
            y = sb("y", [P, D], F32, s)
            ones = sb("ones", [P, P], F32, s)
            lg = sb("lg", [P, 12, 16], F32, s)
            pos16 = sb("pos16", [P, 2, 16], F32, s)
            gate16 = sb("gate16", [P, 2, 16], F32, s)
            sb("gap", [P, 10240 - 6272], F32, s)
            router = sb("router", [P, KT * NE], F32, s)
            r_hi = sb("r_hi", [P, KT * NE + P - NE], F32R, s)
            r_lo = sb("r_lo", [P, KT * NE + P - NE], F32R, s)
        ctx.enter_context(nc.sbuf_tensor("region", [P, 11264], F32))
        m_hi = sb("m_hi", [P, KT, 256], F32R)
        m_lo = sb("m_lo", [P, KT, 256], F32R)

        dmat = u[:, 0:4096].rearrange("p (h n) -> p h n", h=RH)
        xa_v0 = u[:, 0:2048].rearrange("p (t n) -> p t n", t=2)
        ev_v = u[:, 4096:5120].rearrange("p (t n) -> p t n", t=2)
        ev_g = u[:, 5120:6144].rearrange("p (t n) -> p t n", t=2)
        xa_q0 = u[:, 4096:6144].rearrange("p (k n) -> p k n", k=KT)
        ev_qt = u[:, 6144:7168].rearrange("p (k n) -> p k n", k=4)
        ev_kt = u[:, 7168:8192].rearrange("p (k n) -> p k n", k=4)
        xa_k0 = u[:, 8192:10240].rearrange("p (k n) -> p k n", k=KT)
        after_i, before_i = u[:, 10240:10752], u[:, 10752:11264]
        od_qt = u[:, 0:2048].rearrange("p (k n) -> p k n", k=KT)
        xa_q1 = od_qt
        od_kt = u[:, 2048:4096].rearrange("p (k n) -> p k n", k=KT)
        od_v = u[:, 4096:6144].rearrange("p (t n) -> p t n", t=2)
        od_kr = u[:, 6144:8192].rearrange("p (t n) -> p t n", t=2)
        xa_k1 = tb[:, :].rearrange("p (k n) -> p k n", k=KT)
        xa_v1 = u[:, 8192:10240].rearrange("p (t n) -> p t n", t=2)
        od_s = od_o[:, :, :]
        tat = ta[:, :].rearrange("p (t n) -> p t n", t=2)
        tbt = tb[:, :].rearrange("p (t n) -> p t n", t=2)
        ev_qr = ta[:, 0:1024].rearrange("p (t n) -> p t n", t=2)
        ev_kr = ta[:, 1024:2048].rearrange("p (t n) -> p t n", t=2)
        ev_c = tb[:, 0:1024].rearrange("p (k n) -> p k n", k=4)
        ev_u = tb[:, 1024:2048].rearrange("p (k n) -> p k n", k=4)
        ret_s = ta[:, :].rearrange("p (s j i) -> p s j i", s=4, j=2)
        xa_p = ta[:, :].rearrange("p (h t m) -> p h t m", h=XH, t=2)
        xa_pt0 = tb[:, :].rearrange("p (h m l) -> p h m l", h=XH, m=2)
        xa_pt1 = u[:, 6144:8192].rearrange("p (h m l) -> p h m l", h=XH, m=2)
        od_p = ta[:, :].rearrange("p (s g t k) -> p s g t k", s=2, g=2, t=2)
        od_pt = u[:, 6144:8192].rearrange("p (s k q) -> p s k q", s=4, k=2)
        f_sig, f_act = ta[:, 0:512], ta[:, 512:1024]
        fin_g = tb[:, 0:D]
        fin_o = u[:, 0:2048].rearrange("p (t n) -> p t n", t=2)

        ps = ctx.enter_context(nc.psum_tensor("ps", [P, 8, 512], F32))

        def pair(b):
            return ps[:, b, :].rearrange("p (a n) -> p a n", a=2)

        in_x, in_mem, in_row, in_const, in_pos, in_misc, in_fin, in_router = (sem(n) for n in (
            "in_x", "in_mem", "in_row", "in_const", "in_pos", "in_misc", "in_fin",
            "in_router"))
        raw_in = [sem(f"raw_in{i}") for i in range(RAW)]
        hi_cut, lo_cut, slab_used, acc_free = sem("hi_cut"), sem("lo_cut"), sem("slab_used"), sem("acc_free")
        act_link, dve_link, pool_link = sem("act_link"), sem("dve_link"), sem("pool_link")
        setup_t, setup_v, setup_s = sem("setup_t"), sem("setup_v"), sem("setup_s")
        n_sq, n_var, n_rstd, n_out = sem("n_sq"), sem("n_var"), sem("n_rstd"), sem("n_out")
        t_ps, t_hi, t_lo = sem("t_ps"), sem("t_hi"), sem("t_lo")
        g_silu, d_exp, d_got = sem("g_silu"), sem("d_exp"), sem("d_got")
        qk_ps, qk_t = sem("qk_ps"), sem("qk_t")
        conv_hi, conv_lo = sem("conv_hi"), sem("conv_lo")
        rs_ps, rs_dec, rs_o, sq_heads = sem("rs_ps"), sem("rs_dec"), sem("rs_o"), sem("sq_heads")
        xs_ps, xs_mx, xs_exp, xs_n, xs_tp, xs_t, xs_o, xs_hi, xs_lo = (sem(n) for n in (
            "xs_ps", "xs_mx", "xs_exp", "xs_n", "xs_tp", "xs_t", "xs_o", "xs_hi", "xs_lo"))
        f_silu, f_mul, f_rnd, f_low, f_add = (sem(n) for n in ("f_silu", "f_mul", "f_rnd", "f_low", "f_add"))
        oq_ps, oq_t = sem("oq_ps"), sem("oq_t")
        ds_ps, ds_mx, ds_exp, ds_c, ds_tp, ds_t, ds_o, ds_out, lam_e, lam_s = (sem(n) for n in (
            "ds_ps", "ds_mx", "ds_exp", "ds_c", "ds_tp", "ds_t", "ds_o", "ds_out", "lam_e", "lam_s"))
        r_ps, r_m, r_cnt, r_tab, r_e, r_w = (sem(n) for n in ("r_ps", "r_m", "r_cnt", "r_tab", "r_e", "r_w"))
        r_z, r_lt, r_ls = sem("r_z"), sem("r_lt"), sem("r_ls")
        packed, e_ps, e_h, e_l = sem("packed"), sem("e_ps"), sem("e_h"), sem("e_l")
        g_sig, act_rdy = sem("g_sig"), sem("act_rdy")
        at_ps, at_h, at_l = sem("at_ps"), sem("at_h"), sem("at_l")
        pg_rdy, pg_ps, pg_t = sem("pg_rdy"), sem("pg_ps"), sem("pg_t")
        y_sb, c_ps, x_half, combined, out_rdy, out_done = (sem(n) for n in (
            "y_sb", "c_ps", "x_half", "combined", "out_rdy", "out_done"))

        def kpn(w):
            return w.rearrange("(k p) n -> p k n", p=P)

        wi, od = kpn(ev_w_in[0]), kpn(od_w_in[0])

        def t_slab(w, c0):
            return [w[:, 4 * h:4 * h + 4, c0:c0 + 512] for h in range(2)]

        def f_slab(w, c0):
            return w[:, 0:KT, c0:c0 + 256]

        def t_all(w, c0=0, n=2):
            return [s for b in range(n) for s in t_slab(w, c0 + 512 * b)]

        def f_all(w, c0=0, n=4):
            return [f_slab(w, c0 + 256 * b) for b in range(n)]

        C = ev_conv_w.shape[2]
        slabs = {
            "evq": t_slab(wi, 3 * C), "evk": t_slab(wi, 3 * C + 512), "evv": t_slab(wi, 3 * C + 1024),
            "evg": t_slab(wi, 3 * C + 1536),
            "evc": f_all(wi, C, 2) + f_all(wi, 2 * C, 2) + f_all(wi, 0, 2),
            "evo": t_all(kpn(ev_w_out[0])), "odo": t_all(kpn(od_w_out[0])),
            "odq": t_all(od, 0), "odk": t_all(od, D), "odv": t_all(od, 2 * D),
        }
        slabs["k1a"], slabs["k1b"] = (f_all(kpn(xa_wkv[1]), 512 * b, 2) for b in range(2))
        slabs["k0"] = f_all(kpn(xa_wkv[0]))
        for i in range(2):
            slabs[f"q{i}"] = f_all(kpn(xa_wq[i]))
            slabs[f"v{i}a"], slabs[f"v{i}b"] = (t_slab(kpn(xa_wkv[i]), D + 512 * b) for b in range(2))
            slabs[f"o{i}"] = t_all(kpn(xa_wo[i]))
        ffg, ffu, ffd = kpn(ffd_w_gate[0]), kpn(ffd_w_up[0]), kpn(ffd_w_down[0])
        eg = moe_w_gate[0].rearrange("e (k p) n -> e p k n", p=P)
        eu = moe_w_up[0].rearrange("e (k p) n -> e p k n", p=P)
        ed = moe_w_down[0].rearrange("e (k p) n -> e p k n", p=P)

        def shaped(t, k):
            return t.rearrange("p (k n) -> p k n", k=k)

        G0 = FIRST["moe"]

        def load(sp, n, src, r=0, first=False):
            if not first:
                sp.wait_ge(lo_cut, n - RAW + 1 + RAW * r)
            k = src.shape[1]
            sp.dma_start(shaped(raw[:, n % RAW, :], k), src).then_inc(raw_in[n % RAW], 16)

        def cut_hi(act, n, r=0):
            act.wait_ge(raw_in[n % RAW], 16 * (n // RAW + 1) + 16 * r)
            if n >= CUT:
                act.wait_ge(slab_used, n - CUT + 1 + RAW * r)
            nc.scalar.activation(w_hi[:, n % CUT, :], raw[:, n % RAW, :], ACT.Copy).then_inc(hi_cut, 1)

        def cut_lo(dve, n, r=0):
            dve.wait_ge(hi_cut, n + 1 + RAW * r)
            nc.vector.tensor_tensor(w_lo[:, n % CUT, :], raw[:, n % RAW, :], w_hi[:, n % CUT, :].bitcast(F32),
                                    ALU.subtract).then_inc(lo_cut, 1)

        block = ctx.enter_context(nc.Block())

        @block.sync
        def _(sp):
            sp.dma_start(X[:, :, :], x[0].rearrange("(t p) n -> p t n", p=P)).then_inc(in_x, 16)
            sp.dma_start(const[:, :], consts[:, 0:3 * P + 56]).then_inc(in_const, 16)
            for name, k in STREAM:
                if name in ("fgu", "fdn"):
                    continue
                n = FIRST[name]
                for i, s in enumerate(slabs[name]):
                    load(sp, n + i, s, first=n + i < RAW)
                if name == "evq":
                    sp.wait_ge(in_row, 160)
                    sp.dma_start(tbt, mem[0].rearrange("(t p) n -> p t n", p=P)).then_inc(in_mem, 16)
                if name == "k1a":
                    g = FIRST["fgu"]
                    with sp.Fori(0, 3) as r:
                        for j in range(3):
                            load(sp, g + 2 * j, ffg[:, :, bass.ds(r * 768 + 256 * j, 256)], r)
                            load(sp, g + 2 * j + 1, ffu[:, :, bass.ds(r * 768 + 256 * j, 256)], r)
                    for j in range(9, 11):
                        load(sp, g + 2 * j, f_slab(ffg, 256 * j))
                        load(sp, g + 2 * j + 1, f_slab(ffu, 256 * j))
                    for j in range(11):
                        load(sp, FIRST["fdn"] + j, ffd[:, 2 * j:2 * j + 2, :])

            def expert(q, e):
                def at(w, rows_, c):
                    return w[bass.ds(e, 1), :, rows_, c][0] if not isinstance(e, int) else w[e, :, rows_, c]
                for h in range(2):
                    load(sp, G0 + h, at(eg, slice(4 * h, 4 * h + 4), slice(0, 512)), 7 * q)
                for h in range(2):
                    load(sp, G0 + 2 + h, at(eu, slice(4 * h, 4 * h + 4), slice(0, 512)), 7 * q)
                with sp.Fori(1, NB) as b:
                    r = 7 * q + b - 1
                    for h in range(2):
                        load(sp, G0 + 4 + h, at(eg, slice(4 * h, 4 * h + 4), bass.ds(b * 512, 512)), r)
                    for h in range(2):
                        load(sp, G0 + 6 + h, at(eu, slice(4 * h, 4 * h + 4), bass.ds(b * 512, 512)), r)
                    for h in range(2):
                        load(sp, G0 + 8 + h, at(ed, bass.ds(b * 4 - 4 + 2 * h, 2), slice(0, D)), r)
                for h in range(2):
                    load(sp, G0 + 4 + h, at(ed, slice(4 * NB - 4 + 2 * h, 4 * NB - 2 + 2 * h), slice(0, D)), 7 * q + 6)

            with sp.Fori(0, NE) as q:
                expert(q, q)
            sp.wait_ge(r_tab, 1)
            n_pass = sp.value_load(table[0:1, 0:1], min_val=NE, max_val=NE + 3)
            with sp.If(n_pass > NE):
                with sp.Fori(NE, n_pass) as q:
                    col = sp.value_load(table[0:1, bass.ds(q + 1, 1)], min_val=NE, max_val=2 * NE - 1)
                    expert(q, col - NE)
            for t in range(2):
                sp.wait_ge(out_rdy, t + 1)
                sp.dma_start(out[0, t * P:(t + 1) * P, :], fin_o[:, t, :]).then_inc(out_done, 16)
            sp.wait_ge(out_done, 32)

        @block.gpsimd
        def _(pool):
            nc.gpsimd.memset(half[:, :], -0.5).then_inc(pool_link, 1)
            pool.wait_ge(pool_link, 1)

            def root(k, w):
                pool.wait_ge(n_var, k + 1)
                nc.gpsimd.tensor_tensor(rstd[:, 0:w], var[:, 0:w], half[:, 0:w], ALU.pow).then_inc(n_rstd, 1)

            for name, k in NORMS.items():
                if name == "dif":
                    pool.wait_ge(f_add, 2)
                    pool.dma_start(router[:, :].rearrange("p (k e) -> p k e", k=KT),
                                   kpn(moe_router[0])).then_inc(in_router, 16)
                if name == "fin":
                    pool.wait_ge(acc_free, BANKS["o1"] + 4)
                    pool.dma_start(fin_g, final_norm_g.partition_broadcast(P)).then_inc(in_fin, 16)
                root(k, 16 if name in ("ret", "dif") else 2)
                if name == "mem":
                    pool.dma_start(after_i, consts[:, CONST["after_i"][0]:CONST["after_i"][1]]).then_inc(in_misc, 16)
                    pool.dma_start(before_i, consts[:, CONST["before_i"][0]:CONST["before_i"][1]]).then_inc(in_misc, 16)
                    pool.dma_start(decay[:, 0, :], ev_ret_decay_f[0].partition_broadcast(P)).then_inc(in_misc, 16)
                    pool.dma_start(decay[:, 1, :], ev_ret_decay_b[0].partition_broadcast(P)).then_inc(in_misc, 16)
                    for i, v in enumerate((od_lam_q1, od_lam_k1, od_lam_q2, od_lam_k2)):
                        pool.dma_start(lamv[:, i, :], v[0].partition_broadcast(P)).then_inc(in_misc, 16)

        @block.scalar
        def _(act):
            links = [0]

            def link(ins):
                links[0] += 1
                ins.then_inc(act_link, 1)
                act.wait_ge(act_link, links[0])

            act.dma_start(pos_i[:, :], positions[0].rearrange("(k p) -> k p", p=P)).then_inc(in_pos, 16)
            for name, v in (("mem", mem_norm_g), ("x0", mix_norm_g[0]), ("x1", mix_norm_g[1]), ("xa0", xa_norm_g[0]),
                            ("xa1", xa_norm_g[1]), ("ffn", ffn_norm_g[0]), ("moe", ffn_norm_g[1]),
                            ("ret", ev_ret_gn_g[0]), ("dif", od_gn_g[0])):
                r, k = ROWS[name], v.shape[0] // P
                act.dma_start(rows[r:r + k, :], v.rearrange("(k p) -> k p", p=P)).then_inc(in_row, 16)
            act.dma_start(rows[ROWS["conv"]:N_ROWS, :],
                          ev_conv_w[0].rearrange("j (k p) -> (j k) p", p=P)).then_inc(in_row, 16)

            def squares(name, src):
                k = 2 * [n for n in NORMS if n not in ("ret", "dif")].index(name)
                for t in range(2):
                    nc.scalar.activation(rot[:, :, :].rearrange("p a n -> p (a n)"), src[:, t, :], ACT.Square,
                                         accum_out=sums[:, t:t + 1]).then_inc(n_sq, 1)
                    act.wait_ge(n_sq, k + t + 1)

            def turn_hi(name, hi, k0=0):
                base, n = TURNS[name]
                for k in range(n):
                    act.wait_ge(t_ps, (base + k) // 2 + 1)
                    nc.scalar.activation(hi[:, k0 + k, :], pair(4 + k // 2)[:, k % 2, :], ACT.Copy,
                                         scale=cols[:, ROWS[name] + k:ROWS[name] + k + 1]).then_inc(t_hi, 1)

            def stage(name, k, events=()):
                events = dict(events)
                for i in range(k):
                    cut_hi(act, FIRST[name] + i + AHEAD)
                    if i in events:
                        events[i]()

            act.wait_ge(pool_link, 1)
            nc.scalar.activation(mx[:, 15:16], half[:, 0:1], ACT.Square).then_inc(act_link, 1)
            act.wait_ge(in_x, 16)
            squares("x0", X)
            for n in range(AHEAD):
                cut_hi(act, n)
            act.wait_ge(setup_v, 3)
            turn_hi("x0", a_hi)
            act.wait_ge(setup_v, 4)
            nc.scalar.activation(sin[:, :, :], ang[:, :, :], ACT.Sin).then_inc(setup_s, 1)
            nc.scalar.activation(cos[:, :, :], ang[:, :, :], ACT.Sin, scale=0.5).then_inc(setup_s, 1)
            stage("evq", 2)
            act.wait_ge(in_mem, 16)
            squares("mem", tbt)
            turn_hi("mem", m_hi)
            stage("evk", 2)
            stage("evv", 2)
            act.wait_ge(in_misc, 8 * 16)
            nc.scalar.activation(decay[:, :, :], decay[:, :, :], ACT.Exp).then_inc(setup_s, 1)
            stage("evg", 2)
            stage("evc", 6)
            act.wait_ge(acc_free, BANKS["evc"])
            nc.scalar.activation(ev_g, ev_g, ACT.Silu).then_inc(g_silu, 1)
            act.wait_ge(acc_free, BANKS["evc"] + 6)
            nc.scalar.activation(a_hi[:, 0:4, :], ev_u, ACT.Copy).then_inc(conv_hi, 1)

            def decays(heads):
                for h in heads:
                    act.wait_ge(d_exp, h + 1)
                    nc.scalar.activation(dmat[:, h, :], dmat[:, h, :], ACT.Exp).then_inc(d_got, 1)

            decays(range(4))
            stage("k0", 4)
            decays(range(4, RH))
            act.wait_ge(rs_o, 1)
            nc.scalar.activation(ta[:, 0:1024].rearrange("p (t n) -> p t n", t=2), ps[:, 6:8, :],
                                 ACT.Square).then_inc(sq_heads, 1)
            stage("v0a", 2)
            turn_hi("ret", a_hi, 4)
            stage("evo", 4)

            def cross(i, xa_pt):
                name = f"xa{i}"
                act.wait_ge(acc_free, BANKS[f"v{i}b"])
                squares(name, X)
                stage(f"v{i}b", 2)
                turn_hi(name, a_hi)
                stage(f"q{i}", 4)
                for h in range(XH):
                    act.wait_ge(xs_mx, XH * i + h + 1)
                    for t in range(2):
                        nc.scalar.activation(xa_p[:, h, t, :], pair(4 + h)[:, t, :], ACT.Exp,
                                             bias=nmx[:, 2 * h + t:2 * h + t + 1], scale=1.0 / 16.0,
                                             accum_out=den[:, 2 * h + t:2 * h + t + 1]).then_inc(xs_exp, 1)
                for h in range(XH):
                    act.wait_ge(xs_tp, XH * i + h + 1)
                    nc.scalar.activation(xa_pt[:, h, :, :], pair(4 + h), ACT.Copy).then_inc(xs_t, 1)
                for h in range(XH):
                    act.wait_ge(xs_o, XH * i + h + 1)
                    nc.scalar.activation(a_hi[:, 2 * h:2 * h + 2, :], pair(4 + h), ACT.Copy).then_inc(xs_hi, 1)
                stage(f"o{i}", 4)

            cross(0, xa_pt0)
            act.wait_ge(acc_free, BANKS["k1a"])
            squares("ffn", X)
            stage("k1a", 2)
            turn_hi("ffn", a_hi)
            g = FIRST["fgu"]

            def ff_pair(j, r, f):
                cut_hi(act, g + 2 * j + AHEAD, r)
                act.wait_ge(slab_used, g + 2 * j + 1 + 6 * r)
                nc.scalar.activation(f_sig, ps[:, 2 * (j % 3), :], ACT.Silu).then_inc(f_silu, 1)
                cut_hi(act, g + 2 * j + 1 + AHEAD, r)
                act.wait_ge(f_mul, f + 1)
                nc.scalar.activation(f_hi[:, bass.ds(2 * f, 2), :], f_act.rearrange("p (a n) -> p a n", a=2),
                                     ACT.Copy).then_inc(f_rnd, 1)

            with act.Fori(0, 3) as r:
                for j in range(3):
                    ff_pair(j, r, 3 * r + j)
            for j in range(9, 11):
                ff_pair(j, 0, j)
            stage("fdn", 11)

            act.wait_ge(f_add, 2)
            squares("x1", X)
            stage("k1b", 2)
            turn_hi("x1", a_hi)
            stage("odq", 4)
            stage("odk", 4)
            for b in range(8):
                act.wait_ge(oq_ps, b + 1)
                dst = (od_qt if b < 4 else od_kt)[:, 2 * (b % 4):2 * (b % 4) + 2, :]
                nc.scalar.activation(dst, pair(4 + b % 4), ACT.Copy).then_inc(oq_t, 1)
            stage("odv", 4)
            act.wait_ge(lam_s, 1)
            nc.scalar.activation(lams[:, 2:4], lams[:, 0:2], ACT.Exp).then_inc(lam_e, 1)
            act.wait_ge(in_router, 16)
            act.wait_ge(r_z, 1)
            nc.scalar.activation(r_hi[:, 0:KT * NE], router[:, :], ACT.Copy).then_inc(r_w, 1)

            def d_exps(h):
                act.wait_ge(ds_mx, h + 1)
                if h >= 2:
                    act.wait_ge(ds_tp, h - 1)
                for g_ in range(2):
                    for t in range(2):
                        i = 2 * g_ + t
                        nc.scalar.activation(od_p[:, h % 2, g_, t, :], pair(4 + 2 * (h % 2) + g_)[:, t, :], ACT.Exp,
                                             bias=nmx[:, 4 * (h % 2) + i:4 * (h % 2) + i + 1], scale=0.125,
                                             accum_out=den[:, 4 * (h % 2) + i:4 * (h % 2) + i + 1]).then_inc(ds_exp, 1)

            for h in range(DH + 1):
                if h < DH:
                    d_exps(h)
                if h >= 1:
                    act.wait_ge(ds_tp, h)
                    nc.scalar.activation(od_pt[:, (h - 1) % 4, :, :], pair((h - 1) % 2), ACT.Copy).then_inc(ds_t, 1)
            act.wait_ge(ds_out, DH)
            nc.scalar.activation(tat, od_s, ACT.Square).then_inc(sq_heads, 1)
            stage("v1a", 2)
            turn_hi("dif", a_hi)
            stage("odo", 4)
            cross(1, xa_pt1)

            act.wait_ge(acc_free, BANKS["o1"] + 4)
            squares("moe", X)
            turn_hi("moe", a_hi)
            cut_hi(act, G0 + 2)
            act.wait_ge(r_m, 1)
            nc.scalar.activation(lg[:, 9, 2:4], lg[:, 9, 0:2], ACT.Exp).then_inc(r_e, 1)
            act.wait_ge(r_tab, 1)
            n_pass = act.value_load(table[0:1, 0:1], min_val=NE, max_val=NE + 3)
            nc.scalar.activation(mx[:, 0:1], ident[:, 0:1], ACT.Silu).then_inc(g_sig, 1)

            def pack_hi(k):
                for i in range(KT):
                    if i % 4 == 0:
                        act.wait_ge(e_ps, 2 * k + i // 4 + 1)
                    nc.scalar.activation(e_hi[:, i, :], ps[:, 6 + i // 4, (i % 4) * P:(i % 4 + 1) * P], ACT.Copy,
                                         scale=cols[:, ROWS["moe"] + i:ROWS["moe"] + i + 1]).then_inc(e_h, 1)

            def e_silu(i, opening=0):
                act.wait_ge(slab_used, G0 + 6 * i + opening)
                act.wait_ge(act_rdy, i + 1)
                nc.scalar.activation(e_sig[:, :], ps[:, 0, :], ACT.Silu).then_inc(g_sig, 1)

            def e_turn_hi(i):
                act.wait_ge(at_ps, i + 1)
                nc.scalar.activation(at_hi[:, :, :], shaped(ps[:, 4, :], 4), ACT.Copy).then_inc(at_h, 1)

            pack_hi(0)
            with act.Fori(0, n_pass) as q:
                cut_hi(act, G0 + 3, 7 * q)
                e_silu(7 * q, 2)
                cut_hi(act, G0 + 4, 7 * q)
                cut_hi(act, G0 + 5, 7 * q)
                with act.Fori(1, NB) as b:
                    i = 7 * q + b
                    r = i - 1
                    cut_hi(act, G0 + 6, r)
                    cut_hi(act, G0 + 7, r)
                    e_silu(i)
                    e_turn_hi(i - 1)
                    cut_hi(act, G0 + 8, r)
                    cut_hi(act, G0 + 9, r)
                    cut_hi(act, G0 + 4, i)
                    cut_hi(act, G0 + 5, i)
                e_turn_hi(7 * q + NB - 1)
                with act.If(q < n_pass - 1):
                    cut_hi(act, G0, 7 * q + 7)
                    pack_hi(q + 1)
                    cut_hi(act, G0 + 1, 7 * q + 7)
                    cut_hi(act, G0 + 2, 7 * q + 7)
            n_fin = 2 * [n for n in NORMS if n not in ("ret", "dif")].index("fin")
            for t in range(2):
                act.wait_ge(x_half if t == 0 else combined, n_pass + t)
                nc.scalar.activation(rot[:, :, :].rearrange("p a n -> p (a n)"), X[:, t, :], ACT.Square,
                                     accum_out=sums[:, t:t + 1]).then_inc(n_sq, 1)
                act.wait_ge(n_sq, n_fin + t + 1)

        @block.vector
        def _(dve):
            links = [0]

            def link(ins):
                links[0] += 1
                ins.then_inc(dve_link, 1)
                dve.wait_ge(dve_link, links[0])

            V = nc.vector

            def means(name, w, count):
                V.tensor_scalar(var[:, 0:w], sums[:, 0:w], 1.0 / count, EPS, ALU.mult, ALU.add).then_inc(n_var, 1)
                dve.wait_ge(n_rstd, NORMS[name] + 1)

            def norm(name, src, dst):
                k = 2 * [n for n in NORMS if n not in ("ret", "dif")].index(name)
                dve.wait_ge(n_sq, k + 2)
                means(name, 2, D)
                for t in range(2):
                    ins = V.tensor_scalar(dst[:, t, :], src[:, t, :], rstd[:, t:t + 1], None, ALU.mult)
                    ins.then_inc(n_out, 1)

            def turn_lo(name, hi, lo, k0=0):
                base, n = TURNS[name]
                for k in range(n):
                    dve.wait_ge(t_hi, base + (k | 1) + 1)
                    V.scalar_tensor_tensor(out=lo[:, k0 + k, :], in0=pair(4 + k // 2)[:, k % 2, :],
                                           scalar=cols[:, ROWS[name] + k:ROWS[name] + k + 1],
                                           in1=hi[:, k0 + k, :].bitcast(F32), op0=ALU.mult,
                                           op1=ALU.subtract).then_inc(t_lo, 1)

            def stage(name, k, events=()):
                events = dict(events)
                for i in range(k):
                    cut_lo(dve, FIRST[name] + i + AHEAD)
                    if i in events:
                        dve.wait_ge(slab_used, FIRST[name] + i + 1)
                        events[i]()

            def acc(name, i, w):
                b = (BANKS[name] + w * i) % 4
                return ps[:, b:b + w, :] if w > 1 else pair(b)

            def freed(ins, w):
                ins.then_inc(acc_free, w)

            dve.wait_ge(in_pos, 16)
            V.tensor_copy(pos_f[:, :], pos_i[:, :]).then_inc(setup_v, 1)
            dve.wait_ge(setup_t, 1)
            V.tensor_copy(pos[:, :], ps[:, 7, 0:2]).then_inc(setup_v, 1)
            dve.wait_ge(setup_t, 2)
            V.tensor_copy(cols[:, :], ps[:, 6, 0:N_ROWS]).then_inc(setup_v, 1)
            norm("x0", X, tat)
            for n in range(AHEAD):
                cut_lo(dve, n)
            dve.wait_ge(setup_v, 3)
            turn_lo("x0", a_hi, a_lo)
            dr = ROWS["dif"]
            link(V.tensor_scalar(cols[:, dr:dr + 8], cols[:, dr:dr + 8], 1.0 - LAM0, None, ALU.mult))
            for t in range(2):
                link(V.tensor_scalar(ang[:, t, :], freq, pos[:, t:t + 1], None, ALU.mult))
            c1 = 6.28125
            rest = 2 * math.pi - c1
            c2 = math.floor(rest * 2 ** 20) / 2 ** 20
            c3 = rest - c2
            big = 12582912.0
            link(V.tensor_scalar(turnsb[:, :, :], ang[:, :, :], 1.0 / (2 * math.pi), None, ALU.mult))
            link(V.tensor_scalar(turnsb[:, :, :], turnsb[:, :, :], big, None, ALU.add))
            link(V.tensor_scalar(turnsb[:, :, :], turnsb[:, :, :], -big, None, ALU.add))
            link(V.scalar_tensor_tensor(out=ang[:, :, :], in0=turnsb[:, :, :], scalar=-c1, in1=ang[:, :, :],
                                        op0=ALU.mult, op1=ALU.add))
            link(V.scalar_tensor_tensor(out=ang[:, :, :], in0=turnsb[:, :, :], scalar=-c2, in1=ang[:, :, :],
                                        op0=ALU.mult, op1=ALU.add))
            link(V.scalar_tensor_tensor(out=ang[:, :, :], in0=turnsb[:, :, :], scalar=-c3, in1=ang[:, :, :],
                                        op0=ALU.mult, op1=ALU.add))
            V.tensor_scalar(ang[:, :, :], ang[:, :, :], 3.141592, -3.141592, ALU.min, ALU.max).then_inc(setup_v, 1)
            dve.wait_ge(setup_s, 2)
            link(V.tensor_tensor(cos[:, :, :], cos[:, :, :], cos[:, :, :], ALU.mult))
            link(V.tensor_scalar(cos[:, :, :], cos[:, :, :], -2.0, 1.0, ALU.mult, ALU.add))

            def rotate(src, dst, heads, half_, f0, done):
                shape = [P, 2, heads, half_]
                c = cos[:, :, f0:f0 + half_].unsqueeze(2).broadcast_to(shape)
                s = sin[:, :, f0:f0 + half_].unsqueeze(2).broadcast_to(shape)
                s4 = src.rearrange("p t (h d) -> p t h d", h=heads)
                d4 = dst.rearrange("p t (h d) -> p t h d", h=heads)
                x1, x2 = s4[:, :, :, 0:half_], s4[:, :, :, half_:2 * half_]
                n = 2 * heads * half_
                a = rot[:, 0, 0:n].rearrange("p (t h d) -> p t h d", t=2, h=heads)
                b = rot[:, 1, 0:n].rearrange("p (t h d) -> p t h d", t=2, h=heads)
                V.tensor_tensor(a, x1, c, ALU.mult)
                link(V.tensor_tensor(b, x2, s, ALU.mult))
                link(V.tensor_tensor(d4[:, :, :, 0:half_], a, b, ALU.subtract))
                V.tensor_tensor(a, x1, s, ALU.mult)
                link(V.tensor_tensor(b, x2, c, ALU.mult))
                done(V.tensor_tensor(d4[:, :, :, half_:2 * half_], a, b, ALU.add))

            def rotated(ins):
                ins.then_inc(acc_free, 2)

            stage("evq", 2)
            norm("mem", tbt, tbt)
            turn_lo("mem", m_hi, m_lo)
            dve.wait_ge(slab_used, FIRST["evk"])
            rotate(acc("evq", 0, 2), ev_qr, RH, 32, 0, rotated)
            dve.wait_ge(acc_free, BANKS["evk"])
            stage("evk", 2, {1: lambda: rotate(acc("evk", 0, 2), ev_kr, RH, 32, 0, rotated)})
            stage("evv", 2, {1: lambda: freed(V.tensor_copy(ev_v, acc("evv", 0, 2)), 2)})
            dve.wait_ge(setup_s, 3)
            link(V.tensor_scalar(decay[:, :, :], decay[:, :, :], -1.0, None, ALU.mult))

            def exponents(heads):
                for h in heads:
                    link(V.tensor_scalar(dmat[:, h, :], after_i, decay[:, 0, h:h + 1], None, ALU.mult))
                    V.scalar_tensor_tensor(out=dmat[:, h, :], in0=before_i, scalar=decay[:, 1, h:h + 1],
                                           in1=dmat[:, h, :], op0=ALU.mult, op1=ALU.add).then_inc(d_exp, 1)

            stage("evg", 2, {1: lambda: freed(V.tensor_copy(ev_g, acc("evg", 0, 2)), 2)})

            def conv_event(i):
                def f():
                    w = ROWS["conv"]
                    s = slice(2 * (i % 2), 2 * (i % 2) + 2)
                    dve.wait_ge(acc_free, BANKS["evc"] + i)
                    if i < 2:
                        freed(V.tensor_copy(ev_c[:, s, :], acc("evc", i, 1)), 1)
                        exponents(range(2 * i, 2 * i + 2))
                    elif i < 4:
                        freed(V.tensor_tensor(ev_u[:, s, :], acc("evc", i, 1), ev_c[:, s, :], ALU.mult), 1)
                    if i == 3:
                        dve.wait_ge(acc_free, BANKS["evc"] + 4)
                        for k in range(4):
                            link(V.tensor_scalar(ev_c[:, k, :], ev_u[:, k, :], cols[:, w + 4 + k:w + 5 + k], None,
                                                 ALU.mult))
                            link(V.scalar_tensor_tensor(out=ev_c[:, k, 1:256], in0=ev_u[:, k, 0:255],
                                                        scalar=cols[:, w + k:w + k + 1], in1=ev_c[:, k, 1:256],
                                                        op0=ALU.mult, op1=ALU.add))
                            link(V.scalar_tensor_tensor(out=ev_c[:, k, 0:255], in0=ev_u[:, k, 1:256],
                                                        scalar=cols[:, w + 8 + k:w + 9 + k], in1=ev_c[:, k, 0:255],
                                                        op0=ALU.mult, op1=ALU.add))
                    if i >= 4:
                        freed(V.tensor_tensor(ev_u[:, s, :], acc("evc", i, 1), ev_c[:, s, :], ALU.mult), 1)
                return f

            stage("evc", 6, {i: conv_event(i) for i in range(6)})
            dve.wait_ge(conv_hi, 1)
            V.tensor_tensor(a_lo[:, 0:4, :], ev_u, a_hi[:, 0:4, :].bitcast(F32), ALU.subtract).then_inc(conv_lo, 1)
            for b in range(4):
                dve.wait_ge(qk_ps, b + 1)
                dst = (ev_qt if b < 2 else ev_kt)[:, 2 * (b % 2):2 * (b % 2) + 2, :]
                V.tensor_copy(dst, pair(4 + b)).then_inc(qk_t, 1)
            def k_event(name, i, dst, o):
                def f():
                    freed(V.tensor_copy(dst[:, o:o + 2, :], acc(name, i, 1)), 1)
                    if name == "k0":
                        exponents([4 + i])
                return f

            stage("k0", 4, {i: k_event("k0", i, xa_k0, 2 * i) for i in range(4)})
            for h in range(RH):
                dve.wait_ge(rs_ps, h + 1)
                dve.wait_ge(d_got, h + 1)
                V.scalar_tensor_tensor(out=ret_s[:, h % 4, :, :].rearrange("p j i -> p (j i)"), in0=ps[:, 4 + h % 2, :],
                                       scalar=0.125, in1=dmat[:, h, :], op0=ALU.mult, op1=ALU.mult).then_inc(rs_dec, 1)
            dve.wait_ge(sq_heads, 1)
            link(V.tensor_reduce(sums[:, 0:16], ta[:, 0:1024].rearrange("p (g d) -> p g d", d=64), AX.X, ALU.add))
            means("ret", 16, 64)
            tn = ta[:, 1024:2048].rearrange("p (g d) -> p g d", d=64)
            link(V.tensor_tensor(tn, ps[:, 6:8, :].rearrange("p t (h d) -> p (t h) d", d=64),
                                 rstd[:, 0:16].unsqueeze(2).broadcast_to([P, 16, 64]), ALU.mult))
            dve.wait_ge(g_silu, 1)
            tr = ta[:, 1024:2048].rearrange("p (t n) -> p t n", t=2)
            V.tensor_tensor(tr, tr, ev_g, ALU.mult).then_inc(n_out, 2)

            def v_event(i, name, dst, o=0):
                c = 512 * (i + o)
                return lambda: freed(V.tensor_copy(dst[:, :, c:c + 512], acc(name, i, 2)), 2)

            stage("v0a", 2, {1: v_event(0, "v0a", xa_v0)})
            turn_lo("ret", a_hi, a_lo, 4)

            def x_event(i, name):
                def f():
                    s = slice(512 * i, 512 * i + 512)
                    freed(V.tensor_tensor(X[:, :, s], acc(name, i, 2), X[:, :, s], ALU.add), 2)
                return f

            stage("evo", 4, {1: x_event(0, "evo"), 3: x_event(1, "evo")})

            def cross(i, xq, xv):
                name = f"xa{i}"
                norm(name, X, tat)
                stage(f"v{i}b", 2, {1: v_event(0, f"v{i}b", xv, 1)})
                turn_lo(name, a_hi, a_lo)

                def q_event(k):
                    return lambda: freed(V.tensor_copy(xq[:, 2 * k:2 * k + 2, :], acc(f"q{i}", k, 1)), 1)

                stage(f"q{i}", 4, {k: q_event(k) for k in range(4)})
                for h in range(XH):
                    dve.wait_ge(xs_ps, XH * i + h + 1)
                    link(V.tensor_reduce(mx[:, 2 * h:2 * h + 2], pair(4 + h), AX.X, ALU.max))
                    V.tensor_scalar(nmx[:, 2 * h:2 * h + 2], mx[:, 2 * h:2 * h + 2], -1.0 / 16.0, None,
                                    ALU.mult).then_inc(xs_mx, 1)
                for h in range(XH):
                    dve.wait_ge(xs_exp, 2 * (XH * i + h + 1))
                    link(V.reciprocal(rden[:, 2 * h:2 * h + 2], den[:, 2 * h:2 * h + 2]))
                    for t in range(2):
                        ins = V.tensor_scalar(xa_p[:, h, t, :], xa_p[:, h, t, :],
                                              rden[:, 2 * h + t:2 * h + t + 1], None, ALU.mult)
                    ins.then_inc(xs_n, 1)
                for h in range(XH):
                    dve.wait_ge(xs_hi, XH * i + h + 1)
                    V.tensor_tensor(a_lo[:, 2 * h:2 * h + 2, :], pair(4 + h), a_hi[:, 2 * h:2 * h + 2, :].bitcast(F32),
                                    ALU.subtract).then_inc(xs_lo, 1)
                stage(f"o{i}", 4, {1: x_event(0, f"o{i}"), 3: x_event(1, f"o{i}")})

            cross(0, xa_q0, xa_v0)
            norm("ffn", X, tat)
            stage("k1a", 2, {i: k_event("k1a", i, xa_k1, 2 * i) for i in range(2)})
            turn_lo("ffn", a_hi, a_lo)
            g = FIRST["fgu"]

            def ff_pair(j, r, f):
                cut_lo(dve, g + 2 * j + AHEAD, r)
                cut_lo(dve, g + 2 * j + 1 + AHEAD, r)
                dve.wait_ge(slab_used, g + 2 * j + 2 + 6 * r)
                dve.wait_ge(f_silu, f + 1)
                V.tensor_tensor(f_act, ps[:, 2 * (j % 3) + 1, :], f_sig, ALU.mult).then_inc(f_mul, 1)
                dve.wait_ge(f_rnd, f + 1)
                V.tensor_tensor(f_lo[:, bass.ds(2 * f, 2), :], f_act.rearrange("p (a n) -> p a n", a=2),
                                f_hi[:, bass.ds(2 * f, 2), :].bitcast(F32), ALU.subtract).then_inc(f_low, 1)
                dve.wait_ge(f_low, f + 1)

            with dve.Fori(0, 3) as r:
                for j in range(3):
                    ff_pair(j, r, 3 * r + j)
            for j in range(9, 11):
                ff_pair(j, 0, j)

            def fd_event():
                for h in range(2):
                    V.tensor_tensor(X[:, :, 512 * h:512 * h + 512], ps[:, 4 + 2 * h:6 + 2 * h, :],
                                    X[:, :, 512 * h:512 * h + 512], ALU.add).then_inc(f_add, 1)

            stage("fdn", 11, {10: fd_event})

            norm("x1", X, tat)
            stage("k1b", 2, {i: k_event("k1b", i, xa_k1, 4 + 2 * i) for i in range(2)})
            turn_lo("x1", a_hi, a_lo)

            def qk_event(i, name, dst):
                def f():
                    d = dst[:, :, 512 * i:512 * i + 512]
                    a = acc(name, i, 2)
                    dve.wait_ge(acc_free, BANKS[name] + 2 * i)
                    link(V.tensor_copy(d, a))
                    rotate(a, d, 8, 8, 32, rotated)
                return f

            stage("odq", 4, {1: qk_event(0, "odq", tat), 3: qk_event(1, "odq", tat)})
            stage("odk", 4, {1: qk_event(0, "odk", od_kr), 3: qk_event(1, "odk", od_kr)})
            stage("odv", 4, {1: v_event(0, "odv", od_v), 3: v_event(1, "odv", od_v)})
            for i in range(2):
                V.tensor_tensor_reduce(rot[:, i, 0:64], lamv[:, 2 * i, :], lamv[:, 2 * i + 1, :], 1.0, 0.0, ALU.mult,
                                       ALU.add, lams[:, i:i + 1]).then_inc(dve_link, 1)
                links[0] += 1
            dve.wait_ge(dve_link, links[0])
            V.memset(lams[:, 2:4], 0.0).then_inc(lam_s, 1)
            dve.wait_ge(lam_e, 1)
            link(V.tensor_tensor(lams[:, 0:1], lams[:, 3:4], lams[:, 2:3], ALU.subtract))
            link(V.tensor_scalar(lams[:, 0:1], lams[:, 0:1], -LAM0, None, ALU.add))
            V.memset(r_hi[:, KT * NE:].bitcast(F32), 0.0).then_inc(dve_link, 1)
            V.memset(r_lo[:, KT * NE:].bitcast(F32), 0.0).then_inc(dve_link, 1)
            links[0] += 2
            dve.wait_ge(dve_link, links[0])
            V.memset(lams[:, 1:2], 0.0).then_inc(r_z, 1)
            dve.wait_ge(r_w, 1)
            link(V.tensor_tensor(r_lo[:, 0:KT * NE], router[:, :], r_hi[:, 0:KT * NE].bitcast(F32), ALU.subtract))

            def d_max(h):
                o = 4 * (h % 2)
                dve.wait_ge(ds_ps, h + 1)
                link(V.tensor_reduce(mx[:, o:o + 4],
                                     ps[:, 4 + o // 2:6 + o // 2, :].rearrange("p g (t k) -> p (g t) k", t=2), AX.X,
                                     ALU.max))
                V.tensor_scalar(nmx[:, o:o + 4], mx[:, o:o + 4], -0.125, None, ALU.mult).then_inc(ds_mx, 1)

            def d_mix(h):
                o = 4 * (h % 2)
                dve.wait_ge(ds_exp, 4 * h + 4)
                link(V.reciprocal(rden[:, o:o + 4], den[:, o:o + 4]))
                link(V.tensor_scalar(rden[:, o + 2:o + 4], rden[:, o + 2:o + 4], lams[:, 0:1], None, ALU.mult))
                for t in range(2):
                    ins = V.tensor_scalar(od_p[:, h % 2, 0, t, :], od_p[:, h % 2, 0, t, :], rden[:, o + t:o + t + 1],
                                          None, ALU.mult)
                link(ins)
                for t in range(2):
                    ins = V.scalar_tensor_tensor(out=od_p[:, h % 2, 0, t, :], in0=od_p[:, h % 2, 1, t, :],
                                                 scalar=rden[:, o + 2 + t:o + 3 + t], in1=od_p[:, h % 2, 0, t, :],
                                                 op0=ALU.mult, op1=ALU.add)
                ins.then_inc(ds_c, 1)

            def d_out(h):
                dve.wait_ge(ds_o, h + 1)
                V.tensor_copy(od_s[:, :, h * P:(h + 1) * P],
                              ps[:, 2 + h % 2, 0:2 * P].rearrange("p (t v) -> p t v", t=2)).then_inc(ds_out, 1)

            d_max(0)
            d_max(1)
            d_mix(0)
            for h in range(DH):
                if h + 1 < DH:
                    d_mix(h + 1)
                if h + 2 < DH:
                    d_max(h + 2)
                d_out(h)
            dve.wait_ge(sq_heads, 2)
            link(V.tensor_reduce(sums[:, 0:16], ta[:, :].rearrange("p (g d) -> p g d", d=P), AX.X, ALU.add))
            means("dif", 16, P)
            V.tensor_tensor(ta[:, :].rearrange("p (g d) -> p g d", d=P), od_s.rearrange("p t (h d) -> p (t h) d", d=P),
                            rstd[:, 0:16].unsqueeze(2).broadcast_to([P, 16, P]), ALU.mult).then_inc(n_out, 2)
            stage("v1a", 2, {1: v_event(0, "v1a", xa_v1)})
            turn_lo("dif", a_hi, a_lo)
            stage("odo", 4, {1: x_event(0, "odo"), 3: x_event(1, "odo")})
            cross(1, xa_q1, xa_v1)

            norm("moe", X, tat)
            turn_lo("moe", a_hi, a_lo)
            V.memset(ones[:, :], 1.0)
            cut_lo(dve, G0 + 2)
            dve.wait_ge(r_lt, 1)
            V.tensor_copy(logits[:, :], ps[0:NE, 0, 0:256]).then_inc(r_ls, 1)
            dve.wait_ge(r_ps, 1)

            def small(i):
                return lg[:, i, :].rearrange("p (t e) -> p t e", t=2)

            def wide(v):
                return v.unsqueeze(2).broadcast_to([P, 2, NE])

            logit, eq, first, one1, left, one2, rank = (small(i) for i in range(7))
            m1, m2, r1 = lg[:, 7, 0:2], lg[:, 7, 2:4], lg[:, 7, 4:6]
            e8 = experts[:, 0:NE].unsqueeze(1).broadcast_to([P, 2, NE])
            link(V.tensor_copy(logit, ps[:, 2, 0:16].rearrange("p (t e) -> p t e", t=2)))
            link(V.tensor_scalar(rank, e8, -1.0, float(NE), ALU.mult, ALU.add))

            def pick(vals, m, one):
                link(V.tensor_reduce(m, vals, AX.X, ALU.max))
                link(V.tensor_tensor(eq, vals, wide(m), ALU.is_equal))
                link(V.tensor_tensor(first, eq, rank, ALU.mult))
                link(V.tensor_reduce(r1, first, AX.X, ALU.max))
                link(V.tensor_tensor(one, rank, wide(r1), ALU.is_equal))

            pick(logit, m1, one1)
            link(V.scalar_tensor_tensor(out=left, in0=one1, scalar=-3e38, in1=logit, op0=ALU.mult, op1=ALU.add))
            pick(left, m2, one2)
            V.tensor_tensor(lg[:, 9, 0:2], m2, m1, ALU.subtract).then_inc(r_m, 1)
            mask = small(8)
            V.tensor_tensor(mask, one1, one2, ALU.add).then_inc(r_cnt, 1)
            dve.wait_ge(r_e, 1)
            w1, w2 = lg[:, 9, 4:6], lg[:, 9, 6:8]
            link(V.tensor_scalar(w1, lg[:, 9, 2:4], 1.0, None, ALU.add))
            link(V.reciprocal(w1, w1))
            link(V.tensor_tensor(w2, w1, lg[:, 9, 2:4], ALU.mult))
            link(V.tensor_tensor(first, one1, wide(w1), ALU.mult))
            link(V.tensor_tensor(left, one2, wide(w2), ALU.mult))
            for b in range(2):
                link(V.tensor_tensor(gate16[:, :, NE * b:NE * b + NE], first, left, ALU.add))
            dve.wait_ge(r_ps, 2)
            cps = ps[:, 1, 0:16].rearrange("p (t e) -> p t e", t=2)
            link(V.tensor_tensor(first, cps, mask, ALU.mult))
            link(V.tensor_tensor(first, first, mask, ALU.add))
            link(V.tensor_scalar(pos16[:, :, 0:NE], first, -1.0, None, ALU.add))
            link(V.tensor_scalar(pos16[:, :, NE:2 * NE], first, -1.0 - BLK, None, ALU.add))
            V.memset(lg[:, 11, 1:2], 0.0).then_inc(act_rdy, 1)
            V.memset(lg[:, 11, 2:3], 0.0).then_inc(combined, 1)

            def pack_tokens(col):
                for t in range(2):
                    at = pos16[:, t, col:col + 1] if isinstance(col, int) else pos16[:, t, bass.ds(col, 1)]
                    ins = V.tensor_scalar(pack[:, t, :], slot, at, None, ALU.is_equal)
                ins.then_inc(packed, 1)

            pack_tokens(0)
            over, incl, rk, hit = (row16[:, i, 0:8] for i in range(4))
            link(V.tensor_scalar(over, ps[0:1, 1, 16:24], float(BLK), None, ALU.is_gt))
            link(V.tensor_tensor_scan(incl, ones[0:1, 0:8], over, 0.0, ALU.mult, ALU.add))
            link(V.tensor_tensor(rk, incl, over, ALU.subtract))
            link(V.tensor_scalar(row16[:, 0, 8:9], incl[:, 7:8], float(NE), None, ALU.add))
            link(V.tensor_copy(table[:, 0:1], row16[:, 0, 8:9]))
            link(V.tensor_copy(table[:, 1:1 + NE], experts[0:1, 0:NE]))
            for k in range(3):
                link(V.scalar_tensor_tensor(out=hit, in0=rk, scalar=float(k), in1=over, op0=ALU.is_equal,
                                            op1=ALU.mult))
                link(V.tensor_tensor(hit, hit, experts[0:1, NE:2 * NE], ALU.mult))
                link(V.tensor_reduce(row16[:, 1, 8 + k:9 + k], hit, AX.X, ALU.max))
            link(V.tensor_scalar(row16[:, 1, 8:11], row16[:, 1, 8:11], float(NE), None, ALU.max))
            V.tensor_copy(table[:, 1 + NE:4 + NE], row16[:, 1, 8:11]).then_inc(r_tab, 1)
            dve.wait_ge(r_tab, 1)
            n_pass = dve.value_load(table[0:1, 0:1], min_val=NE, max_val=NE + 3)

            def column(k):
                return dve.value_load(table[0:1, bass.ds(k + 1, 1)], min_val=0, max_val=2 * NE - 1)

            def pack_lo(k):
                for i in range(KT):
                    dve.wait_ge(e_h, KT * k + 4 * (i // 4) + 4)
                    ins = V.scalar_tensor_tensor(out=e_lo[:, i, :], in0=ps[:, 6 + i // 4, (i % 4) * P:(i % 4 + 1) * P],
                                                 scalar=cols[:, ROWS["moe"] + i:ROWS["moe"] + i + 1],
                                                 in1=e_hi[:, i, :].bitcast(F32), op0=ALU.mult, op1=ALU.subtract)
                ins.then_inc(e_l, 1)

            def e_mul(i, opening=0):
                dve.wait_ge(slab_used, G0 + 6 * i + 2 + opening)
                dve.wait_ge(g_sig, i + 2)
                V.tensor_tensor(e_act[:, :], ps[:, 1, :], e_sig[:, :], ALU.mult).then_inc(act_rdy, 1)

            def e_turn_lo(i):
                dve.wait_ge(at_h, i + 1)
                V.tensor_tensor(at_lo[:, :, :], shaped(ps[:, 4, :], 4), at_hi[:, :, :].bitcast(F32),
                                ALU.subtract).then_inc(at_l, 1)

            def add_pass(done):
                for t in range(2):
                    b0 = 6 if t == 0 else 2
                    dve.wait_ge(c_ps, 2 * done + t + 1)
                    V.tensor_tensor(X[:, t, :], ps[:, b0:b0 + 2, :].rearrange("p a n -> p (a n)"), X[:, t, :],
                                    ALU.add).then_inc(x_half if t == 0 else combined, 1)

            pack_lo(0)
            with dve.Fori(0, n_pass) as q:
                col = column(q)
                for t in range(2):
                    ins = V.tensor_scalar(pgate[:, t, :], slot, pos16[:, t, bass.ds(col, 1)],
                                          gate16[:, t, bass.ds(col, 1)], ALU.is_equal, ALU.mult)
                ins.then_inc(pg_rdy, 1)
                cut_lo(dve, G0 + 3, 7 * q)
                cut_lo(dve, G0 + 4, 7 * q)
                cut_lo(dve, G0 + 5, 7 * q)
                e_mul(7 * q, 2)
                with dve.If(q > 0):
                    add_pass(q)
                dve.wait_ge(pg_ps, q + 1)
                V.tensor_copy(spread[:, :], ps[:, 5, 0:256]).then_inc(pg_t, 1)
                with dve.If(q < n_pass - 1):
                    pack_tokens(column(q + 1))
                with dve.Fori(1, NB) as b:
                    i = 7 * q + b
                    r = i - 1
                    cut_lo(dve, G0 + 6, r)
                    cut_lo(dve, G0 + 7, r)
                    e_turn_lo(i - 1)
                    cut_lo(dve, G0 + 8, r)
                    cut_lo(dve, G0 + 9, r)
                    e_mul(i)
                    cut_lo(dve, G0 + 4, i)
                    cut_lo(dve, G0 + 5, i)
                e_turn_lo(7 * q + NB - 1)
                with dve.If(q < n_pass - 1):
                    cut_lo(dve, G0, 7 * q + 7)
                    pack_lo(q + 1)
                    cut_lo(dve, G0 + 1, 7 * q + 7)
                dve.wait_ge(slab_used, G0 + PASS + PASS * q)
                V.tensor_copy(y[:, :], ps[:, 2:4, :].rearrange("p a n -> p (a n)")).then_inc(y_sb, 1)
                with dve.If(q < n_pass - 1):
                    cut_lo(dve, G0 + 2, 7 * q + 7)
            add_pass(n_pass)
            dve.wait_ge(in_fin, 16)
            dve.wait_ge(n_sq, 2 * sum(n not in ("ret", "dif") for n in NORMS))
            means("fin", 2, D)
            for t in range(2):
                V.scalar_tensor_tensor(out=fin_o[:, t, :], in0=X[:, t, :], scalar=rstd[:, t:t + 1], in1=fin_g,
                                       op0=ALU.mult, op1=ALU.mult).then_inc(out_rdy, 1)

        @block.tensor
        def _(pe):
            T = nc.tensor

            def cuts(ah, al, wh, wl):
                return ((ah, wh), (ah, wl), (al, wh))

            def slab_ready(n, r=0):
                pe.wait_ge(lo_cut, n + 1 + RAW * r)

            def room(name, upto):
                if upto > 4:
                    pe.wait_ge(acc_free, upto - 4)

            def gemm_t(name, blocks, hi, lo, base=None):
                for b in range(blocks):
                    c = BANKS[name] + 2 * b
                    room(name, c + 2)
                    for h in range(2):
                        n = FIRST[name] + 2 * b + h
                        slab_ready(n)
                        wh, wl = (shaped(w[:, n % CUT, :], 4) for w in (w_hi, w_lo))
                        for k in range(4):
                            if base is not None and b == 0:
                                pe.wait_ge(t_lo, max(base + 4 * h + k + 1, 1))
                            for t in range(2):
                                ah, al = (a[:, 4 * h + k, t * P:(t + 1) * P] for a in (hi, lo))
                                for j, (s, m) in enumerate(cuts(ah, al, wh[:, k, :], wl[:, k, :])):
                                    mm = T.matmul(ps[:, (c + t) % 4, :], s, m, start=(h == 0 and k == 0 and j == 0),
                                                  stop=(h == 1 and k == 3 and j == 2))
                        mm.then_inc(slab_used, 1)

            def fm_slab(n, r, bank, hi, lo, base=None):
                slab_ready(n, r)
                wh, wl = (shaped(w[:, n % CUT, :], KT) for w in (w_hi, w_lo))
                for o in range(2):
                    for k in range(KT):
                        if base is not None and o == 0:
                            pe.wait_ge(t_lo, base + k + 1)
                        s_hi, s_lo = (w[:, k, o * P:(o + 1) * P] for w in (wh, wl))
                        for j, (s, m) in enumerate(cuts(s_hi, s_lo, hi[:, k, :], lo[:, k, :])):
                            mm = T.matmul(pair(bank)[:, o, :], s, m, start=(k == 0 and j == 0),
                                          stop=(k == KT - 1 and j == 2))
                mm.then_inc(slab_used, 1)

            def gemm_f(name, count, hi, lo, base=None):
                for i in range(count):
                    c = BANKS[name] + i
                    room(name, c + 1)
                    fm_slab(FIRST[name] + i, 0, c % 4, hi, lo, base if i == 0 else None)

            def turn(name, src, after):
                base, n = TURNS[name]
                pe.wait_ge(n_out, 2 * after)
                for b in range(n // 2):
                    for k in (2 * b, 2 * b + 1):
                        for t in range(2):
                            mm = T.transpose(pair(4 + b)[:, k % 2, t * P:(t + 1) * P], src[:, t, k * P:(k + 1) * P],
                                             ident)
                    mm.then_inc(t_ps, 1)

            def turned(name):
                base, n = TURNS[name]
                pe.wait_ge(t_lo, base + n)

            pe.wait_ge(in_const, 16)
            pe.wait_ge(setup_v, 1)
            T.transpose(ps[:, 7, 0:2], pos_f[:, :], ident[0:2, 0:2]).then_inc(setup_t, 1)
            pe.wait_ge(in_row, 160)
            T.transpose(ps[:, 6, 0:N_ROWS], rows[:, :], ident[0:N_ROWS, 0:N_ROWS]).then_inc(setup_t, 1)
            pe.wait_ge(setup_v, 3)
            turn("x0", tat, 1)
            gemm_t("evq", 1, a_hi, a_lo, TURNS["x0"][0])
            turn("mem", tbt, 2)
            gemm_t("evk", 1, a_hi, a_lo)
            gemm_t("evv", 1, a_hi, a_lo)
            gemm_t("evg", 1, a_hi, a_lo)
            gemm_f("evc", 6, a_hi, a_lo)
            turned("mem")
            pe.wait_ge(acc_free, BANKS["evv"])
            for b in range(4):
                src = ev_qr if b < 2 else ev_kr
                for k in (2 * (b % 2), 2 * (b % 2) + 1):
                    for t in range(2):
                        mm = T.transpose(pair(4 + b)[:, k % 2, t * P:(t + 1) * P], src[:, t, k * P:(k + 1) * P], ident)
                mm.then_inc(qk_ps, 1)
            gemm_f("k0", 4, m_hi, m_lo)
            pe.wait_ge(qk_t, 4)

            def ret_scores(h):
                if h >= 2:
                    pe.wait_ge(rs_dec, h - 1)
                a, hp = 64 * (h % 2), h // 2
                for j in range(2):
                    mm = T.matmul(pair(4 + h % 2)[:, j, :], ev_kt[a:a + 64, hp, j * P:(j + 1) * P],
                                  ev_qt[a:a + 64, hp, :], start=True, stop=True)
                mm.then_inc(rs_ps, 1)

            ret_scores(0)
            ret_scores(1)
            for h in range(RH):
                pe.wait_ge(rs_dec, h + 1)
                for t in range(2):
                    for j in range(2):
                        mm = T.matmul(ps[:, 6 + t, 64 * h:64 * h + 64], ret_s[:, h % 4, j, t * P:(t + 1) * P],
                                      ev_v[:, j, 64 * h:64 * h + 64], start=(j == 0), stop=(j == 1))
                if h + 2 < RH:
                    ret_scores(h + 2)
            mm.then_inc(rs_o, 1)
            gemm_t("v0a", 1, m_hi, m_lo)
            turn("ret", ta[:, 1024:2048].rearrange("p (t n) -> p t n", t=2), 3)
            pe.wait_ge(conv_lo, 1)
            gemm_t("evo", 2, a_hi, a_lo, TURNS["ret"][0] - 4)

            def cross(i, xq, xk, xv, xa_pt):
                name = f"xa{i}"
                gemm_t(f"v{i}b", 1, m_hi, m_lo)
                turn(name, tat, NORMS[name] + 1)
                gemm_f(f"q{i}", 4, a_hi, a_lo, TURNS[name][0])
                for h in range(XH):
                    pe.wait_ge(acc_free, BANKS[f"q{i}"] + h + 1)
                    for t in range(2):
                        for k in range(2):
                            mm = T.matmul(pair(4 + h)[:, t, :], xq[:, 2 * h + k, t * P:(t + 1) * P],
                                          xk[:, 2 * h + k, :], start=(k == 0), stop=(k == 1))
                    mm.then_inc(xs_ps, 1)
                for h in range(XH):
                    pe.wait_ge(xs_n, XH * i + h + 1)
                    for m in range(2):
                        for t in range(2):
                            mm = T.transpose(pair(4 + h)[:, m, t * P:(t + 1) * P], xa_p[:, h, t, m * P:(m + 1) * P],
                                             ident)
                    mm.then_inc(xs_tp, 1)
                for h in range(XH):
                    pe.wait_ge(xs_t, XH * i + h + 1)
                    for d in range(2):
                        for m in range(2):
                            mm = T.matmul(pair(4 + h)[:, d, :], xv[:, m, 256 * h + d * P:256 * h + (d + 1) * P],
                                          xa_pt[:, h, m, :], start=(m == 0), stop=(m == 1))
                    mm.then_inc(xs_o, 1)
                pe.wait_ge(xs_lo, XH * (i + 1))
                gemm_t(f"o{i}", 2, a_hi, a_lo)

            cross(0, xa_q0, xa_k0, xa_v0, xa_pt0)

            gemm_f("k1a", 2, m_hi, m_lo)
            turn("ffn", tat, NORMS["ffn"] + 1)
            pe.wait_ge(acc_free, BANKS["k1b"])
            g = FIRST["fgu"]

            def ff_pair(j, r, f, first=False):
                if not first:
                    pe.wait_ge(f_low, f - 2)
                base = TURNS["ffn"][0] if first and j == 0 else None
                fm_slab(g + 2 * j, r, 2 * (j % 3), a_hi, a_lo, base)
                fm_slab(g + 2 * j + 1, r, 2 * (j % 3) + 1, a_hi, a_lo)

            for j in range(3):
                ff_pair(j, 0, j, first=True)
            with pe.Fori(1, 3) as r:
                for j in range(3):
                    ff_pair(j, r, 3 * r + j)
            for j in range(9, 11):
                ff_pair(j, 0, j)
            for i in range(11):
                pe.wait_ge(f_low, i + 1)
                n = FIRST["fdn"] + i
                slab_ready(n)
                wh, wl = (shaped(w[:, n % CUT, :], 2) for w in (w_hi, w_lo))
                for k in range(2):
                    for t in range(2):
                        ah, al = (a[:, 2 * i + k, t * P:(t + 1) * P] for a in (f_hi, f_lo))
                        for h in range(2):
                            s = slice(512 * h, 512 * h + 512)
                            for j, (st, mv) in enumerate(cuts(ah, al, wh[:, k, s], wl[:, k, s])):
                                mm = T.matmul(ps[:, 4 + 2 * h + t, :], st, mv, start=(i == 0 and k == 0 and j == 0),
                                              stop=(i == 10 and k == 1 and j == 2))
                mm.then_inc(slab_used, 1)

            pe.wait_ge(f_mul, 11)
            gemm_f("k1b", 2, m_hi, m_lo)
            turn("x1", tat, NORMS["x1"] + 1)
            gemm_t("odq", 2, a_hi, a_lo, TURNS["x1"][0])
            gemm_t("odk", 2, a_hi, a_lo)
            for b in range(8):
                if b % 4 == 0:
                    pe.wait_ge(acc_free, BANKS["odk" if b == 0 else "odv"])
                if b >= 4:
                    pe.wait_ge(oq_t, b - 3)
                src = tat if b < 4 else od_kr
                for k in (2 * (b % 4), 2 * (b % 4) + 1):
                    for t in range(2):
                        mm = T.transpose(pair(4 + b % 4)[:, k % 2, t * P:(t + 1) * P], src[:, t, k * P:(k + 1) * P],
                                         ident)
                mm.then_inc(oq_ps, 1)
            gemm_t("odv", 2, a_hi, a_lo)
            pe.wait_ge(oq_t, 8)
            pe.wait_ge(acc_free, BANKS["v1a"])

            def d_scores(h):
                if h >= 2:
                    pe.wait_ge(ds_exp, 4 * (h - 1))
                for g_ in range(2):
                    a = 64 * g_
                    for t in range(2):
                        mm = T.matmul(pair(4 + 2 * (h % 2) + g_)[:, t, :], od_qt[a:a + 64, h, t * P:(t + 1) * P],
                                      od_kt[a:a + 64, h, :], start=True, stop=True)
                mm.then_inc(ds_ps, 1)

            d_scores(0)
            d_scores(1)
            for h in range(DH):
                pe.wait_ge(ds_c, h + 1)
                for k in range(2):
                    for t in range(2):
                        mm = T.transpose(pair(h % 2)[:, k, t * P:(t + 1) * P], od_p[:, h % 2, 0, t, k * P:(k + 1) * P],
                                         ident)
                mm.then_inc(ds_tp, 1)
                if h + 2 < DH:
                    d_scores(h + 2)
                pe.wait_ge(ds_t, h + 1)
                if h >= 2:
                    pe.wait_ge(ds_out, h - 1)
                for t in range(2):
                    for k in range(2):
                        mm = T.matmul(ps[:, 2 + h % 2, t * P:(t + 1) * P], od_pt[:, h % 4, k, t * P:(t + 1) * P],
                                      od_v[:, k, h * P:(h + 1) * P], start=(k == 0), stop=(k == 1))
                mm.then_inc(ds_o, 1)
            pe.wait_ge(ds_out, DH)
            gemm_t("v1a", 1, m_hi, m_lo)
            turn("dif", tat, NORMS["dif"] + 1)
            gemm_t("odo", 2, a_hi, a_lo, TURNS["dif"][0])
            cross(1, xa_q1, xa_k1, xa_v1, xa_pt1)

            turn("moe", tat, NORMS["moe"] + 1)
            pe.wait_ge(acc_free, BANKS["o1"] + 4)
            for k in range(KT):
                pe.wait_ge(t_lo, TURNS["moe"][0] + k + 1)
                rh, rl = (a[:, NE * k:NE * k + P] for a in (r_hi, r_lo))
                for j, (s, m) in enumerate(cuts(rh, rl, a_hi[:, k, :], a_lo[:, k, :])):
                    mm = T.matmul(ps[:, 0, 0:256], s, m, start=(k == 0 and j == 0), stop=(k == KT - 1 and j == 2))
            mm.then_inc(r_lt, 1)
            pe.wait_ge(r_ls, 1)
            for t in range(2):
                mm = T.transpose(ps[:, 2, NE * t:NE * t + NE], logits[:, t * P:(t + 1) * P], ident[0:NE, 0:NE])
            mm.then_inc(r_ps, 1)
            pe.wait_ge(r_cnt, 1)
            mask = lg[:, 8, :]
            T.matmul(ps[:, 1, 0:8], before, mask[:, 0:8], start=True, stop=True)
            T.matmul(ps[:, 1, 8:16], before, mask[:, 8:16], start=True, stop=False)
            T.matmul(ps[:, 1, 8:16], ones[:, :], mask[:, 0:8], start=False, stop=True).then_inc(c_ps, 2)
            T.matmul(ps[:, 1, 16:24], ones[:, :], mask[:, 0:8], start=True, stop=False)
            T.matmul(ps[:, 1, 16:24], ones[:, :], mask[:, 8:16], start=False, stop=True).then_inc(r_ps, 1)

            def gather(k):
                pe.wait_ge(packed, k + 1)
                for i in range(KT):
                    for t in range(2):
                        mm = T.matmul(ps[:, 6 + i // 4, (i % 4) * P:(i % 4 + 1) * P], tat[:, t, i * P:(i + 1) * P],
                                      pack[:, t, :], start=(t == 0), stop=(t == 1))
                    if i % 4 == 3:
                        mm.then_inc(e_ps, 1)

            def half_in(n, r, bank, h):
                slab_ready(n, r)
                wh, wl = (shaped(w[:, n % CUT, :], 4) for w in (w_hi, w_lo))
                for k in range(4):
                    ah, al = e_hi[:, 4 * h + k, :], e_lo[:, 4 * h + k, :]
                    for j, (s, m) in enumerate(cuts(ah, al, wh[:, k, :], wl[:, k, :])):
                        mm = T.matmul(ps[:, bank, :], s, m, start=(h == 0 and k == 0 and j == 0),
                                      stop=(h == 1 and k == 3 and j == 2))
                mm.then_inc(slab_used, 1)

            def turn_act(i):
                pe.wait_ge(act_rdy, i + 2)
                for k in range(4):
                    mm = T.transpose(ps[:, 4, k * P:(k + 1) * P], e_act[:, k * P:(k + 1) * P], ident)
                mm.then_inc(at_ps, 1)

            def down(n, r, i, first, last):
                pe.wait_ge(at_l, i + 1)
                for h in range(2):
                    slab_ready(n + h, r)
                    wh, wl = (shaped(w[:, (n + h) % CUT, :], 2) for w in (w_hi, w_lo))
                    for k in range(2):
                        ah, al = at_hi[:, 2 * h + k, :], at_lo[:, 2 * h + k, :]
                        for o in range(2):
                            c = slice(512 * o, 512 * o + 512)
                            for j, (s, m) in enumerate(cuts(ah, al, wh[:, k, c], wl[:, k, c])):
                                mm = T.matmul(ps[:, 2 + o, :], s, m,
                                              start=(first and h == 0 and k == 0 and j == 0),
                                              stop=(last and h == 1 and k == 1 and j == 2), skip_group_check=True)
                    mm.then_inc(slab_used, 1)

            def combine(k):
                pe.wait_ge(y_sb, k + 1)
                pe.wait_ge(pg_t, k + 1)
                for t in range(2):
                    b0 = 6 if t == 0 else 2
                    for o in range(2):
                        mm = T.matmul(ps[:, b0 + o, :], spread[:, t * P:(t + 1) * P], y[:, 512 * o:512 * o + 512],
                                      start=True, stop=True)
                    mm.then_inc(c_ps, 1)

            gather(0)
            pe.wait_ge(r_tab, 1)
            n_pass = pe.value_load(table[0:1, 0:1], min_val=NE, max_val=NE + 3)
            with pe.Fori(0, n_pass) as q:
                pe.wait_ge(e_l, q + 1)
                i = 7 * q
                pe.wait_ge(g_sig, i + 1)
                half_in(G0, i, 0, 0)
                half_in(G0 + 1, i, 0, 1)
                pe.wait_ge(act_rdy, i + 1)
                half_in(G0 + 2, i, 1, 0)
                half_in(G0 + 3, i, 1, 1)
                with pe.If(q > 0):
                    combine(q - 1)
                pe.wait_ge(pg_rdy, q + 1)
                for t in range(2):
                    mm = T.transpose(ps[:, 5, t * P:(t + 1) * P], pgate[:, t, :], ident)
                mm.then_inc(pg_ps, 1)
                for lo_, hi_ in ((1, 2), (2, NB)):
                    with pe.Fori(lo_, hi_) as b:
                        i = 7 * q + b
                        pe.wait_ge(g_sig, i + 1)
                        half_in(G0 + 4, i - 1, 0, 0)
                        half_in(G0 + 5, i - 1, 0, 1)
                        turn_act(i - 1)
                        pe.wait_ge(act_rdy, i + 1)
                        half_in(G0 + 6, i - 1, 1, 0)
                        half_in(G0 + 7, i - 1, 1, 1)
                        if lo_ == 1:
                            pe.wait_ge(combined, q + 1)
                        down(G0 + 8, i - 1, i - 1, lo_ == 1, False)
                turn_act(7 * q + NB - 1)
                with pe.If(q < n_pass - 1):
                    gather(q + 1)
                down(G0 + 4, 7 * q + 6, 7 * q + NB - 1, False, True)
            combine(n_pass - 1)


INPUTS = ["x", "mem", "positions", "mem_norm_g", "final_norm_g", "mix_norm_g", "xa_norm_g", "ffn_norm_g", "xa_wq",
          "xa_wkv", "xa_wo", "ev_w_in", "ev_conv_w", "ev_ret_decay_f", "ev_ret_decay_b", "ev_ret_gn_g", "ev_w_out",
          "ffd_w_gate", "ffd_w_up", "ffd_w_down", "od_w_in", "od_lam_q1", "od_lam_k1", "od_lam_q2", "od_lam_k2",
          "od_gn_g", "od_w_out", "moe_router", "moe_w_gate", "moe_w_up", "moe_w_down"]


def kernel(**inputs):
    import concourse.bacc as bacc
    from concourse.bass_utils import run_bass_kernel_spmd

    nc = bacc.Bacc("TRN2", target_bir_lowering=False, num_devices=1)
    arrays, args = {}, {}
    for name in INPUTS + ["consts"]:
        a = constants() if name == "consts" else np.ascontiguousarray(inputs[name])
        arrays[f"in_{name}"] = a
        args[name] = nc.dram_tensor(f"in_{name}", a.shape, mybir.dt.from_np(a.dtype), kind="ExternalInput").ap()
    shape = tuple(inputs["x"].shape)
    args["out"] = nc.dram_tensor("out_0", shape, F32, kind="ExternalOutput").ap()
    trunk_kernel(nc, **args)
    r = run_bass_kernel_spmd(nc, [arrays], core_ids=[0])
    return r.results[0]["out_0"]
```

```python
import math
from contextlib import ExitStack, nullcontext

import numpy as np

import concourse.bass as bass
from concourse import mybir

F32 = mybir.dt.float32
F32R = mybir.dt.float32r
I32 = mybir.dt.int32
ACT = mybir.ActivationFunctionType
ALU = mybir.AluOpType
AX = mybir.AxisListType

P = 128
RAW = 6
CUT = 3
AHEAD = CUT - 1
EPS = 1e-6

RET_THETA, ROPE_THETA = 10000.0, 500000.0


def shapes(x, mem, moe_gate, ffd_gate, ev_in):
    s = {}
    s["L"], s["D"] = x.shape[1], x.shape[2]
    s["M"] = mem.shape[1]
    s["E"], s["FE"] = moe_gate.shape[1], moe_gate.shape[3]
    s["FF"] = ffd_gate.shape[2]
    return s


STREAM = [("evq", 2), ("evk", 2), ("evv", 2), ("evg", 2), ("evc", 6), ("k0", 4), ("v0a", 2), ("evo", 4),
          ("v0b", 2), ("q0", 4), ("o0", 4), ("k1a", 2), ("fgu", 22), ("fdn", 11), ("k1b", 2), ("odq", 4), ("odk", 4),
          ("odv", 4), ("v1a", 2), ("odo", 4), ("v1b", 2), ("q1", 4), ("o1", 4)]
FIRST = {}
_n = 0
for _name, _k in STREAM:
    FIRST[_name] = _n
    _n += _k
FIRST["moe"] = _n
BANKS = {}
_n = 0
for _name, _k in STREAM:
    if _name not in ("fgu", "fdn"):
        BANKS[_name] = _n
        _n += _k
TURNS = {}
_n = 0
for _name, _k in [("x0", 8), ("mem", 8), ("ret", 4), ("xa0", 8), ("ffn", 8), ("x1", 8), ("dif", 8), ("xa1", 8),
                  ("moe", 8)]:
    TURNS[_name] = (_n, _k)
    _n += _k
NORMS = {n: i for i, n in enumerate(["x0", "mem", "ret", "xa0", "ffn", "x1", "dif", "xa1", "moe", "fin"])}

ROWS = {}
_n = 0
for _name, _k in [("mem", 8), ("x0", 8), ("x1", 8), ("xa0", 8), ("xa1", 8), ("ffn", 8), ("moe", 8), ("ret", 4),
                  ("dif", 8), ("conv", 12)]:
    ROWS[_name] = _n
    _n += _k
N_ROWS = _n

CONST = {}
_n = 0
for _name, _k in [("ident", P), ("before", P), ("slot", P), ("freq", 40), ("experts", 16), ("after_i", 512),
                  ("before_i", 512)]:
    CONST[_name] = (_n, _n + _k)
    _n += _k
N_CONST = _n


def constants():
    c = np.zeros((P, N_CONST), np.float32)
    p = np.arange(P)

    def put(name, a):
        c[:, CONST[name][0]:CONST[name][1]] = a
    put("ident", np.eye(P))
    put("before", (p[:, None] < p[None, :]))
    put("slot", np.broadcast_to(p[None, :], (P, P)))
    j = (np.arange(2)[None, :, None] * P + p[:, None, None])
    d = np.arange(2 * P)[None, None, :] - j
    put("after_i", np.maximum(d, 0).reshape(P, -1))
    put("before_i", np.maximum(-d, 0).reshape(P, -1))
    f = []
    for theta, rot in ((RET_THETA, 64), (ROPE_THETA, 16)):
        half = rot // 2
        f.append(np.exp(np.float32(-math.log(theta)) * np.arange(half, dtype=np.float32) * np.float32(2.0 / rot)))
    put("freq", np.concatenate(f)[None, :].astype(np.float32))
    put("experts", np.arange(16)[None, :])
    return c


def trunk_kernel(nc, x, mem, positions, mem_norm_g, final_norm_g, mix_norm_g, xa_norm_g, ffn_norm_g, xa_wq, xa_wkv,
                 xa_wo, ev_w_in, ev_conv_w, ev_ret_decay_f, ev_ret_decay_b, ev_ret_gn_g, ev_w_out, ffd_w_gate,
                 ffd_w_up, ffd_w_down, od_w_in, od_lam_q1, od_lam_k1, od_lam_q2, od_lam_k2, od_gn_g, od_w_out,
                 moe_router, moe_w_gate, moe_w_up, moe_w_down, consts, out):
    D = x.shape[2]
    KT = D // P
    NE = moe_router.shape[2]
    NB = moe_w_gate.shape[3] // 512
    FT = ffd_w_gate.shape[2] // P
    RH = ev_ret_decay_f.shape[1]
    DH = od_gn_g.shape[1] // P
    XH = 4
    PASS = 6 * NB
    LAM0 = 0.8 - 0.6 * math.exp(-0.3)
    BLK = P

    ctx = ExitStack()
    with ctx:
        def sb(name, shape, dt=F32, stack=ctx):
            return stack.enter_context(nc.sbuf_tensor(name, shape, dt))

        def sem(name):
            return ctx.enter_context(nc.semaphore(name))

        raw = sb("raw", [P, RAW, 2048])
        w_hi = sb("w_hi", [P, CUT, 2048], F32R)
        w_lo = sb("w_lo", [P, CUT, 2048], F32R)
        X = sb("X", [P, 2, D])
        with ExitStack() as s:
            od_o = sb("od_o", [P, 2, D], F32, s)
        a_hi = sb("a_hi", [P, KT, 256], F32R)
        a_lo = sb("a_lo", [P, KT, 256], F32R)
        ta = sb("ta", [P, 2048])
        tb = sb("tb", [P, 2048])
        rot = sb("rot", [P, 2, 512])
        const = sb("const", [P, 3 * P + 56])
        ident, before, slot = const[:, 0:P], const[:, P:2 * P], const[:, 2 * P:3 * P]
        freq, experts = const[:, 3 * P:3 * P + 40], const[:, 3 * P + 40:3 * P + 56]
        rows = sb("rows", [N_ROWS, P])
        cols = sb("cols", [P, N_ROWS])
        pos_i = sb("pos_i", [2, P], I32)
        pos_f = sb("pos_f", [2, P])
        pos = sb("pos", [P, 2])
        ang = sb("ang", [P, 2, 40])
        turnsb = sb("turnsb", [P, 2, 40])
        cos = sb("cos", [P, 2, 40])
        sin = sb("sin", [P, 2, 40])
        decay = sb("decay", [P, 2, RH])
        lamv = sb("lamv", [P, 4, 64])
        lams = sb("lams", [P, 4])
        half = sb("half", [P, 16])
        sums = sb("sums", [P, 16])
        var = sb("var", [P, 16])
        rstd = sb("rstd", [P, 16])
        mx = sb("mx", [P, 16])
        nmx = sb("nmx", [P, 16])
        den = sb("den", [P, 16])
        rden = sb("rden", [P, 16])
        row16 = sb("row16", [1, 4, 16])
        logits = sb("logits", [NE, 256])
        table = sb("table", [1, 24], I32)

        with ExitStack() as s:
            u = sb("u", [P, 11264], F32, s)
        with ExitStack() as s:
            f_hi = sb("f_hi", [P, FT, 256], F32R, s)
            f_lo = sb("f_lo", [P, FT, 256], F32R, s)
        with ExitStack() as s:
            e_hi = sb("e_hi", [P, KT, BLK], F32R, s)
            e_lo = sb("e_lo", [P, KT, BLK], F32R, s)
            at_hi = sb("at_hi", [P, 4, BLK], F32R, s)
            at_lo = sb("at_lo", [P, 4, BLK], F32R, s)
            e_sig = sb("e_sig", [P, 512], F32, s)
            e_act = sb("e_act", [P, 512], F32, s)
            pack = sb("pack", [P, 2, BLK], F32, s)
            pgate = sb("pgate", [P, 2, BLK], F32, s)
            spread = sb("spread", [P, 2 * P], F32, s)
            y = sb("y", [P, D], F32, s)
            ones = sb("ones", [P, P], F32, s)
            lg = sb("lg", [P, 12, 16], F32, s)
            pos16 = sb("pos16", [P, 2, 16], F32, s)
            gate16 = sb("gate16", [P, 2, 16], F32, s)
            held_u = sb("held_u", [P, 2, 2048], F32, s)
            router = sb("router", [P, KT * NE], F32, s)
            r_hi = sb("r_hi", [P, KT * NE + P - NE], F32R, s)
            r_lo = sb("r_lo", [P, KT * NE + P - NE], F32R, s)
        ctx.enter_context(nc.sbuf_tensor("region", [P, 11264], F32))
        with ExitStack() as s:
            held_m = sb("held_m", [P, 2, 2048], F32, s)
        m_hi = sb("m_hi", [P, KT, 256], F32R)
        m_lo = sb("m_lo", [P, KT, 256], F32R)

        dmat = u[:, 0:4096].rearrange("p (h n) -> p h n", h=RH)
        xa_v0 = u[:, 0:2048].rearrange("p (t n) -> p t n", t=2)
        ev_v = u[:, 4096:5120].rearrange("p (t n) -> p t n", t=2)
        ev_g = u[:, 5120:6144].rearrange("p (t n) -> p t n", t=2)
        xa_q0 = u[:, 4096:6144].rearrange("p (k n) -> p k n", k=KT)
        ev_qt = u[:, 6144:7168].rearrange("p (k n) -> p k n", k=4)
        ev_kt = u[:, 7168:8192].rearrange("p (k n) -> p k n", k=4)
        xa_k0 = u[:, 8192:10240].rearrange("p (k n) -> p k n", k=KT)
        after_i, before_i = u[:, 10240:10752], u[:, 10752:11264]
        od_qt = u[:, 0:2048].rearrange("p (k n) -> p k n", k=KT)
        xa_q1 = od_qt
        od_kt = u[:, 2048:4096].rearrange("p (k n) -> p k n", k=KT)
        od_v = u[:, 4096:6144].rearrange("p (t n) -> p t n", t=2)
        od_kr = u[:, 6144:8192].rearrange("p (t n) -> p t n", t=2)
        xa_k1 = tb[:, :].rearrange("p (k n) -> p k n", k=KT)
        xa_v1 = u[:, 8192:10240].rearrange("p (t n) -> p t n", t=2)
        od_s = od_o[:, :, :]
        tat = ta[:, :].rearrange("p (t n) -> p t n", t=2)
        tbt = tb[:, :].rearrange("p (t n) -> p t n", t=2)
        ev_qr = ta[:, 0:1024].rearrange("p (t n) -> p t n", t=2)
        ev_kr = ta[:, 1024:2048].rearrange("p (t n) -> p t n", t=2)
        ev_c = tb[:, 0:1024].rearrange("p (k n) -> p k n", k=4)
        ev_u = tb[:, 1024:2048].rearrange("p (k n) -> p k n", k=4)
        ret_s = ta[:, :].rearrange("p (s j i) -> p s j i", s=4, j=2)
        xa_p = ta[:, :].rearrange("p (h t m) -> p h t m", h=XH, t=2)
        xa_pt0 = tb[:, :].rearrange("p (h m l) -> p h m l", h=XH, m=2)
        xa_pt1 = u[:, 6144:8192].rearrange("p (h m l) -> p h m l", h=XH, m=2)
        od_p = ta[:, :].rearrange("p (s g t k) -> p s g t k", s=2, g=2, t=2)
        od_pt = u[:, 6144:8192].rearrange("p (s k q) -> p s k q", s=4, k=2)
        f_sig, f_act = ta[:, 0:512], ta[:, 512:1024]
        fin_g = tb[:, 0:D]
        fin_o = u[:, 0:2048].rearrange("p (t n) -> p t n", t=2)

        ps = ctx.enter_context(nc.psum_tensor("ps", [P, 8, 512], F32))

        def pair(b):
            return ps[:, b, :].rearrange("p (a n) -> p a n", a=2)

        in_x, in_mem, in_row, in_const, in_pos, in_misc, in_fin, in_router = (sem(n) for n in (
            "in_x", "in_mem", "in_row", "in_const", "in_pos", "in_misc", "in_fin",
            "in_router"))
        raw_in = [sem(f"raw_in{i}") for i in range(RAW)]
        in_held = [sem(f"in_held{i}") for i in range(4)]
        hi_cut, lo_cut, slab_used, acc_free = sem("hi_cut"), sem("lo_cut"), sem("slab_used"), sem("acc_free")
        act_link, dve_link, pool_link = sem("act_link"), sem("dve_link"), sem("pool_link")
        setup_t, setup_v, setup_s = sem("setup_t"), sem("setup_v"), sem("setup_s")
        n_sq, n_var, n_rstd, n_out = sem("n_sq"), sem("n_var"), sem("n_rstd"), sem("n_out")
        t_ps, t_hi, t_lo = sem("t_ps"), sem("t_hi"), sem("t_lo")
        g_silu, d_exp, d_got = sem("g_silu"), sem("d_exp"), sem("d_got")
        qk_ps, qk_t = sem("qk_ps"), sem("qk_t")
        conv_hi, conv_lo = sem("conv_hi"), sem("conv_lo")
        rs_ps, rs_dec, rs_o, sq_heads = sem("rs_ps"), sem("rs_dec"), sem("rs_o"), sem("sq_heads")
        xs_ps, xs_mx, xs_exp, xs_n, xs_tp, xs_t, xs_o, xs_hi, xs_lo = (sem(n) for n in (
            "xs_ps", "xs_mx", "xs_exp", "xs_n", "xs_tp", "xs_t", "xs_o", "xs_hi", "xs_lo"))
        f_silu, f_mul, f_rnd, f_low, f_add = (sem(n) for n in ("f_silu", "f_mul", "f_rnd", "f_low", "f_add"))
        oq_ps, oq_t = sem("oq_ps"), sem("oq_t")
        ds_ps, ds_mx, ds_exp, ds_c, ds_tp, ds_t, ds_o, ds_out, lam_e, lam_s = (sem(n) for n in (
            "ds_ps", "ds_mx", "ds_exp", "ds_c", "ds_tp", "ds_t", "ds_o", "ds_out", "lam_e", "lam_s"))
        r_ps, r_m, r_cnt, r_tab, r_e, r_w = (sem(n) for n in ("r_ps", "r_m", "r_cnt", "r_tab", "r_e", "r_w"))
        r_z, r_lt, r_ls = sem("r_z"), sem("r_lt"), sem("r_ls")
        packed, e_ps, e_h, e_l = sem("packed"), sem("e_ps"), sem("e_h"), sem("e_l")
        g_sig, act_rdy = sem("g_sig"), sem("act_rdy")
        at_ps, at_h, at_l = sem("at_ps"), sem("at_h"), sem("at_l")
        pg_rdy, pg_ps, pg_t = sem("pg_rdy"), sem("pg_ps"), sem("pg_t")
        y_sb, c_ps, x_half, combined, out_rdy, out_done = (sem(n) for n in (
            "y_sb", "c_ps", "x_half", "combined", "out_rdy", "out_done"))

        def kpn(w):
            return w.rearrange("(k p) n -> p k n", p=P)

        wi, od = kpn(ev_w_in[0]), kpn(od_w_in[0])

        def t_slab(w, c0):
            return [w[:, 4 * h:4 * h + 4, c0:c0 + 512] for h in range(2)]

        def f_slab(w, c0):
            return w[:, 0:KT, c0:c0 + 256]

        def t_all(w, c0=0, n=2):
            return [s for b in range(n) for s in t_slab(w, c0 + 512 * b)]

        def f_all(w, c0=0, n=4):
            return [f_slab(w, c0 + 256 * b) for b in range(n)]

        C = ev_conv_w.shape[2]
        slabs = {
            "evq": t_slab(wi, 3 * C), "evk": t_slab(wi, 3 * C + 512), "evv": t_slab(wi, 3 * C + 1024),
            "evg": t_slab(wi, 3 * C + 1536),
            "evc": f_all(wi, C, 2) + f_all(wi, 2 * C, 2) + f_all(wi, 0, 2),
            "evo": t_all(kpn(ev_w_out[0])), "odo": t_all(kpn(od_w_out[0])),
            "odq": t_all(od, 0), "odk": t_all(od, D), "odv": t_all(od, 2 * D),
        }
        slabs["k1a"], slabs["k1b"] = (f_all(kpn(xa_wkv[1]), 512 * b, 2) for b in range(2))
        slabs["k0"] = f_all(kpn(xa_wkv[0]))
        for i in range(2):
            slabs[f"q{i}"] = f_all(kpn(xa_wq[i]))
            slabs[f"v{i}a"], slabs[f"v{i}b"] = (t_slab(kpn(xa_wkv[i]), D + 512 * b) for b in range(2))
            slabs[f"o{i}"] = t_all(kpn(xa_wo[i]))
        ffg, ffu, ffd = kpn(ffd_w_gate[0]), kpn(ffd_w_up[0]), kpn(ffd_w_down[0])
        eg = moe_w_gate[0].rearrange("e (k p) n -> e p k n", p=P)
        eu = moe_w_up[0].rearrange("e (k p) n -> e p k n", p=P)
        ed = moe_w_down[0].rearrange("e (k p) n -> e p k n", p=P)

        def shaped(t, k):
            return t.rearrange("p (k n) -> p k n", k=k)

        G0 = FIRST["moe"]
        LOGITS = BANKS["o1"] % 4
        HP, HB = NE // 2, 3
        HELD = G0 + PASS * HP + 6 * HB + 2
        held = [held_m[:, 0, :], held_m[:, 1, :], held_u[:, 0, :], held_u[:, 1, :]]

        def place(n, r, behind):
            if isinstance(r, int):
                n, r = n + RAW * r, 0
                if HELD <= n < HELD + 4:
                    return held[n - HELD], in_held[n - HELD], 16
                behind = n >= HELD + 4
            t = n - 4 if behind else n
            return raw[:, t % RAW, :], raw_in[t % RAW], 16 * (t // RAW + 1) + 16 * r

        def load(sp, n, src, r=0, behind=False):
            at_, arrived, _ = place(n, r, behind)
            a = n + RAW * r
            if not isinstance(r, int):
                sp.wait_ge(lo_cut, a - RAW + 1)
            elif RAW <= a < HELD or a >= HELD + 4:
                sp.wait_ge(lo_cut, a - RAW + 1 - (4 if HELD + 4 <= a < HELD + 4 + RAW else 0))
            sp.dma_start(shaped(at_, src.shape[1]), src).then_inc(arrived, 16)

        def cut_hi(act, n, r=0, behind=False):
            at_, arrived, count = place(n, r, behind)
            act.wait_ge(arrived, count)
            if n >= CUT:
                act.wait_ge(slab_used, n - CUT + 1 + RAW * r)
            nc.scalar.activation(w_hi[:, n % CUT, :], at_, ACT.Copy).then_inc(hi_cut, 1)

        def cut_lo(dve, n, r=0, behind=False):
            dve.wait_ge(hi_cut, n + 1 + RAW * r)
            nc.vector.tensor_tensor(w_lo[:, n % CUT, :], place(n, r, behind)[0], w_hi[:, n % CUT, :].bitcast(F32),
                                    ALU.subtract).then_inc(lo_cut, 1)

        block = ctx.enter_context(nc.Block())

        @block.sync
        def _(sp):
            sp.dma_start(X[:, :, :], x[0].rearrange("(t p) n -> p t n", p=P)).then_inc(in_x, 16)
            sp.dma_start(const[:, :], consts[:, 0:3 * P + 56]).then_inc(in_const, 16)
            for name, k in STREAM:
                if name in ("fgu", "fdn"):
                    continue
                n = FIRST[name]
                if name == "o1":
                    sp.wait_ge(slab_used, FIRST["v1b"] + 2)
                    for h in range(2):
                        load(sp, HELD + h, ed[HP, :, 4 * HB - 4 + 2 * h:4 * HB - 2 + 2 * h, :])
                for i, s in enumerate(slabs[name]):
                    load(sp, n + i, s)
                if name == "evq":
                    sp.wait_ge(in_row, 160)
                    sp.dma_start(tbt, mem[0].rearrange("(t p) n -> p t n", p=P)).then_inc(in_mem, 16)
                if name == "k1a":
                    g = FIRST["fgu"]
                    with sp.Fori(0, 3) as r:
                        for j in range(3):
                            load(sp, g + 2 * j, ffg[:, :, bass.ds(r * 768 + 256 * j, 256)], r)
                            load(sp, g + 2 * j + 1, ffu[:, :, bass.ds(r * 768 + 256 * j, 256)], r)
                    for j in range(9, 11):
                        load(sp, g + 2 * j, f_slab(ffg, 256 * j))
                        load(sp, g + 2 * j + 1, f_slab(ffu, 256 * j))
                    for j in range(11):
                        load(sp, FIRST["fdn"] + j, ffd[:, 2 * j:2 * j + 2, :])

            def at(w, e, rows_, c):
                return w[e, :, rows_, c] if isinstance(e, int) else w[bass.ds(e, 1), :, rows_, c][0]

            def across(b):
                return slice(512 * b, 512 * b + 512) if isinstance(b, int) else bass.ds(b * 512, 512)

            def gate_in(q, e, b, behind):
                for h in range(2):
                    load(sp, G0 + 4 + h, at(eg, e, slice(4 * h, 4 * h + 4), across(b)), 7 * q + b - 1, behind)

            def up_in(q, e, b, behind):
                for h in range(2):
                    load(sp, G0 + 6 + h, at(eu, e, slice(4 * h, 4 * h + 4), across(b)), 7 * q + b - 1, behind)

            def down_in(q, e, b, behind):
                for h in range(2):
                    k = 4 * b - 4 + 2 * h
                    load(sp, G0 + 8 + h, at(ed, e, slice(k, k + 2) if isinstance(b, int) else bass.ds(k, 2),
                                            slice(0, D)), 7 * q + b - 1, behind)

            def opening_in(q, e, behind):
                for w, n in ((eg, 0), (eu, 2)):
                    for h in range(2):
                        load(sp, G0 + n + h, at(w, e, slice(4 * h, 4 * h + 4), slice(0, 512)), 7 * q, behind)

            def blocks_in(q, e, lo, hi, behind):
                with sp.Fori(lo, hi) as b:
                    gate_in(q, e, b, behind)
                    up_in(q, e, b, behind)
                    down_in(q, e, b, behind)

            def last_in(q, e, behind):
                for h in range(2):
                    k = 4 * NB - 4 + 2 * h
                    load(sp, G0 + 4 + h, at(ed, e, slice(k, k + 2), slice(0, D)), 7 * q + 6, behind)

            def expert(q, e, behind):
                opening_in(q, e, behind)
                blocks_in(q, e, 1, NB, behind)
                last_in(q, e, behind)

            sp.wait_ge(xs_o, 2 * XH)
            gate_in(HP, HP, HB + 1, False)
            with sp.Fori(0, HP) as q:
                expert(q, q, False)
            opening_in(HP, HP, False)
            blocks_in(HP, HP, 1, HB, False)
            gate_in(HP, HP, HB, False)
            up_in(HP, HP, HB, False)
            up_in(HP, HP, HB + 1, True)
            down_in(HP, HP, HB + 1, True)
            gate_in(HP, HP, HB + 2, True)
            up_in(HP, HP, HB + 2, True)
            down_in(HP, HP, HB + 2, True)
            blocks_in(HP, HP, HB + 3, NB, True)
            last_in(HP, HP, True)
            with sp.Fori(HP + 1, NE) as q:
                expert(q, q, True)
            sp.wait_ge(r_tab, 1)
            n_pass = sp.value_load(table[0:1, 0:1], min_val=NE, max_val=NE + 3)
            with sp.If(n_pass > NE):
                with sp.Fori(NE, n_pass) as q:
                    col = sp.value_load(table[0:1, bass.ds(q + 1, 1)], min_val=NE, max_val=2 * NE - 1)
                    expert(q, col - NE, True)
            for t in range(2):
                sp.wait_ge(out_rdy, t + 1)
                sp.dma_start(out[0, t * P:(t + 1) * P, :], fin_o[:, t, :]).then_inc(out_done, 16)
            sp.wait_ge(out_done, 32)

        @block.gpsimd
        def _(pool):
            nc.gpsimd.memset(half[:, :], -0.5).then_inc(pool_link, 1)
            pool.wait_ge(pool_link, 1)

            def root(k, w):
                pool.wait_ge(n_var, k + 1)
                nc.gpsimd.tensor_tensor(rstd[:, 0:w], var[:, 0:w], half[:, 0:w], ALU.pow).then_inc(n_rstd, 1)

            for name, k in NORMS.items():
                if name == "dif":
                    pool.wait_ge(f_add, 2)
                    pool.dma_start(router[:, :].rearrange("p (k e) -> p k e", k=KT),
                                   kpn(moe_router[0])).then_inc(in_router, 16)
                if name == "fin":
                    pool.wait_ge(acc_free, BANKS["o1"] + 4)
                    pool.dma_start(fin_g, final_norm_g.partition_broadcast(P)).then_inc(in_fin, 16)
                root(k, 16 if name in ("ret", "dif") else 2)
                if name == "mem":
                    pool.dma_start(after_i, consts[:, CONST["after_i"][0]:CONST["after_i"][1]]).then_inc(in_misc, 16)
                    pool.dma_start(before_i, consts[:, CONST["before_i"][0]:CONST["before_i"][1]]).then_inc(in_misc, 16)
                    pool.dma_start(decay[:, 0, :], ev_ret_decay_f[0].partition_broadcast(P)).then_inc(in_misc, 16)
                    pool.dma_start(decay[:, 1, :], ev_ret_decay_b[0].partition_broadcast(P)).then_inc(in_misc, 16)
                    for i, v in enumerate((od_lam_q1, od_lam_k1, od_lam_q2, od_lam_k2)):
                        pool.dma_start(lamv[:, i, :], v[0].partition_broadcast(P)).then_inc(in_misc, 16)

        @block.scalar
        def _(act):
            links = [0]

            def link(ins):
                links[0] += 1
                ins.then_inc(act_link, 1)
                act.wait_ge(act_link, links[0])

            act.dma_start(pos_i[:, :], positions[0].rearrange("(k p) -> k p", p=P)).then_inc(in_pos, 16)
            for name, v in (("mem", mem_norm_g), ("x0", mix_norm_g[0]), ("x1", mix_norm_g[1]), ("xa0", xa_norm_g[0]),
                            ("xa1", xa_norm_g[1]), ("ffn", ffn_norm_g[0]), ("moe", ffn_norm_g[1]),
                            ("ret", ev_ret_gn_g[0]), ("dif", od_gn_g[0])):
                r, k = ROWS[name], v.shape[0] // P
                act.dma_start(rows[r:r + k, :], v.rearrange("(k p) -> k p", p=P)).then_inc(in_row, 16)
            act.dma_start(rows[ROWS["conv"]:N_ROWS, :],
                          ev_conv_w[0].rearrange("j (k p) -> (j k) p", p=P)).then_inc(in_row, 16)

            def squares(name, src):
                k = 2 * [n for n in NORMS if n not in ("ret", "dif")].index(name)
                for t in range(2):
                    nc.scalar.activation(rot[:, :, :].rearrange("p a n -> p (a n)"), src[:, t, :], ACT.Square,
                                         accum_out=sums[:, t:t + 1]).then_inc(n_sq, 1)
                    act.wait_ge(n_sq, k + t + 1)

            def turn_hi(name, hi, k0=0, tiles=None):
                base, n = TURNS[name]
                for k in tiles or range(n):
                    act.wait_ge(t_ps, (base + k) // 2 + 1)
                    nc.scalar.activation(hi[:, k0 + k, :], pair(4 + k // 2)[:, k % 2, :], ACT.Copy,
                                         scale=cols[:, ROWS[name] + k:ROWS[name] + k + 1]).then_inc(t_hi, 1)

            def stage(name, k, events=()):
                events = dict(events)
                for i in range(k):
                    cut_hi(act, FIRST[name] + i + AHEAD)
                    if i in events:
                        events[i]()

            act.wait_ge(pool_link, 1)
            nc.scalar.activation(mx[:, 15:16], half[:, 0:1], ACT.Square).then_inc(act_link, 1)
            act.wait_ge(in_x, 16)
            squares("x0", X)
            for n in range(AHEAD):
                cut_hi(act, n)
            act.wait_ge(setup_v, 3)
            turn_hi("x0", a_hi)
            act.wait_ge(setup_v, 4)
            nc.scalar.activation(sin[:, :, :], ang[:, :, :], ACT.Sin).then_inc(setup_s, 1)
            nc.scalar.activation(cos[:, :, :], ang[:, :, :], ACT.Sin, scale=0.5).then_inc(setup_s, 1)
            stage("evq", 2)
            act.wait_ge(in_mem, 16)
            squares("mem", tbt)
            turn_hi("mem", m_hi)
            stage("evk", 2)
            stage("evv", 2)
            act.wait_ge(in_misc, 8 * 16)
            nc.scalar.activation(decay[:, :, :], decay[:, :, :], ACT.Exp).then_inc(setup_s, 1)
            stage("evg", 2)
            stage("evc", 6)
            act.wait_ge(acc_free, BANKS["evc"])
            nc.scalar.activation(ev_g, ev_g, ACT.Silu).then_inc(g_silu, 1)
            act.wait_ge(acc_free, BANKS["evc"] + 6)
            nc.scalar.activation(a_hi[:, 0:4, :], ev_u, ACT.Copy).then_inc(conv_hi, 1)

            def decays(heads):
                for h in heads:
                    act.wait_ge(d_exp, h + 1)
                    nc.scalar.activation(dmat[:, h, :], dmat[:, h, :], ACT.Exp).then_inc(d_got, 1)

            decays(range(4))
            stage("k0", 4)
            decays(range(4, RH))
            act.wait_ge(rs_o, 1)
            nc.scalar.activation(ta[:, 0:1024].rearrange("p (t n) -> p t n", t=2), ps[:, 6:8, :],
                                 ACT.Square).then_inc(sq_heads, 1)
            stage("v0a", 2)
            turn_hi("ret", a_hi, 4)
            stage("evo", 4)

            def cross(i, xa_pt):
                name = f"xa{i}"
                act.wait_ge(acc_free, BANKS[f"v{i}b"])
                squares(name, X)
                stage(f"v{i}b", 2)
                turn_hi(name, a_hi)
                stage(f"q{i}", 4)
                for h in range(XH):
                    act.wait_ge(xs_mx, XH * i + h + 1)
                    for t in range(2):
                        nc.scalar.activation(xa_p[:, h, t, :], pair(4 + h)[:, t, :], ACT.Exp,
                                             bias=nmx[:, 2 * h + t:2 * h + t + 1], scale=1.0 / 16.0,
                                             accum_out=den[:, 2 * h + t:2 * h + t + 1]).then_inc(xs_exp, 1)
                for h in range(XH):
                    act.wait_ge(xs_tp, XH * i + h + 1)
                    nc.scalar.activation(xa_pt[:, h, :, :], pair(4 + h), ACT.Copy).then_inc(xs_t, 1)
                for h in range(XH):
                    act.wait_ge(xs_o, XH * i + h + 1)
                    nc.scalar.activation(a_hi[:, 2 * h:2 * h + 2, :], pair(4 + h), ACT.Copy).then_inc(xs_hi, 1)
                stage(f"o{i}", 4 if i == 0 else 3)

            cross(0, xa_pt0)
            act.wait_ge(acc_free, BANKS["k1a"])
            squares("ffn", X)
            stage("k1a", 2)
            turn_hi("ffn", a_hi)
            g = FIRST["fgu"]

            def ff_pair(j, r, f):
                cut_hi(act, g + 2 * j + AHEAD, r)
                act.wait_ge(slab_used, g + 2 * j + 1 + 6 * r)
                nc.scalar.activation(f_sig, ps[:, 2 * (j % 3), :], ACT.Silu).then_inc(f_silu, 1)
                cut_hi(act, g + 2 * j + 1 + AHEAD, r)
                act.wait_ge(f_mul, f + 1)
                nc.scalar.activation(f_hi[:, bass.ds(2 * f, 2), :], f_act.rearrange("p (a n) -> p a n", a=2),
                                     ACT.Copy).then_inc(f_rnd, 1)

            with act.Fori(0, 3) as r:
                for j in range(3):
                    ff_pair(j, r, 3 * r + j)
            for j in range(9, 11):
                ff_pair(j, 0, j)
            stage("fdn", 11)

            act.wait_ge(f_add, 2)
            squares("x1", X)
            stage("k1b", 2)
            turn_hi("x1", a_hi)
            stage("odq", 4)
            stage("odk", 4)
            for b in range(8):
                act.wait_ge(oq_ps, b + 1)
                dst = (od_qt if b < 4 else od_kt)[:, 2 * (b % 4):2 * (b % 4) + 2, :]
                nc.scalar.activation(dst, pair(4 + b % 4), ACT.Copy).then_inc(oq_t, 1)
            stage("odv", 4)
            act.wait_ge(lam_s, 1)
            nc.scalar.activation(lams[:, 2:4], lams[:, 0:2], ACT.Exp).then_inc(lam_e, 1)
            act.wait_ge(in_router, 16)
            act.wait_ge(r_z, 1)
            nc.scalar.activation(r_hi[:, 0:KT * NE], router[:, :], ACT.Copy).then_inc(r_w, 1)

            def d_exps(h):
                act.wait_ge(ds_mx, h + 1)
                if h >= 2:
                    act.wait_ge(ds_tp, h - 1)
                for g_ in range(2):
                    for t in range(2):
                        i = 2 * g_ + t
                        nc.scalar.activation(od_p[:, h % 2, g_, t, :], pair(4 + 2 * (h % 2) + g_)[:, t, :], ACT.Exp,
                                             bias=nmx[:, 4 * (h % 2) + i:4 * (h % 2) + i + 1], scale=0.125,
                                             accum_out=den[:, 4 * (h % 2) + i:4 * (h % 2) + i + 1]).then_inc(ds_exp, 1)

            for h in range(DH + 1):
                if h < DH:
                    d_exps(h)
                if h >= 1:
                    act.wait_ge(ds_tp, h)
                    nc.scalar.activation(od_pt[:, (h - 1) % 4, :, :], pair((h - 1) % 2), ACT.Copy).then_inc(ds_t, 1)
            act.wait_ge(ds_out, DH)
            nc.scalar.activation(tat, od_s, ACT.Square).then_inc(sq_heads, 1)
            stage("v1a", 2)
            turn_hi("dif", a_hi)
            stage("odo", 4)
            cross(1, xa_pt1)

            sq = 2 * [n for n in NORMS if n not in ("ret", "dif")].index("moe")
            for h in range(2):
                act.wait_ge(acc_free, BANKS["o1"] + 2 * h + 2)
                turn_hi("moe", a_hi, tiles=range(4 * h, 4 * h + 4))
                for t in range(2):
                    nc.scalar.activation(rot[:, t, :], X[:, t, 512 * h:512 * h + 512], ACT.Square,
                                         accum_out=sums[:, 2 * h + t:2 * h + t + 1]).then_inc(n_sq, 1)
                act.wait_ge(n_sq, sq + 2 * h + 2)
            cut_hi(act, G0 + 1)
            act.wait_ge(n_rstd, NORMS["moe"] + 1)
            for t in range(2):
                nc.scalar.activation(tat[:, t, :], X[:, t, :], ACT.Copy,
                                     scale=rstd[:, t:t + 1]).then_inc(n_out, 1)
            cut_hi(act, G0 + 2)
            act.wait_ge(r_m, 1)
            nc.scalar.activation(lg[:, 9, 2:4], lg[:, 9, 0:2], ACT.Exp).then_inc(r_e, 1)
            act.wait_ge(r_tab, 1)
            n_pass = act.value_load(table[0:1, 0:1], min_val=NE, max_val=NE + 3)
            nc.scalar.activation(mx[:, 0:1], ident[:, 0:1], ACT.Silu).then_inc(g_sig, 1)

            def pack_hi(k):
                for i in range(KT):
                    if i % 4 == 0:
                        act.wait_ge(e_ps, 2 * k + i // 4 + 1)
                    nc.scalar.activation(e_hi[:, i, :], ps[:, 6 + i // 4, (i % 4) * P:(i % 4 + 1) * P], ACT.Copy,
                                         scale=cols[:, ROWS["moe"] + i:ROWS["moe"] + i + 1]).then_inc(e_h, 1)

            def e_silu(i, opening=0):
                act.wait_ge(slab_used, G0 + 6 * i + opening)
                act.wait_ge(act_rdy, i + 1)
                nc.scalar.activation(e_sig[:, :], ps[:, 0, :], ACT.Silu).then_inc(g_sig, 1)

            def e_turn_hi(i):
                act.wait_ge(at_ps, i + 1)
                nc.scalar.activation(at_hi[:, :, :], shaped(ps[:, 4, :], 4), ACT.Copy).then_inc(at_h, 1)

            pack_hi(0)
            for n in range(3, 6):
                cut_hi(act, G0 + n)

            def a_block(q, b, behind):
                i = 7 * q + b
                r = i - 1
                cut_hi(act, G0 + 6, r, behind)
                cut_hi(act, G0 + 7, r, behind)
                e_silu(i)
                e_turn_hi(i - 1)
                cut_hi(act, G0 + 8, r, behind)
                cut_hi(act, G0 + 9, r, behind)
                cut_hi(act, G0 + 4, i, behind)
                cut_hi(act, G0 + 5, i, behind)

            def a_next(q, behind):
                cut_hi(act, G0, 7 * q, behind)
                pack_hi(q)
                for n in range(1, 6):
                    cut_hi(act, G0 + n, 7 * q, behind)

            def a_pass(q, spans):
                e_silu(7 * q, 2)
                for lo, hi, behind in spans:
                    if behind is None:
                        a_block(q, lo, None)
                    else:
                        with act.Fori(lo, hi) as b:
                            a_block(q, b, behind)
                e_turn_hi(7 * q + NB - 1)

            with act.Fori(0, HP) as q:
                a_pass(q, [(1, NB, False)])
                a_next(q + 1, False)
            a_pass(HP, [(1, HB, False), (HB, HB + 1, None), (HB + 1, NB, True)])
            with act.Fori(HP + 1, n_pass) as q:
                a_next(q, True)
                a_pass(q, [(1, NB, True)])
            n_fin = 2 + 2 * [n for n in NORMS if n not in ("ret", "dif")].index("fin")
            for t in range(2):
                act.wait_ge(x_half if t == 0 else combined, n_pass + t)
                nc.scalar.activation(rot[:, :, :].rearrange("p a n -> p (a n)"), X[:, t, :], ACT.Square,
                                     accum_out=sums[:, t:t + 1]).then_inc(n_sq, 1)
                act.wait_ge(n_sq, n_fin + t + 1)

        @block.vector
        def _(dve):
            links = [0]

            def link(ins):
                links[0] += 1
                ins.then_inc(dve_link, 1)
                dve.wait_ge(dve_link, links[0])

            V = nc.vector

            def means(name, w, count):
                V.tensor_scalar(var[:, 0:w], sums[:, 0:w], 1.0 / count, EPS, ALU.mult, ALU.add).then_inc(n_var, 1)
                dve.wait_ge(n_rstd, NORMS[name] + 1)

            def norm(name, src, dst):
                k = 2 * [n for n in NORMS if n not in ("ret", "dif")].index(name)
                dve.wait_ge(n_sq, k + 2)
                means(name, 2, D)
                for t in range(2):
                    ins = V.tensor_scalar(dst[:, t, :], src[:, t, :], rstd[:, t:t + 1], None, ALU.mult)
                    ins.then_inc(n_out, 1)

            def turn_lo(name, hi, lo, k0=0, tiles=None):
                base, n = TURNS[name]
                for k in tiles or range(n):
                    dve.wait_ge(t_hi, base + (k | 1) + 1)
                    V.scalar_tensor_tensor(out=lo[:, k0 + k, :], in0=pair(4 + k // 2)[:, k % 2, :],
                                           scalar=cols[:, ROWS[name] + k:ROWS[name] + k + 1],
                                           in1=hi[:, k0 + k, :].bitcast(F32), op0=ALU.mult,
                                           op1=ALU.subtract).then_inc(t_lo, 1)

            def stage(name, k, events=()):
                events = dict(events)
                for i in range(k):
                    cut_lo(dve, FIRST[name] + i + AHEAD)
                    if i in events:
                        dve.wait_ge(slab_used, FIRST[name] + i + 1)
                        events[i]()

            def acc(name, i, w):
                b = (BANKS[name] + w * i) % 4
                return ps[:, b:b + w, :] if w > 1 else pair(b)

            def freed(ins, w):
                ins.then_inc(acc_free, w)

            dve.wait_ge(in_pos, 16)
            V.tensor_copy(pos_f[:, :], pos_i[:, :]).then_inc(setup_v, 1)
            dve.wait_ge(setup_t, 1)
            V.tensor_copy(pos[:, :], ps[:, 7, 0:2]).then_inc(setup_v, 1)
            dve.wait_ge(setup_t, 2)
            V.tensor_copy(cols[:, :], ps[:, 6, 0:N_ROWS]).then_inc(setup_v, 1)
            norm("x0", X, tat)
            for n in range(AHEAD):
                cut_lo(dve, n)
            dve.wait_ge(setup_v, 3)
            turn_lo("x0", a_hi, a_lo)
            dr = ROWS["dif"]
            link(V.tensor_scalar(cols[:, dr:dr + 8], cols[:, dr:dr + 8], 1.0 - LAM0, None, ALU.mult))
            for t in range(2):
                link(V.tensor_scalar(ang[:, t, :], freq, pos[:, t:t + 1], None, ALU.mult))
            c1 = 6.28125
            rest = 2 * math.pi - c1
            c2 = math.floor(rest * 2 ** 20) / 2 ** 20
            c3 = rest - c2
            big = 12582912.0
            link(V.tensor_scalar(turnsb[:, :, :], ang[:, :, :], 1.0 / (2 * math.pi), None, ALU.mult))
            link(V.tensor_scalar(turnsb[:, :, :], turnsb[:, :, :], big, None, ALU.add))
            link(V.tensor_scalar(turnsb[:, :, :], turnsb[:, :, :], -big, None, ALU.add))
            link(V.scalar_tensor_tensor(out=ang[:, :, :], in0=turnsb[:, :, :], scalar=-c1, in1=ang[:, :, :],
                                        op0=ALU.mult, op1=ALU.add))
            link(V.scalar_tensor_tensor(out=ang[:, :, :], in0=turnsb[:, :, :], scalar=-c2, in1=ang[:, :, :],
                                        op0=ALU.mult, op1=ALU.add))
            link(V.scalar_tensor_tensor(out=ang[:, :, :], in0=turnsb[:, :, :], scalar=-c3, in1=ang[:, :, :],
                                        op0=ALU.mult, op1=ALU.add))
            V.tensor_scalar(ang[:, :, :], ang[:, :, :], 3.141592, -3.141592, ALU.min, ALU.max).then_inc(setup_v, 1)
            dve.wait_ge(setup_s, 2)
            link(V.tensor_tensor(cos[:, :, :], cos[:, :, :], cos[:, :, :], ALU.mult))
            link(V.tensor_scalar(cos[:, :, :], cos[:, :, :], -2.0, 1.0, ALU.mult, ALU.add))

            def rotate(src, dst, heads, half_, f0, done):
                shape = [P, 2, heads, half_]
                c = cos[:, :, f0:f0 + half_].unsqueeze(2).broadcast_to(shape)
                s = sin[:, :, f0:f0 + half_].unsqueeze(2).broadcast_to(shape)
                s4 = src.rearrange("p t (h d) -> p t h d", h=heads)
                d4 = dst.rearrange("p t (h d) -> p t h d", h=heads)
                x1, x2 = s4[:, :, :, 0:half_], s4[:, :, :, half_:2 * half_]
                n = 2 * heads * half_
                a = rot[:, 0, 0:n].rearrange("p (t h d) -> p t h d", t=2, h=heads)
                b = rot[:, 1, 0:n].rearrange("p (t h d) -> p t h d", t=2, h=heads)
                V.tensor_tensor(a, x1, c, ALU.mult)
                link(V.tensor_tensor(b, x2, s, ALU.mult))
                link(V.tensor_tensor(d4[:, :, :, 0:half_], a, b, ALU.subtract))
                V.tensor_tensor(a, x1, s, ALU.mult)
                link(V.tensor_tensor(b, x2, c, ALU.mult))
                done(V.tensor_tensor(d4[:, :, :, half_:2 * half_], a, b, ALU.add))

            def rotated(ins):
                ins.then_inc(acc_free, 2)

            stage("evq", 2)
            norm("mem", tbt, tbt)
            turn_lo("mem", m_hi, m_lo)
            dve.wait_ge(slab_used, FIRST["evk"])
            rotate(acc("evq", 0, 2), ev_qr, RH, 32, 0, rotated)
            dve.wait_ge(acc_free, BANKS["evk"])
            stage("evk", 2, {1: lambda: rotate(acc("evk", 0, 2), ev_kr, RH, 32, 0, rotated)})
            stage("evv", 2, {1: lambda: freed(V.tensor_copy(ev_v, acc("evv", 0, 2)), 2)})
            dve.wait_ge(setup_s, 3)
            link(V.tensor_scalar(decay[:, :, :], decay[:, :, :], -1.0, None, ALU.mult))

            def exponents(heads):
                for h in heads:
                    link(V.tensor_scalar(dmat[:, h, :], after_i, decay[:, 0, h:h + 1], None, ALU.mult))
                    V.scalar_tensor_tensor(out=dmat[:, h, :], in0=before_i, scalar=decay[:, 1, h:h + 1],
                                           in1=dmat[:, h, :], op0=ALU.mult, op1=ALU.add).then_inc(d_exp, 1)

            stage("evg", 2, {1: lambda: freed(V.tensor_copy(ev_g, acc("evg", 0, 2)), 2)})

            def conv_event(i):
                def f():
                    w = ROWS["conv"]
                    s = slice(2 * (i % 2), 2 * (i % 2) + 2)
                    dve.wait_ge(acc_free, BANKS["evc"] + i)
                    if i < 2:
                        freed(V.tensor_copy(ev_c[:, s, :], acc("evc", i, 1)), 1)
                        exponents(range(2 * i, 2 * i + 2))
                    elif i < 4:
                        freed(V.tensor_tensor(ev_u[:, s, :], acc("evc", i, 1), ev_c[:, s, :], ALU.mult), 1)
                    if i == 3:
                        dve.wait_ge(acc_free, BANKS["evc"] + 4)
                        for k in range(4):
                            link(V.tensor_scalar(ev_c[:, k, :], ev_u[:, k, :], cols[:, w + 4 + k:w + 5 + k], None,
                                                 ALU.mult))
                            link(V.scalar_tensor_tensor(out=ev_c[:, k, 1:256], in0=ev_u[:, k, 0:255],
                                                        scalar=cols[:, w + k:w + k + 1], in1=ev_c[:, k, 1:256],
                                                        op0=ALU.mult, op1=ALU.add))
                            link(V.scalar_tensor_tensor(out=ev_c[:, k, 0:255], in0=ev_u[:, k, 1:256],
                                                        scalar=cols[:, w + 8 + k:w + 9 + k], in1=ev_c[:, k, 0:255],
                                                        op0=ALU.mult, op1=ALU.add))
                    if i >= 4:
                        freed(V.tensor_tensor(ev_u[:, s, :], acc("evc", i, 1), ev_c[:, s, :], ALU.mult), 1)
                return f

            stage("evc", 6, {i: conv_event(i) for i in range(6)})
            dve.wait_ge(conv_hi, 1)
            V.tensor_tensor(a_lo[:, 0:4, :], ev_u, a_hi[:, 0:4, :].bitcast(F32), ALU.subtract).then_inc(conv_lo, 1)
            for b in range(4):
                dve.wait_ge(qk_ps, b + 1)
                dst = (ev_qt if b < 2 else ev_kt)[:, 2 * (b % 2):2 * (b % 2) + 2, :]
                V.tensor_copy(dst, pair(4 + b)).then_inc(qk_t, 1)
            def k_event(name, i, dst, o):
                def f():
                    freed(V.tensor_copy(dst[:, o:o + 2, :], acc(name, i, 1)), 1)
                    if name == "k0":
                        exponents([4 + i])
                return f

            stage("k0", 4, {i: k_event("k0", i, xa_k0, 2 * i) for i in range(4)})
            for h in range(RH):
                dve.wait_ge(rs_ps, h + 1)
                dve.wait_ge(d_got, h + 1)
                V.scalar_tensor_tensor(out=ret_s[:, h % 4, :, :].rearrange("p j i -> p (j i)"), in0=ps[:, 4 + h % 2, :],
                                       scalar=0.125, in1=dmat[:, h, :], op0=ALU.mult, op1=ALU.mult).then_inc(rs_dec, 1)
            dve.wait_ge(sq_heads, 1)
            link(V.tensor_reduce(sums[:, 0:16], ta[:, 0:1024].rearrange("p (g d) -> p g d", d=64), AX.X, ALU.add))
            means("ret", 16, 64)
            tn = ta[:, 1024:2048].rearrange("p (g d) -> p g d", d=64)
            link(V.tensor_tensor(tn, ps[:, 6:8, :].rearrange("p t (h d) -> p (t h) d", d=64),
                                 rstd[:, 0:16].unsqueeze(2).broadcast_to([P, 16, 64]), ALU.mult))
            dve.wait_ge(g_silu, 1)
            tr = ta[:, 1024:2048].rearrange("p (t n) -> p t n", t=2)
            V.tensor_tensor(tr, tr, ev_g, ALU.mult).then_inc(n_out, 2)

            def v_event(i, name, dst, o=0):
                c = 512 * (i + o)
                return lambda: freed(V.tensor_copy(dst[:, :, c:c + 512], acc(name, i, 2)), 2)

            stage("v0a", 2, {1: v_event(0, "v0a", xa_v0)})
            turn_lo("ret", a_hi, a_lo, 4)

            def x_event(i, name):
                def f():
                    s = slice(512 * i, 512 * i + 512)
                    freed(V.tensor_tensor(X[:, :, s], acc(name, i, 2), X[:, :, s], ALU.add), 2)
                return f

            stage("evo", 4, {1: x_event(0, "evo"), 3: x_event(1, "evo")})

            def cross(i, xq, xv):
                name = f"xa{i}"
                norm(name, X, tat)
                stage(f"v{i}b", 2, {1: v_event(0, f"v{i}b", xv, 1)})
                turn_lo(name, a_hi, a_lo)

                def q_event(k):
                    return lambda: freed(V.tensor_copy(xq[:, 2 * k:2 * k + 2, :], acc(f"q{i}", k, 1)), 1)

                stage(f"q{i}", 4, {k: q_event(k) for k in range(4)})
                for h in range(XH):
                    dve.wait_ge(xs_ps, XH * i + h + 1)
                    link(V.tensor_reduce(mx[:, 2 * h:2 * h + 2], pair(4 + h), AX.X, ALU.max))
                    V.tensor_scalar(nmx[:, 2 * h:2 * h + 2], mx[:, 2 * h:2 * h + 2], -1.0 / 16.0, None,
                                    ALU.mult).then_inc(xs_mx, 1)
                for h in range(XH):
                    dve.wait_ge(xs_exp, 2 * (XH * i + h + 1))
                    link(V.reciprocal(rden[:, 2 * h:2 * h + 2], den[:, 2 * h:2 * h + 2]))
                    for t in range(2):
                        ins = V.tensor_scalar(xa_p[:, h, t, :], xa_p[:, h, t, :],
                                              rden[:, 2 * h + t:2 * h + t + 1], None, ALU.mult)
                    ins.then_inc(xs_n, 1)
                for h in range(XH):
                    dve.wait_ge(xs_hi, XH * i + h + 1)
                    V.tensor_tensor(a_lo[:, 2 * h:2 * h + 2, :], pair(4 + h), a_hi[:, 2 * h:2 * h + 2, :].bitcast(F32),
                                    ALU.subtract).then_inc(xs_lo, 1)
                if i == 0:
                    stage("o0", 4, {1: x_event(0, "o0"), 3: x_event(1, "o0")})

            cross(0, xa_q0, xa_v0)
            norm("ffn", X, tat)
            stage("k1a", 2, {i: k_event("k1a", i, xa_k1, 2 * i) for i in range(2)})
            turn_lo("ffn", a_hi, a_lo)
            g = FIRST["fgu"]

            def ff_pair(j, r, f):
                cut_lo(dve, g + 2 * j + AHEAD, r)
                cut_lo(dve, g + 2 * j + 1 + AHEAD, r)
                dve.wait_ge(slab_used, g + 2 * j + 2 + 6 * r)
                dve.wait_ge(f_silu, f + 1)
                V.tensor_tensor(f_act, ps[:, 2 * (j % 3) + 1, :], f_sig, ALU.mult).then_inc(f_mul, 1)
                dve.wait_ge(f_rnd, f + 1)
                V.tensor_tensor(f_lo[:, bass.ds(2 * f, 2), :], f_act.rearrange("p (a n) -> p a n", a=2),
                                f_hi[:, bass.ds(2 * f, 2), :].bitcast(F32), ALU.subtract).then_inc(f_low, 1)
                dve.wait_ge(f_low, f + 1)

            with dve.Fori(0, 3) as r:
                for j in range(3):
                    ff_pair(j, r, 3 * r + j)
            for j in range(9, 11):
                ff_pair(j, 0, j)

            def fd_event():
                for h in range(2):
                    V.tensor_tensor(X[:, :, 512 * h:512 * h + 512], ps[:, 4 + 2 * h:6 + 2 * h, :],
                                    X[:, :, 512 * h:512 * h + 512], ALU.add).then_inc(f_add, 1)

            stage("fdn", 11, {10: fd_event})

            norm("x1", X, tat)
            stage("k1b", 2, {i: k_event("k1b", i, xa_k1, 4 + 2 * i) for i in range(2)})
            turn_lo("x1", a_hi, a_lo)

            def qk_event(i, name, dst):
                def f():
                    d = dst[:, :, 512 * i:512 * i + 512]
                    a = acc(name, i, 2)
                    dve.wait_ge(acc_free, BANKS[name] + 2 * i)
                    link(V.tensor_copy(d, a))
                    rotate(a, d, 8, 8, 32, rotated)
                return f

            stage("odq", 4, {1: qk_event(0, "odq", tat), 3: qk_event(1, "odq", tat)})
            stage("odk", 4, {1: qk_event(0, "odk", od_kr), 3: qk_event(1, "odk", od_kr)})
            stage("odv", 4, {1: v_event(0, "odv", od_v), 3: v_event(1, "odv", od_v)})
            for i in range(2):
                V.tensor_tensor_reduce(rot[:, i, 0:64], lamv[:, 2 * i, :], lamv[:, 2 * i + 1, :], 1.0, 0.0, ALU.mult,
                                       ALU.add, lams[:, i:i + 1]).then_inc(dve_link, 1)
                links[0] += 1
            dve.wait_ge(dve_link, links[0])
            V.memset(lams[:, 2:4], 0.0).then_inc(lam_s, 1)
            dve.wait_ge(lam_e, 1)
            link(V.tensor_tensor(lams[:, 0:1], lams[:, 3:4], lams[:, 2:3], ALU.subtract))
            link(V.tensor_scalar(lams[:, 0:1], lams[:, 0:1], -LAM0, None, ALU.add))
            V.memset(r_hi[:, KT * NE:].bitcast(F32), 0.0).then_inc(dve_link, 1)
            V.memset(r_lo[:, KT * NE:].bitcast(F32), 0.0).then_inc(dve_link, 1)
            links[0] += 2
            dve.wait_ge(dve_link, links[0])
            V.memset(lams[:, 1:2], 0.0).then_inc(r_z, 1)
            dve.wait_ge(r_w, 1)
            link(V.tensor_tensor(r_lo[:, 0:KT * NE], router[:, :], r_hi[:, 0:KT * NE].bitcast(F32), ALU.subtract))

            def d_max(h):
                o = 4 * (h % 2)
                dve.wait_ge(ds_ps, h + 1)
                link(V.tensor_reduce(mx[:, o:o + 4],
                                     ps[:, 4 + o // 2:6 + o // 2, :].rearrange("p g (t k) -> p (g t) k", t=2), AX.X,
                                     ALU.max))
                V.tensor_scalar(nmx[:, o:o + 4], mx[:, o:o + 4], -0.125, None, ALU.mult).then_inc(ds_mx, 1)

            def d_mix(h):
                o = 4 * (h % 2)
                dve.wait_ge(ds_exp, 4 * h + 4)
                link(V.reciprocal(rden[:, o:o + 4], den[:, o:o + 4]))
                link(V.tensor_scalar(rden[:, o + 2:o + 4], rden[:, o + 2:o + 4], lams[:, 0:1], None, ALU.mult))
                for t in range(2):
                    ins = V.tensor_scalar(od_p[:, h % 2, 0, t, :], od_p[:, h % 2, 0, t, :], rden[:, o + t:o + t + 1],
                                          None, ALU.mult)
                link(ins)
                for t in range(2):
                    ins = V.scalar_tensor_tensor(out=od_p[:, h % 2, 0, t, :], in0=od_p[:, h % 2, 1, t, :],
                                                 scalar=rden[:, o + 2 + t:o + 3 + t], in1=od_p[:, h % 2, 0, t, :],
                                                 op0=ALU.mult, op1=ALU.add)
                ins.then_inc(ds_c, 1)

            def d_out(h):
                dve.wait_ge(ds_o, h + 1)
                V.tensor_copy(od_s[:, :, h * P:(h + 1) * P],
                              ps[:, 2 + h % 2, 0:2 * P].rearrange("p (t v) -> p t v", t=2)).then_inc(ds_out, 1)

            d_max(0)
            d_max(1)
            d_mix(0)
            for h in range(DH):
                if h + 1 < DH:
                    d_mix(h + 1)
                if h + 2 < DH:
                    d_max(h + 2)
                d_out(h)
            dve.wait_ge(sq_heads, 2)
            link(V.tensor_reduce(sums[:, 0:16], ta[:, :].rearrange("p (g d) -> p g d", d=P), AX.X, ALU.add))
            means("dif", 16, P)
            V.tensor_tensor(ta[:, :].rearrange("p (g d) -> p g d", d=P), od_s.rearrange("p t (h d) -> p (t h) d", d=P),
                            rstd[:, 0:16].unsqueeze(2).broadcast_to([P, 16, P]), ALU.mult).then_inc(n_out, 2)
            stage("v1a", 2, {1: v_event(0, "v1a", xa_v1)})
            turn_lo("dif", a_hi, a_lo)
            stage("odo", 4, {1: x_event(0, "odo"), 3: x_event(1, "odo")})
            cross(1, xa_q1, xa_v1)

            stage("o1", 3, {1: x_event(0, "o1"), 2: lambda: turn_lo("moe", a_hi, a_lo, tiles=range(4))})
            dve.wait_ge(slab_used, FIRST["o1"] + 4)
            x_event(1, "o1")()
            turn_lo("moe", a_hi, a_lo, tiles=range(4, 8))
            def small(i):
                return lg[:, i, :].rearrange("p (t e) -> p t e", t=2)

            def wide(v):
                return v.unsqueeze(2).broadcast_to([P, 2, NE])

            logit, eq, first, one1, left, one2, rank = (small(i) for i in range(7))
            m1, m2, r1 = lg[:, 7, 0:2], lg[:, 7, 2:4], lg[:, 7, 4:6]
            e8 = experts[:, 0:NE].unsqueeze(1).broadcast_to([P, 2, NE])
            V.memset(ones[:, :], 1.0)
            dve.wait_ge(n_sq, 2 * [n for n in NORMS if n not in ("ret", "dif")].index("moe") + 4)
            link(V.tensor_tensor(sums[:, 0:2], sums[:, 0:2], sums[:, 2:4], ALU.add))
            V.tensor_scalar(var[:, 0:2], sums[:, 0:2], 1.0 / D, EPS, ALU.mult, ALU.add).then_inc(n_var, 1)
            cut_lo(dve, G0 + 1)
            dve.wait_ge(r_lt, 1)
            V.tensor_copy(logits[:, :], ps[0:NE, LOGITS, 0:256]).then_inc(r_ls, 1)
            link(V.tensor_scalar(rank, e8, -1.0, float(NE), ALU.mult, ALU.add))
            dve.wait_ge(n_rstd, NORMS["moe"] + 1)
            dve.wait_ge(r_ps, 1)

            link(V.tensor_tensor(logit, ps[:, 2, 0:16].rearrange("p (t e) -> p t e", t=2), wide(rstd[:, 0:2]),
                                 ALU.mult))

            def pick(vals, m, one):
                link(V.tensor_reduce(m, vals, AX.X, ALU.max))
                link(V.tensor_tensor(eq, vals, wide(m), ALU.is_equal))
                link(V.tensor_tensor(first, eq, rank, ALU.mult))
                link(V.tensor_reduce(r1, first, AX.X, ALU.max))
                link(V.tensor_tensor(one, rank, wide(r1), ALU.is_equal))

            pick(logit, m1, one1)
            link(V.scalar_tensor_tensor(out=left, in0=one1, scalar=-3e38, in1=logit, op0=ALU.mult, op1=ALU.add))
            pick(left, m2, one2)
            V.tensor_tensor(lg[:, 9, 0:2], m2, m1, ALU.subtract).then_inc(r_m, 1)
            mask = small(8)
            V.tensor_tensor(mask, one1, one2, ALU.add).then_inc(r_cnt, 1)
            dve.wait_ge(r_e, 1)
            w1, w2 = lg[:, 9, 4:6], lg[:, 9, 6:8]
            link(V.tensor_scalar(w1, lg[:, 9, 2:4], 1.0, None, ALU.add))
            link(V.reciprocal(w1, w1))
            link(V.tensor_tensor(w2, w1, lg[:, 9, 2:4], ALU.mult))
            link(V.tensor_tensor(first, one1, wide(w1), ALU.mult))
            link(V.tensor_tensor(left, one2, wide(w2), ALU.mult))
            for b in range(2):
                link(V.tensor_tensor(gate16[:, :, NE * b:NE * b + NE], first, left, ALU.add))
            dve.wait_ge(r_ps, 2)
            cps = ps[:, 1, 0:16].rearrange("p (t e) -> p t e", t=2)
            link(V.tensor_tensor(first, cps, mask, ALU.mult))
            link(V.tensor_tensor(first, first, mask, ALU.add))
            link(V.tensor_scalar(pos16[:, :, 0:NE], first, -1.0, None, ALU.add))
            link(V.tensor_scalar(pos16[:, :, NE:2 * NE], first, -1.0 - BLK, None, ALU.add))
            V.memset(lg[:, 11, 1:2], 0.0).then_inc(act_rdy, 1)
            V.memset(lg[:, 11, 2:3], 0.0).then_inc(combined, 1)

            def pack_tokens(col):
                for t in range(2):
                    at = pos16[:, t, col:col + 1] if isinstance(col, int) else pos16[:, t, bass.ds(col, 1)]
                    ins = V.tensor_scalar(pack[:, t, :], slot, at, None, ALU.is_equal)
                ins.then_inc(packed, 1)

            pack_tokens(0)
            over, incl, rk, hit = (row16[:, i, 0:8] for i in range(4))
            link(V.tensor_scalar(over, ps[0:1, 1, 16:24], float(BLK), None, ALU.is_gt))
            link(V.tensor_tensor_scan(incl, ones[0:1, 0:8], over, 0.0, ALU.mult, ALU.add))
            link(V.tensor_tensor(rk, incl, over, ALU.subtract))
            link(V.tensor_scalar(row16[:, 0, 8:9], incl[:, 7:8], float(NE), None, ALU.add))
            link(V.tensor_copy(table[:, 0:1], row16[:, 0, 8:9]))
            link(V.tensor_copy(table[:, 1:1 + NE], experts[0:1, 0:NE]))
            for k in range(3):
                link(V.scalar_tensor_tensor(out=hit, in0=rk, scalar=float(k), in1=over, op0=ALU.is_equal,
                                            op1=ALU.mult))
                link(V.tensor_tensor(hit, hit, experts[0:1, NE:2 * NE], ALU.mult))
                link(V.tensor_reduce(row16[:, 1, 8 + k:9 + k], hit, AX.X, ALU.max))
            link(V.tensor_scalar(row16[:, 1, 8:11], row16[:, 1, 8:11], float(NE), None, ALU.max))
            V.tensor_copy(table[:, 1 + NE:4 + NE], row16[:, 1, 8:11]).then_inc(r_tab, 1)
            dve.wait_ge(r_tab, 1)
            n_pass = dve.value_load(table[0:1, 0:1], min_val=NE, max_val=NE + 3)

            def column(k):
                return dve.value_load(table[0:1, bass.ds(k + 1, 1)], min_val=0, max_val=2 * NE - 1)

            def pack_lo(k):
                for i in range(KT):
                    dve.wait_ge(e_h, KT * k + 4 * (i // 4) + 4)
                    ins = V.scalar_tensor_tensor(out=e_lo[:, i, :], in0=ps[:, 6 + i // 4, (i % 4) * P:(i % 4 + 1) * P],
                                                 scalar=cols[:, ROWS["moe"] + i:ROWS["moe"] + i + 1],
                                                 in1=e_hi[:, i, :].bitcast(F32), op0=ALU.mult, op1=ALU.subtract)
                ins.then_inc(e_l, 1)

            def e_mul(i, opening=0):
                dve.wait_ge(slab_used, G0 + 6 * i + 2 + opening)
                dve.wait_ge(g_sig, i + 2)
                V.tensor_tensor(e_act[:, :], ps[:, 1, :], e_sig[:, :], ALU.mult).then_inc(act_rdy, 1)

            def e_turn_lo(i):
                dve.wait_ge(at_h, i + 1)
                V.tensor_tensor(at_lo[:, :, :], shaped(ps[:, 4, :], 4), at_hi[:, :, :].bitcast(F32),
                                ALU.subtract).then_inc(at_l, 1)

            def add_pass(done):
                for t in range(2):
                    b0 = 6 if t == 0 else 2
                    dve.wait_ge(c_ps, 2 * done + t + 1)
                    V.tensor_tensor(X[:, t, :], ps[:, b0:b0 + 2, :].rearrange("p a n -> p (a n)"), X[:, t, :],
                                    ALU.add).then_inc(x_half if t == 0 else combined, 1)

            def pack_gates(col):
                for t in range(2):
                    p_, g_ = ((a[:, t, col:col + 1] if isinstance(col, int) else a[:, t, bass.ds(col, 1)])
                              for a in (pos16, gate16))
                    ins = V.tensor_scalar(pgate[:, t, :], slot, p_, g_, ALU.is_equal, ALU.mult)
                ins.then_inc(pg_rdy, 1)

            cut_lo(dve, G0 + 2)
            pack_lo(0)
            pack_gates(0)
            for n in range(3, 6):
                cut_lo(dve, G0 + n)

            def v_block(q, b, behind):
                i = 7 * q + b
                r = i - 1
                cut_lo(dve, G0 + 6, r, behind)
                cut_lo(dve, G0 + 7, r, behind)
                e_turn_lo(i - 1)
                cut_lo(dve, G0 + 8, r, behind)
                cut_lo(dve, G0 + 9, r, behind)
                e_mul(i)
                cut_lo(dve, G0 + 4, i, behind)
                cut_lo(dve, G0 + 5, i, behind)

            def v_y(q):
                dve.wait_ge(slab_used, G0 + PASS + PASS * q)
                V.tensor_copy(y[:, :], ps[:, 2:4, :].rearrange("p a n -> p (a n)")).then_inc(y_sb, 1)

            def v_next(q, behind):
                cut_lo(dve, G0, 7 * q, behind)
                pack_lo(q)
                cut_lo(dve, G0 + 1, 7 * q, behind)
                v_y(q - 1)
                for n in range(2, 6):
                    cut_lo(dve, G0 + n, 7 * q, behind)

            def v_pack(q):
                col = column(q)
                pack_tokens(col)
                pack_gates(col)

            def v_pass(q, spans, pack_more):
                e_mul(7 * q, 2)
                with dve.If(q > 0) if not isinstance(q, int) else nullcontext():
                    add_pass(q)
                dve.wait_ge(pg_ps, q + 1)
                V.tensor_copy(spread[:, :], ps[:, 5, 0:256]).then_inc(pg_t, 1)
                with dve.If(pack_more) if pack_more is not None else nullcontext():
                    v_pack(q + 1)
                for lo, hi, behind in spans:
                    if behind is None:
                        v_block(q, lo, None)
                    else:
                        with dve.Fori(lo, hi) as b:
                            v_block(q, b, behind)
                e_turn_lo(7 * q + NB - 1)

            with dve.Fori(0, HP) as q:
                v_pass(q, [(1, NB, False)], None)
                v_next(q + 1, False)
            v_pass(HP, [(1, HB, False), (HB, HB + 1, None), (HB + 1, NB, True)], None)
            with dve.Fori(HP + 1, n_pass) as q:
                v_next(q, True)
                v_pass(q, [(1, NB, True)], q < n_pass - 1)
            v_y(n_pass - 1)
            add_pass(n_pass)
            dve.wait_ge(in_fin, 16)
            dve.wait_ge(n_sq, 2 + 2 * sum(n not in ("ret", "dif") for n in NORMS))
            means("fin", 2, D)
            for t in range(2):
                V.scalar_tensor_tensor(out=fin_o[:, t, :], in0=X[:, t, :], scalar=rstd[:, t:t + 1], in1=fin_g,
                                       op0=ALU.mult, op1=ALU.mult).then_inc(out_rdy, 1)

        @block.tensor
        def _(pe):
            T = nc.tensor

            def cuts(ah, al, wh, wl):
                return ((ah, wh), (ah, wl), (al, wh))

            def slab_ready(n, r=0):
                pe.wait_ge(lo_cut, n + 1 + RAW * r)

            def room(name, upto):
                if upto > 4:
                    pe.wait_ge(acc_free, upto - 4)

            def gemm_t(name, blocks, hi, lo, base=None, before_last=None):
                for b in range(blocks):
                    c = BANKS[name] + 2 * b
                    room(name, c + 2)
                    for h in range(2):
                        n = FIRST[name] + 2 * b + h
                        if before_last is not None and (b, h) == (blocks - 1, 1):
                            before_last()
                        slab_ready(n)
                        wh, wl = (shaped(w[:, n % CUT, :], 4) for w in (w_hi, w_lo))
                        for k in range(4):
                            if base is not None and b == 0:
                                pe.wait_ge(t_lo, max(base + 4 * h + k + 1, 1))
                            for t in range(2):
                                ah, al = (a[:, 4 * h + k, t * P:(t + 1) * P] for a in (hi, lo))
                                for j, (s, m) in enumerate(cuts(ah, al, wh[:, k, :], wl[:, k, :])):
                                    mm = T.matmul(ps[:, (c + t) % 4, :], s, m, start=(h == 0 and k == 0 and j == 0),
                                                  stop=(h == 1 and k == 3 and j == 2))
                        mm.then_inc(slab_used, 1)

            def fm_slab(n, r, bank, hi, lo, base=None):
                slab_ready(n, r)
                wh, wl = (shaped(w[:, n % CUT, :], KT) for w in (w_hi, w_lo))
                for o in range(2):
                    for k in range(KT):
                        if base is not None and o == 0:
                            pe.wait_ge(t_lo, base + k + 1)
                        s_hi, s_lo = (w[:, k, o * P:(o + 1) * P] for w in (wh, wl))
                        for j, (s, m) in enumerate(cuts(s_hi, s_lo, hi[:, k, :], lo[:, k, :])):
                            mm = T.matmul(pair(bank)[:, o, :], s, m, start=(k == 0 and j == 0),
                                          stop=(k == KT - 1 and j == 2))
                mm.then_inc(slab_used, 1)

            def gemm_f(name, count, hi, lo, base=None):
                for i in range(count):
                    c = BANKS[name] + i
                    room(name, c + 1)
                    fm_slab(FIRST[name] + i, 0, c % 4, hi, lo, base if i == 0 else None)

            def turn(name, src, after):
                base, n = TURNS[name]
                pe.wait_ge(n_out, 2 * after)
                for b in range(n // 2):
                    for k in (2 * b, 2 * b + 1):
                        for t in range(2):
                            mm = T.transpose(pair(4 + b)[:, k % 2, t * P:(t + 1) * P], src[:, t, k * P:(k + 1) * P],
                                             ident)
                    mm.then_inc(t_ps, 1)

            def turn_x(h):
                pe.wait_ge(acc_free, BANKS["o1"] + 2 * h + 2)
                for b in (2 * h, 2 * h + 1):
                    for k in (2 * b, 2 * b + 1):
                        for t in range(2):
                            mm = T.transpose(pair(4 + b)[:, k % 2, t * P:(t + 1) * P], X[:, t, k * P:(k + 1) * P],
                                             ident)
                    mm.then_inc(t_ps, 1)

            def turned(name):
                base, n = TURNS[name]
                pe.wait_ge(t_lo, base + n)

            pe.wait_ge(in_const, 16)
            pe.wait_ge(setup_v, 1)
            T.transpose(ps[:, 7, 0:2], pos_f[:, :], ident[0:2, 0:2]).then_inc(setup_t, 1)
            pe.wait_ge(in_row, 160)
            T.transpose(ps[:, 6, 0:N_ROWS], rows[:, :], ident[0:N_ROWS, 0:N_ROWS]).then_inc(setup_t, 1)
            pe.wait_ge(setup_v, 3)
            turn("x0", tat, 1)
            gemm_t("evq", 1, a_hi, a_lo, TURNS["x0"][0])
            turn("mem", tbt, 2)
            gemm_t("evk", 1, a_hi, a_lo)
            gemm_t("evv", 1, a_hi, a_lo)
            gemm_t("evg", 1, a_hi, a_lo)
            gemm_f("evc", 6, a_hi, a_lo)
            turned("mem")
            pe.wait_ge(acc_free, BANKS["evv"])
            for b in range(4):
                src = ev_qr if b < 2 else ev_kr
                for k in (2 * (b % 2), 2 * (b % 2) + 1):
                    for t in range(2):
                        mm = T.transpose(pair(4 + b)[:, k % 2, t * P:(t + 1) * P], src[:, t, k * P:(k + 1) * P], ident)
                mm.then_inc(qk_ps, 1)
            gemm_f("k0", 4, m_hi, m_lo)
            pe.wait_ge(qk_t, 4)

            def ret_scores(h):
                if h >= 2:
                    pe.wait_ge(rs_dec, h - 1)
                a, hp = 64 * (h % 2), h // 2
                for j in range(2):
                    mm = T.matmul(pair(4 + h % 2)[:, j, :], ev_kt[a:a + 64, hp, j * P:(j + 1) * P],
                                  ev_qt[a:a + 64, hp, :], start=True, stop=True)
                mm.then_inc(rs_ps, 1)

            ret_scores(0)
            ret_scores(1)
            for h in range(RH):
                pe.wait_ge(rs_dec, h + 1)
                for t in range(2):
                    for j in range(2):
                        mm = T.matmul(ps[:, 6 + t, 64 * h:64 * h + 64], ret_s[:, h % 4, j, t * P:(t + 1) * P],
                                      ev_v[:, j, 64 * h:64 * h + 64], start=(j == 0), stop=(j == 1))
                if h + 2 < RH:
                    ret_scores(h + 2)
            mm.then_inc(rs_o, 1)
            gemm_t("v0a", 1, m_hi, m_lo)
            turn("ret", ta[:, 1024:2048].rearrange("p (t n) -> p t n", t=2), 3)
            pe.wait_ge(conv_lo, 1)
            gemm_t("evo", 2, a_hi, a_lo, TURNS["ret"][0] - 4)

            def cross(i, xq, xk, xv, xa_pt):
                name = f"xa{i}"
                gemm_t(f"v{i}b", 1, m_hi, m_lo)
                turn(name, tat, NORMS[name] + 1)
                gemm_f(f"q{i}", 4, a_hi, a_lo, TURNS[name][0])
                for h in range(XH):
                    pe.wait_ge(acc_free, BANKS[f"q{i}"] + h + 1)
                    for t in range(2):
                        for k in range(2):
                            mm = T.matmul(pair(4 + h)[:, t, :], xq[:, 2 * h + k, t * P:(t + 1) * P],
                                          xk[:, 2 * h + k, :], start=(k == 0), stop=(k == 1))
                    mm.then_inc(xs_ps, 1)
                for h in range(XH):
                    pe.wait_ge(xs_n, XH * i + h + 1)
                    for m in range(2):
                        for t in range(2):
                            mm = T.transpose(pair(4 + h)[:, m, t * P:(t + 1) * P], xa_p[:, h, t, m * P:(m + 1) * P],
                                             ident)
                    mm.then_inc(xs_tp, 1)
                for h in range(XH):
                    pe.wait_ge(xs_t, XH * i + h + 1)
                    for d in range(2):
                        for m in range(2):
                            mm = T.matmul(pair(4 + h)[:, d, :], xv[:, m, 256 * h + d * P:256 * h + (d + 1) * P],
                                          xa_pt[:, h, m, :], start=(m == 0), stop=(m == 1))
                    mm.then_inc(xs_o, 1)
                pe.wait_ge(xs_lo, XH * (i + 1))
                gemm_t(f"o{i}", 2, a_hi, a_lo, before_last=(lambda: turn_x(0)) if i == 1 else None)

            cross(0, xa_q0, xa_k0, xa_v0, xa_pt0)

            gemm_f("k1a", 2, m_hi, m_lo)
            turn("ffn", tat, NORMS["ffn"] + 1)
            pe.wait_ge(acc_free, BANKS["k1b"])
            g = FIRST["fgu"]

            def ff_pair(j, r, f, first=False):
                if not first:
                    pe.wait_ge(f_low, f - 2)
                base = TURNS["ffn"][0] if first and j == 0 else None
                fm_slab(g + 2 * j, r, 2 * (j % 3), a_hi, a_lo, base)
                fm_slab(g + 2 * j + 1, r, 2 * (j % 3) + 1, a_hi, a_lo)

            for j in range(3):
                ff_pair(j, 0, j, first=True)
            with pe.Fori(1, 3) as r:
                for j in range(3):
                    ff_pair(j, r, 3 * r + j)
            for j in range(9, 11):
                ff_pair(j, 0, j)
            for i in range(11):
                pe.wait_ge(f_low, i + 1)
                n = FIRST["fdn"] + i
                slab_ready(n)
                wh, wl = (shaped(w[:, n % CUT, :], 2) for w in (w_hi, w_lo))
                for k in range(2):
                    for t in range(2):
                        ah, al = (a[:, 2 * i + k, t * P:(t + 1) * P] for a in (f_hi, f_lo))
                        for h in range(2):
                            s = slice(512 * h, 512 * h + 512)
                            for j, (st, mv) in enumerate(cuts(ah, al, wh[:, k, s], wl[:, k, s])):
                                mm = T.matmul(ps[:, 4 + 2 * h + t, :], st, mv, start=(i == 0 and k == 0 and j == 0),
                                              stop=(i == 10 and k == 1 and j == 2))
                mm.then_inc(slab_used, 1)

            pe.wait_ge(f_mul, 11)
            gemm_f("k1b", 2, m_hi, m_lo)
            turn("x1", tat, NORMS["x1"] + 1)
            gemm_t("odq", 2, a_hi, a_lo, TURNS["x1"][0])
            gemm_t("odk", 2, a_hi, a_lo)
            for b in range(8):
                if b % 4 == 0:
                    pe.wait_ge(acc_free, BANKS["odk" if b == 0 else "odv"])
                if b >= 4:
                    pe.wait_ge(oq_t, b - 3)
                src = tat if b < 4 else od_kr
                for k in (2 * (b % 4), 2 * (b % 4) + 1):
                    for t in range(2):
                        mm = T.transpose(pair(4 + b % 4)[:, k % 2, t * P:(t + 1) * P], src[:, t, k * P:(k + 1) * P],
                                         ident)
                mm.then_inc(oq_ps, 1)
            gemm_t("odv", 2, a_hi, a_lo)
            pe.wait_ge(oq_t, 8)
            pe.wait_ge(acc_free, BANKS["v1a"])

            def d_scores(h):
                if h >= 2:
                    pe.wait_ge(ds_exp, 4 * (h - 1))
                for g_ in range(2):
                    a = 64 * g_
                    for t in range(2):
                        mm = T.matmul(pair(4 + 2 * (h % 2) + g_)[:, t, :], od_qt[a:a + 64, h, t * P:(t + 1) * P],
                                      od_kt[a:a + 64, h, :], start=True, stop=True)
                mm.then_inc(ds_ps, 1)

            d_scores(0)
            d_scores(1)
            for h in range(DH):
                pe.wait_ge(ds_c, h + 1)
                for k in range(2):
                    for t in range(2):
                        mm = T.transpose(pair(h % 2)[:, k, t * P:(t + 1) * P], od_p[:, h % 2, 0, t, k * P:(k + 1) * P],
                                         ident)
                mm.then_inc(ds_tp, 1)
                if h + 2 < DH:
                    d_scores(h + 2)
                pe.wait_ge(ds_t, h + 1)
                if h >= 2:
                    pe.wait_ge(ds_out, h - 1)
                for t in range(2):
                    for k in range(2):
                        mm = T.matmul(ps[:, 2 + h % 2, t * P:(t + 1) * P], od_pt[:, h % 4, k, t * P:(t + 1) * P],
                                      od_v[:, k, h * P:(h + 1) * P], start=(k == 0), stop=(k == 1))
                mm.then_inc(ds_o, 1)
            pe.wait_ge(ds_out, DH)
            gemm_t("v1a", 1, m_hi, m_lo)
            turn("dif", tat, NORMS["dif"] + 1)
            gemm_t("odo", 2, a_hi, a_lo, TURNS["dif"][0])
            cross(1, xa_q1, xa_k1, xa_v1, xa_pt1)

            for h in range(2):
                if h == 1:
                    turn_x(1)
                for k in range(4 * h, 4 * h + 4):
                    pe.wait_ge(t_lo, TURNS["moe"][0] + k + 1)
                    rh, rl = (a[:, NE * k:NE * k + P] for a in (r_hi, r_lo))
                    for j, (s, m) in enumerate(cuts(rh, rl, a_hi[:, k, :], a_lo[:, k, :])):
                        mm = T.matmul(ps[:, LOGITS, 0:256], s, m, start=(k == 0 and j == 0),
                                      stop=(k == KT - 1 and j == 2))
            mm.then_inc(r_lt, 1)
            pe.wait_ge(r_ls, 1)
            for t in range(2):
                mm = T.transpose(ps[:, 2, NE * t:NE * t + NE], logits[:, t * P:(t + 1) * P], ident[0:NE, 0:NE])
            mm.then_inc(r_ps, 1)
            pe.wait_ge(r_cnt, 1)
            mask = lg[:, 8, :]
            T.matmul(ps[:, 1, 0:8], before, mask[:, 0:8], start=True, stop=True)
            T.matmul(ps[:, 1, 8:16], before, mask[:, 8:16], start=True, stop=False)
            T.matmul(ps[:, 1, 8:16], ones[:, :], mask[:, 0:8], start=False, stop=True).then_inc(c_ps, 2)
            T.matmul(ps[:, 1, 16:24], ones[:, :], mask[:, 0:8], start=True, stop=False)
            T.matmul(ps[:, 1, 16:24], ones[:, :], mask[:, 8:16], start=False, stop=True).then_inc(r_ps, 1)

            def gather(k):
                pe.wait_ge(packed, k + 1)
                for i in range(KT):
                    for t in range(2):
                        mm = T.matmul(ps[:, 6 + i // 4, (i % 4) * P:(i % 4 + 1) * P], tat[:, t, i * P:(i + 1) * P],
                                      pack[:, t, :], start=(t == 0), stop=(t == 1))
                    if i % 4 == 3:
                        mm.then_inc(e_ps, 1)

            def half_in(n, r, bank, h):
                slab_ready(n, r)
                wh, wl = (shaped(w[:, n % CUT, :], 4) for w in (w_hi, w_lo))
                for k in range(4):
                    ah, al = e_hi[:, 4 * h + k, :], e_lo[:, 4 * h + k, :]
                    for j, (s, m) in enumerate(cuts(ah, al, wh[:, k, :], wl[:, k, :])):
                        mm = T.matmul(ps[:, bank, :], s, m, start=(h == 0 and k == 0 and j == 0),
                                      stop=(h == 1 and k == 3 and j == 2))
                mm.then_inc(slab_used, 1)

            def turn_act(i):
                pe.wait_ge(act_rdy, i + 2)
                for k in range(4):
                    mm = T.transpose(ps[:, 4, k * P:(k + 1) * P], e_act[:, k * P:(k + 1) * P], ident)
                mm.then_inc(at_ps, 1)

            def down(n, r, i, first, last):
                pe.wait_ge(at_l, i + 1)
                for h in range(2):
                    slab_ready(n + h, r)
                    wh, wl = (shaped(w[:, (n + h) % CUT, :], 2) for w in (w_hi, w_lo))
                    for k in range(2):
                        ah, al = at_hi[:, 2 * h + k, :], at_lo[:, 2 * h + k, :]
                        for o in range(2):
                            c = slice(512 * o, 512 * o + 512)
                            for j, (s, m) in enumerate(cuts(ah, al, wh[:, k, c], wl[:, k, c])):
                                mm = T.matmul(ps[:, 2 + o, :], s, m,
                                              start=(first and h == 0 and k == 0 and j == 0),
                                              stop=(last and h == 1 and k == 1 and j == 2), skip_group_check=True)
                    mm.then_inc(slab_used, 1)

            def combine(k):
                pe.wait_ge(y_sb, k + 1)
                pe.wait_ge(pg_t, k + 1)
                for t in range(2):
                    b0 = 6 if t == 0 else 2
                    for o in range(2):
                        mm = T.matmul(ps[:, b0 + o, :], spread[:, t * P:(t + 1) * P], y[:, 512 * o:512 * o + 512],
                                      start=True, stop=True)
                    mm.then_inc(c_ps, 1)

            pe.wait_ge(n_out, 2 * (NORMS["moe"] + 1))
            gather(0)
            pe.wait_ge(r_tab, 1)
            n_pass = pe.value_load(table[0:1, 0:1], min_val=NE, max_val=NE + 3)
            with pe.Fori(0, n_pass) as q:
                pe.wait_ge(e_l, q + 1)
                i = 7 * q
                pe.wait_ge(g_sig, i + 1)
                half_in(G0, i, 0, 0)
                half_in(G0 + 1, i, 0, 1)
                pe.wait_ge(act_rdy, i + 1)
                half_in(G0 + 2, i, 1, 0)
                half_in(G0 + 3, i, 1, 1)
                with pe.If(q > 0):
                    combine(q - 1)
                pe.wait_ge(pg_rdy, q + 1)
                for t in range(2):
                    mm = T.transpose(ps[:, 5, t * P:(t + 1) * P], pgate[:, t, :], ident)
                mm.then_inc(pg_ps, 1)
                for lo_, hi_ in ((1, 2), (2, NB)):
                    with pe.Fori(lo_, hi_) as b:
                        i = 7 * q + b
                        pe.wait_ge(g_sig, i + 1)
                        half_in(G0 + 4, i - 1, 0, 0)
                        half_in(G0 + 5, i - 1, 0, 1)
                        turn_act(i - 1)
                        pe.wait_ge(act_rdy, i + 1)
                        half_in(G0 + 6, i - 1, 1, 0)
                        half_in(G0 + 7, i - 1, 1, 1)
                        if lo_ == 1:
                            pe.wait_ge(combined, q + 1)
                        down(G0 + 8, i - 1, i - 1, lo_ == 1, False)
                turn_act(7 * q + NB - 1)
                with pe.If(q < n_pass - 1):
                    gather(q + 1)
                down(G0 + 4, 7 * q + 6, 7 * q + NB - 1, False, True)
            combine(n_pass - 1)


INPUTS = ["x", "mem", "positions", "mem_norm_g", "final_norm_g", "mix_norm_g", "xa_norm_g", "ffn_norm_g", "xa_wq",
          "xa_wkv", "xa_wo", "ev_w_in", "ev_conv_w", "ev_ret_decay_f", "ev_ret_decay_b", "ev_ret_gn_g", "ev_w_out",
          "ffd_w_gate", "ffd_w_up", "ffd_w_down", "od_w_in", "od_lam_q1", "od_lam_k1", "od_lam_q2", "od_lam_k2",
          "od_gn_g", "od_w_out", "moe_router", "moe_w_gate", "moe_w_up", "moe_w_down"]


def kernel(**inputs):
    import concourse.bacc as bacc
    from concourse.bass_utils import run_bass_kernel_spmd

    nc = bacc.Bacc("TRN2", target_bir_lowering=False, num_devices=1)
    arrays, args = {}, {}
    for name in INPUTS + ["consts"]:
        a = constants() if name == "consts" else np.ascontiguousarray(inputs[name])
        arrays[f"in_{name}"] = a
        args[name] = nc.dram_tensor(f"in_{name}", a.shape, mybir.dt.from_np(a.dtype), kind="ExternalInput").ap()
    shape = tuple(inputs["x"].shape)
    args["out"] = nc.dram_tensor("out_0", shape, F32, kind="ExternalOutput").ap()
    trunk_kernel(nc, **args)
    r = run_bass_kernel_spmd(nc, [arrays], core_ids=[0])
    return r.results[0]["out_0"]
```
